# Optimizing a Trainium2 kernel written in Bass

```python
import jax, jax.numpy as jnp
from jax import lax
import numpy as np

D_MODEL = 1024
BATCH = 1
SEQ = 128
DEPTH = 2
DEC_BATCH = 1
DEC_SEQ = 512
PAST_LEN = 128

GRID_W = 64
WIN_H = 8
WIN_W = 16
H_A = 8
HD_A = 64
A_WIDTH = H_A * HD_A
H_B = 4
HD_B = 128
B_WIDTH = H_B * HD_B
D_FF = 2816
N_MOD = 9
CHUNK = 128
Q_BLOCK = 128
ROPE_THETA = 10000.0
EPS = 1e-6
IN_COLS = 3 * A_WIDTH + 4 * B_WIDTH + 4 * H_B + 2 * D_MODEL

kernel_name = "hybrid_natten_mlstm_diffusion_step"

def _rmsnorm(x, g):
    xf = x.astype(jnp.float32)
    y = xf * lax.rsqrt(jnp.mean(xf * xf, axis=-1, keepdims=True) + EPS)
    return (y * g.astype(jnp.float32)).astype(x.dtype)

def _ada(cond, w, b):
    m = jax.nn.silu(cond) @ w + b
    return m.reshape(m.shape[0], 1, N_MOD, D_MODEL)

def _modulate(h, shift, scale):
    return h * (1 + scale) + shift

def _ffn_sub(x, g, shift, scale, gate, w_up, w_dn):
    h = _modulate(_rmsnorm(x, g), shift, scale)
    a, u = jnp.split(h @ w_up, 2, axis=-1)
    return x + 0.5 * gate * ((jax.nn.silu(a) * u) @ w_dn)

def _mixer_inputs(x, g, shift, scale, w_in, b_gates, g_qn, g_kn):
    B, L = x.shape[:2]
    h = _modulate(_rmsnorm(x, g), shift, scale)
    p = h @ w_in
    sizes = (A_WIDTH,) * 3 + (B_WIDTH,) * 4 + (4 * H_B, 2 * D_MODEL)
    offs = np.cumsum(sizes)[:-1].tolist()
    qa, ka, va, qb, kb, vb, ob, gt, br = jnp.split(p, offs, axis=-1)
    qa = _rmsnorm(qa.reshape(B, L, H_A, HD_A), g_qn)
    ka = _rmsnorm(ka.reshape(B, L, H_A, HD_A), g_kn)
    va = va.reshape(B, L, H_A, HD_A)
    qb = qb.reshape(B, L, H_B, HD_B)
    kb = kb.reshape(B, L, H_B, HD_B)
    vb = vb.reshape(B, L, H_B, HD_B)
    return qa, ka, va, qb, kb, vb, ob, gt + b_gates, br

def _mixer_output(att, hb, ob, br, g_hn, w_pa, w_pb, w_o):
    B, L = att.shape[:2]
    hb = _rmsnorm(jnp.transpose(hb, (0, 2, 1, 3)), g_hn.reshape(H_B, HD_B))
    hb = hb.reshape(B, L, B_WIDTH).astype(ob.dtype) * jax.nn.sigmoid(ob)
    g_a, g_b = jnp.split(jax.nn.sigmoid(br), 2, axis=-1)
    y = g_a * (att.reshape(B, L, A_WIDTH) @ w_pa) + g_b * (hb @ w_pb)
    return y @ w_o

def _ctx_attention(q, k, v):
    B, P, H, d = q.shape
    nb = P // Q_BLOCK
    qblk = jnp.moveaxis(q.reshape(B, nb, Q_BLOCK, H, d), 1, 0)

    def blk(qi):
        s = jnp.einsum('bqhd,bkhd->bhqk', qi, k).astype(jnp.float32) * (d ** -0.5)
        p = jax.nn.softmax(s, axis=-1).astype(v.dtype)
        return jnp.einsum('bhqk,bkhd->bqhd', p, v)

    out = lax.map(blk, qblk)
    return jnp.moveaxis(out, 0, 1).reshape(B, P, H, d)

def _na_attention(q, k, v, k_ctx, v_ctx, rpb):
    B, L, H, d = q.shape
    rows = L // GRID_W
    kh = min(WIN_H, rows)
    r = jnp.arange(rows)
    start_r = jnp.clip(r - WIN_H // 2, 0, rows - kh)
    row_idx = start_r[:, None] + jnp.arange(kh)[None, :]
    cidx = jnp.arange(GRID_W)
    start_c = jnp.clip(cidx - WIN_W // 2, 0, GRID_W - WIN_W)
    col_ok = (cidx[None, :] >= start_c[:, None]) & (cidx[None, :] < start_c[:, None] + WIN_W)
    dr = row_idx - r[:, None] + (WIN_H - 1)
    dc = jnp.clip(cidx[None, :] - cidx[:, None] + (WIN_W - 1), 0, 2 * WIN_W - 2)
    bias = rpb.astype(jnp.float32)[:, dr[:, :, None, None], dc[None, None]]
    bias = jnp.transpose(bias, (0, 1, 3, 2, 4)).reshape(H, rows, GRID_W, kh * GRID_W)
    mask = jnp.broadcast_to(col_ok[:, None, :], (GRID_W, kh, GRID_W)).reshape(GRID_W, kh * GRID_W)
    qg = q.reshape(B, rows, GRID_W, H, d)
    kg = k.reshape(B, rows, GRID_W, H, d)[:, row_idx].reshape(B, rows, kh * GRID_W, H, d)
    vg = v.reshape(B, rows, GRID_W, H, d)[:, row_idx].reshape(B, rows, kh * GRID_W, H, d)
    scale = d ** -0.5
    s_win = jnp.einsum('brqhd,brkhd->bhrqk', qg, kg).astype(jnp.float32) * scale + bias[None]
    s_win = jnp.where(mask, s_win, -1e30)
    s_ctx = jnp.einsum('brqhd,bphd->bhrqp', qg, k_ctx).astype(jnp.float32) * scale
    p = jax.nn.softmax(jnp.concatenate([s_win, s_ctx], axis=-1), axis=-1).astype(v.dtype)
    nw = kh * GRID_W
    out = (jnp.einsum('bhrqk,brkhd->brqhd', p[..., :nw], vg)
           + jnp.einsum('bhrqp,bphd->brqhd', p[..., nw:], v_ctx))
    return out.reshape(B, L, H, d)

def _rope_tables(n_tokens):
    half = HD_B // 2
    nf = half // 2
    inv = ROPE_THETA ** (-jnp.arange(nf, dtype=jnp.float32) / nf)
    t = jnp.arange(n_tokens)
    row = (t // GRID_W).astype(jnp.float32)
    col = (t % GRID_W).astype(jnp.float32)
    ang = jnp.concatenate([row[:, None] * inv, col[:, None] * inv], axis=-1)
    return jnp.cos(ang)[:, None, :], jnp.sin(ang)[:, None, :]

def _apply_rope(x, cos, sin):
    half = x.shape[-1] // 2
    xf = x.astype(jnp.float32)
    x1, x2 = xf[..., :half], xf[..., half:]
    return jnp.concatenate([x1 * cos - x2 * sin, x1 * sin + x2 * cos], axis=-1).astype(x.dtype)

def _mlstm_scan(q, k, v, ig, lf, C0, n0, m0):
    B, H, L, d = q.shape
    T = min(CHUNK, L)
    nc = L // T
    chunk = lambda a: jnp.moveaxis(a.reshape(B, H, nc, T, *a.shape[3:]), 2, 0)
    tril = jnp.tril(jnp.ones((T, T), dtype=bool))

    def step(carry, xs):
        C, n, m = carry
        qc, kc, vc, ic, fc = xs
        b = jnp.cumsum(fc, axis=-1)
        Dm = jnp.where(tril, b[..., :, None] - b[..., None, :] + ic[..., None, :], -jnp.inf)
        inter = b + m[..., None]
        m_t = jnp.maximum(inter, jnp.max(Dm, axis=-1))
        w = jnp.exp(Dm - m_t[..., None])
        a = jnp.exp(inter - m_t)
        s = jnp.einsum('bhtd,bhsd->bhts', qc, kc) * w
        num = (a[..., None] * jnp.einsum('bhvk,bhtk->bhtv', C, qc)
               + jnp.einsum('bhts,bhsv->bhtv', s, vc))
        den = a * jnp.einsum('bhk,bhtk->bht', n, qc) + jnp.sum(s, axis=-1)
        h = num / jnp.maximum(jnp.abs(den), jnp.exp(-m_t))[..., None]
        bT = b[..., -1]
        gl = bT[..., None] - b + ic
        m_new = jnp.maximum(bT + m, jnp.max(gl, axis=-1))
        a_s = jnp.exp(bT + m - m_new)
        w_s = jnp.exp(gl - m_new[..., None])
        C_new = a_s[..., None, None] * C + jnp.einsum('bhs,bhsv,bhsk->bhvk', w_s, vc, kc)
        n_new = a_s[..., None] * n + jnp.einsum('bhs,bhsk->bhk', w_s, kc)
        return (C_new, n_new, m_new), h

    (Cf, nf, mf), hs = lax.scan(step, (C0, n0, m0),
                                (chunk(q), chunk(k), chunk(v), chunk(ig), chunk(lf)))
    h = jnp.moveaxis(hs, 0, 2).reshape(B, H, L, d)
    return h, Cf, nf, mf

def _mlstm_bidir(q, k, v, gates, C0, n0, m0):
    f32 = jnp.float32
    tr = lambda a: jnp.transpose(a, (0, 2, 1, 3)).astype(f32)
    q, k, v = tr(q), tr(k), tr(v)
    B, L = gates.shape[:2]
    g = jnp.transpose(gates.astype(f32).reshape(B, L, 4, H_B), (2, 0, 3, 1))
    ig_f, lf_f = g[0], jax.nn.log_sigmoid(g[1])
    ig_b, lf_b = g[2], jax.nn.log_sigmoid(g[3])
    C0, n0, m0 = C0.astype(f32), n0.astype(f32), m0.astype(f32)
    h_f, Cf, nf, mf = _mlstm_scan(q, k, v, ig_f, lf_f, C0[:, 0], n0[:, 0], m0[:, 0])
    fl = lambda a: jnp.flip(a, axis=2)
    h_b, Cb, nb, mb = _mlstm_scan(fl(q), fl(k), fl(v), fl(ig_b), fl(lf_b), C0[:, 1], n0[:, 1], m0[:, 1])
    h = h_f + fl(h_b)
    return h, jnp.stack([Cf, Cb], axis=1), jnp.stack([nf, nb], axis=1), jnp.stack([mf, mb], axis=1)

def setup_inputs(seed: int = 0) -> dict:
    key = jax.random.key(seed)
    ks = jax.random.split(key, 32)
    nrm = lambda k, shape, s=1.0: jax.random.normal(k, shape, jnp.float32) * s
    b_gates = jnp.concatenate([
        nrm(ks[24], (DEPTH, H_B), 0.1),
        3.0 + nrm(ks[25], (DEPTH, H_B), 0.5),
        nrm(ks[26], (DEPTH, H_B), 0.1),
        3.0 + nrm(ks[27], (DEPTH, H_B), 0.5)], axis=-1)
    return {
        "x_prompt": nrm(ks[0], (BATCH, SEQ, D_MODEL)),
        "x_sample": nrm(ks[1], (DEC_BATCH, DEC_SEQ, D_MODEL)),
        "cache_k": nrm(ks[2], (DEC_BATCH, DEPTH, PAST_LEN, H_A, HD_A)),
        "cache_v": nrm(ks[3], (DEC_BATCH, DEPTH, PAST_LEN, H_A, HD_A)),
        "state_C": nrm(ks[4], (DEC_BATCH, DEPTH, 2, H_B, HD_B, HD_B), 0.1),
        "state_n": nrm(ks[5], (DEC_BATCH, DEPTH, 2, H_B, HD_B), 0.3),
        "state_m": nrm(ks[6], (DEC_BATCH, DEPTH, 2, H_B), 0.5),
        "c": nrm(ks[7], (DEC_BATCH, D_MODEL)),
        "c_ctx": nrm(ks[8], (D_MODEL,)),
        "w_ada": nrm(ks[9], (DEPTH, D_MODEL, N_MOD * D_MODEL), D_MODEL ** -0.5),
        "b_ada": nrm(ks[10], (DEPTH, N_MOD * D_MODEL), 0.02),
        "g_norm": 1.0 + nrm(ks[11], (DEPTH, 3, D_MODEL), 0.05),
        "w_up1": nrm(ks[12], (DEPTH, D_MODEL, 2 * D_FF), D_MODEL ** -0.5),
        "w_dn1": nrm(ks[13], (DEPTH, D_FF, D_MODEL), D_FF ** -0.5),
        "w_in": nrm(ks[14], (DEPTH, D_MODEL, IN_COLS), D_MODEL ** -0.5),
        "b_gates": b_gates,
        "g_qn": 1.0 + nrm(ks[15], (DEPTH, HD_A), 0.05),
        "g_kn": 1.0 + nrm(ks[16], (DEPTH, HD_A), 0.05),
        "rpb": nrm(ks[17], (DEPTH, H_A, 2 * WIN_H - 1, 2 * WIN_W - 1), 0.1),
        "g_hn": 1.0 + nrm(ks[18], (DEPTH, B_WIDTH), 0.05),
        "w_pa": nrm(ks[19], (DEPTH, A_WIDTH, D_MODEL), A_WIDTH ** -0.5),
        "w_pb": nrm(ks[20], (DEPTH, B_WIDTH, D_MODEL), B_WIDTH ** -0.5),
        "w_o": nrm(ks[21], (DEPTH, D_MODEL, D_MODEL), D_MODEL ** -0.5),
        "w_up2": nrm(ks[22], (DEPTH, D_MODEL, 2 * D_FF), D_MODEL ** -0.5),
        "w_dn2": nrm(ks[23], (DEPTH, D_FF, D_MODEL), D_FF ** -0.5),
    }

def reference(x_prompt, x_sample, cache_k, cache_v, state_C, state_n, state_m, c, c_ctx,
              w_ada, b_ada, g_norm, w_up1, w_dn1, w_in, b_gates, g_qn, g_kn, rpb, g_hn,
              w_pa, w_pb, w_o, w_up2, w_dn2):
    B = x_prompt.shape[0]
    L = x_sample.shape[1]
    kscale = HD_B ** -0.5
    cos, sin = _rope_tables(L)
    zC = jnp.zeros((B, 2, H_B, HD_B, HD_B), jnp.float32)
    zn = jnp.zeros((B, 2, H_B, HD_B), jnp.float32)
    zm = jnp.zeros((B, 2, H_B), jnp.float32)
    xp, xs = x_prompt, x_sample
    ks_out, vs_out, Cs_out, ns_out, ms_out = [], [], [], [], []
    for l in range(DEPTH):
        mc = _ada(c_ctx[None], w_ada[l], b_ada[l])
        ml = _ada(c, w_ada[l], b_ada[l])

        xp = _ffn_sub(xp, g_norm[l, 0], mc[:, :, 0], mc[:, :, 1], mc[:, :, 2], w_up1[l], w_dn1[l])
        qa, ka, va, qb, kb, vb, ob, gt, br = _mixer_inputs(
            xp, g_norm[l, 1], mc[:, :, 3], mc[:, :, 4], w_in[l], b_gates[l], g_qn[l], g_kn[l])
        att = _ctx_attention(qa, ka, va)
        hb, Cc, nc_, mc_s = _mlstm_bidir(qb, kb * kscale, vb, gt, zC, zn, zm)
        xp = xp + mc[:, :, 5] * _mixer_output(att, hb, ob, br, g_hn[l], w_pa[l], w_pb[l], w_o[l])
        xp = _ffn_sub(xp, g_norm[l, 2], mc[:, :, 6], mc[:, :, 7], mc[:, :, 8], w_up2[l], w_dn2[l])
        ks_out.append(ka)
        vs_out.append(va)
        Cs_out.append(Cc)
        ns_out.append(nc_)
        ms_out.append(mc_s)

        xs = _ffn_sub(xs, g_norm[l, 0], ml[:, :, 0], ml[:, :, 1], ml[:, :, 2], w_up1[l], w_dn1[l])
        qa, ka, va, qb, kb, vb, ob, gt, br = _mixer_inputs(
            xs, g_norm[l, 1], ml[:, :, 3], ml[:, :, 4], w_in[l], b_gates[l], g_qn[l], g_kn[l])
        att = _na_attention(qa, ka, va, cache_k[:, l], cache_v[:, l], rpb[l])
        qb = _apply_rope(qb, cos, sin)
        kb = _apply_rope(kb, cos, sin)
        hb, _, _, _ = _mlstm_bidir(qb, kb * kscale, vb, gt, state_C[:, l], state_n[:, l], state_m[:, l])
        xs = xs + ml[:, :, 5] * _mixer_output(att, hb, ob, br, g_hn[l], w_pa[l], w_pb[l], w_o[l])
        xs = _ffn_sub(xs, g_norm[l, 2], ml[:, :, 6], ml[:, :, 7], ml[:, :, 8], w_up2[l], w_dn2[l])

    new_cache_k = jnp.stack(ks_out, axis=1)
    new_cache_v = jnp.stack(vs_out, axis=1)
    new_state_C = jnp.stack(Cs_out, axis=1)
    new_state_n = jnp.stack(ns_out, axis=1)
    new_state_m = jnp.stack(ms_out, axis=1)
    return (xp, xs, new_cache_k, new_cache_v, new_state_C, new_state_n, new_state_m)


_drawn_inputs = setup_inputs


def setup_inputs(seed=0):
    import zlib

    import numpy as np

    out = dict(_drawn_inputs(seed))
    spreads = {}
    factors = {'state_C': 4.77, 'state_n': 4.484, 'state_m': 8.0, 'g_qn': 8.0, 'rpb': 8.0, 'g_hn': 4.675}
    for name, (base, spread) in spreads.items():
        noise = np.random.default_rng([zlib.crc32(name.encode()), seed]).standard_normal(out[name].shape)
        drawn = base * np.exp(spread * noise) if base else spread * noise
        out[name] = __import__('jax').numpy.asarray(drawn.astype(out[name].dtype))
    for name, factor in factors.items():
        out[name] = (out[name] * factor).astype(out[name].dtype)
    return out
```

```python
from contextlib import ExitStack

import concourse.bass as bass
from concourse import mybir

F32 = mybir.dt.float32
F32R = mybir.dt.float32r
ACT = mybir.ActivationFunctionType
ALU = mybir.AluOpType
AX_X = mybir.AxisListType.X

P = 128
D_MODEL = 1024
KT = D_MODEL // P
DEPTH = 2
GRID_W = 64
NLAT = 512
NCTX = 128
NTOK = NLAT + NCTX
ROWS = NLAT // GRID_W
H_A, HD_A = 8, 64
H_B, HD_B = 4, 128
D_FF = 2816
N_MOD = 9
EPS = 1e-6
CH = NTOK // P
LCH = NLAT // P
FF_PARTS = (8, 8, 6)
assert sum(FF_PARTS) * P == D_FF
VW = HD_B + 1
ROWP = 36
FROW = 64
QB_KEY = (0, 64, 192, 256)
QB_KIND = (0, 1, 1, 2)
WIN = 256
NUNIT = H_A * CH

C_ID, C_BO, C_ON, C_ROT, C_MASK, C_RESET = 0, 128, 256, 384, 512, 768
C_EPS = C_RESET + NTOK
N_CONST = C_EPS + 1
P_BADA, P_GN, P_GQK, P_GHN, P_BG, P_M0 = 0, 72, 96, 98, 102, 103
N_PAR = 104

ROW_STEPS, ROW_ABS, ROW_M = 18, 1, 8
NUM_FWD, NUM_BWD = 9, 10
NUM_STEPS = H_B * (NUM_FWD + NUM_BWD)

ADA_PAIRS = N_MOD * KT // 2
FFN_PAIRS = D_FF // P + 3 * KT // 2
INA_PAIRS, INB_PAIRS, OB_PAIRS, Y_PAIRS, O_PAIRS = 6, 6, 2, 2 * KT, KT // 2
MIX_PAIRS = INA_PAIRS + INB_PAIRS + OB_PAIRS + Y_PAIRS + O_PAIRS
PAIRS = 2 * FFN_PAIRS + MIX_PAIRS
SPLITS = (PAIRS + 1, PAIRS)
USES = (ADA_PAIRS + SPLITS[0], ADA_PAIRS + SPLITS[1])
BUF = PAIRS // 2
X_UPD = 2 * 3 * KT + KT
X_IN = 16
H_TILES = 4 * KT


def build(nc, io):
    with ExitStack() as ctx:
        def sb(name, shape, dt=F32):
            return ctx.enter_context(nc.sbuf_tensor(name, shape, dt))

        def sem(name):
            return ctx.enter_context(nc.semaphore(name))

        x = sb("x", [P, KT, NTOK])
        h_hi = sb("h_hi", [P, KT, NTOK], F32R)
        h_lo = sb("h_lo", [P, KT, NTOK], F32R)
        g_hi = sb("g_hi", [P, 8, NTOK], F32R)
        g_lo = sb("g_lo", [P, 8, NTOK], F32R)
        w_raw = sb("w_raw", [P, 2, 1024])
        w_hi = sb("w_hi", [P, 2, 1024], F32R)
        w_lo = sb("w_lo", [P, 2, 1024], F32R)
        pool = sb("pool", [P, 19328])
        const = sb("const", [P, N_CONST])
        par = sb("par", [P, N_PAR])
        cond = sb("cond", [P, KT, 2])
        mod = sb("mod", [P, N_MOD * KT, 2])
        mod_a = sb("mod_a", [P, 3, KT, 2])
        gate = sb("gate", [P, 3, KT, 2])
        stat = sb("stat", [P, 3, NUNIT])
        small = sb("small", [P, 80])
        eps = const[:, C_EPS:C_EPS + 1]

        def area(at, *shape):
            n = 1
            for s in shape:
                n *= s
            a = pool[:, at:at + n]
            if len(shape) == 2:
                return a.rearrange("p (a b) -> p a b", b=shape[1])
            if len(shape) == 3:
                return a.rearrange("p (a b c) -> p a b c", b=shape[1], c=shape[2])
            return a

        hx, sq, rstd = area(0, 2, NTOK), area(2 * NTOK, 2, NTOK), area(4 * NTOK, NTOK)
        sg, gt = area(5 * NTOK, 2, NTOK), area(7 * NTOK, 2, NTOK)
        qkv = area(0, 12, NTOK)
        att = area(8 * NTOK, CH, H_A * HD_A)
        v_tok = area(7680, 8, 512)
        cache_v, cache_k = area(11776, 512), area(12288, 4, P)
        bias = area(12800, 6, 384)
        s_neg, p_att, p_t = area(15104, 2, 384), area(15872, 2, 384), area(16640, 2, 384)
        qsq, qrs = area(15104, 2, NTOK), area(16384, 1024)
        wt, st, hnum = area(5120, NTOK), area(5760, NTOK), area(6400, CH, VW)
        c_out = area(7045, 2, VW)
        v_aug = area(7680, CH, H_B, VW)
        k_tok = area(10260, CH, 512)
        cos, sin = area(10260, NTOK), area(10900, NLAT)
        hb = area(12820, CH, 512)
        num, kw = area(15380, CH, VW), area(16025, CH, P)
        col = area(16665, 4, CH * ROWP)
        row_gate, row_m_rel = area(17408, NTOK), area(18048, NTOK)
        row_exp, row_lf, row_b, row_m = (area(12820 + i * NTOK, NTOK) for i in range(4))
        row_g, row_a, row_w = area(15380, NTOK), area(16020, NTOK), area(18688, NTOK)
        rtmp = area(12820, 2, NLAT)
        c_seq = [area(17408, LCH, VW), area(18688, LCH, VW)]
        hsq = area(10260, CH, 512)
        ob_sig, y = area(0, H_B, NTOK), area(2560, KT, NTOK)
        br_sig, ty = area(7680, 2, NTOK), area(8960, 2, NTOK)
        hbt = area(10260, 2, 512)

        ident = const[:, C_ID:C_ID + P]
        head_ones, mean_ones = const[:, C_BO:C_BO + P], const[:, C_ON:C_ON + P]
        rot = const[:, C_ROT:C_ROT + P]
        mask = const[:, C_MASK:C_MASK + 2 * P].rearrange("p (a b) -> p a b", b=P)
        reset = const[:, C_RESET:C_RESET + NTOK]
        mprev, dec = small[:, 0:8], small[:, 8:48].rearrange("p (a b) -> p a b", b=CH)
        hss, den = small[:, 48:68], small[:, 68:73]
        gcols = col.rearrange("p k (c r) -> p k c r", r=ROWP)

        bank = [ctx.enter_context(nc.psum_tensor(f"pair{b}", [P, 3, 512], F32)) for b in range(2)]
        m1 = ctx.enter_context(nc.psum_tensor("m1", [P, 512], F32))
        m2 = ctx.enter_context(nc.psum_tensor("m2", [P, 512], F32))
        pa, pb = bank

        def lat(b, n=2):
            return bank[b][:, 0:n, :]

        def cx(b, n=2):
            return bank[b][:, 2, 0:n * P].rearrange("p (a b) -> p a b", b=P)

        def by_column(ap):
            return ap.rearrange("p (c r) -> p r c", r=ROWS)

        def by_row(ap):
            return ap.rearrange("p (r c) -> p r c", r=ROWS)

        const_in = sem("const_in")
        par_in = sem("par_in")
        x_upd = sem("x_upd")
        landed = [sem("landed0"), sem("landed1")]
        raw_free = [sem("raw_free0"), sem("raw_free1")]
        hi_ready = [sem("hi_ready0"), sem("hi_ready1")]
        lo_ready = [sem("lo_ready0"), sem("lo_ready1")]
        strip_done = [sem("strip_done0"), sem("strip_done1")]
        taken = [sem("taken0"), sem("taken1")]
        cond_ready = sem("cond_ready")
        mods = sem("mods")
        sq_ready, sq_used, ln_done, rstd_ready = sem("sq_ready"), sem("sq_used"), sem("ln_done"), sem("rstd_ready")
        h_scaled, h_mod, h_hi_ready, h_lo_ready = (sem(s) for s in ("h_scaled", "h_mod", "h_hi_ready", "h_lo_ready"))
        silu_done, g_hi_ready, g_lo_ready = (sem(s) for s in ("silu_done", "g_hi_ready", "g_lo_ready"))
        gate_taken = sem("gate_taken")
        qsq_ready, qss_done, qln_done, qrs_ready, qk_normed = (sem(s) for s in ("qsq_ready", "qss_done", "qln_done", "qrs_ready", "qk_normed"))
        vt_done, vt_taken = sem("vt_done"), sem("vt_taken")
        bias_in = [sem("bias_in0"), sem("bias_in1")]
        s_done, s_taken, p_ready, pt_done, pt_taken = (sem(s) for s in ("s_done", "s_taken", "p_ready", "pt_done", "pt_taken"))
        pv_done, rinv_ready, att_ready = sem("pv_done"), sem("rinv_ready"), sem("att_ready")
        at_done, at_hi, at_lo = sem("at_done"), sem("at_hi"), sem("at_lo")
        kv_out, rope_in = sem("kv_out"), sem("rope_in")
        gq = sem("gq")
        rot_done, rope_step = sem("rot_done"), sem("rope_step")
        kt_done, kt_taken, va_done, va_taken, ones_set = (sem(s) for s in ("kt_done", "kt_taken", "va_done", "va_taken", "ones_set"))
        row_step, row_act = sem("row_step"), sem("row_act")
        cols_done, cols_ready = sem("cols_done"), sem("cols_ready")
        c_in = [sem("c_in0"), sem("c_in1")]
        kq_done, mb_done, mb_taken, wt_ready, st_ready, kw_ready, upd_done = (sem(s) for s in (
            "kq_done", "mb_done", "mb_taken", "wt_ready", "st_ready", "kw_ready", "upd_done"))
        intra_done, inter_done, c_step, num_step = sem("intra_done"), sem("inter_done"), sem("c_step"), sem("num_step")
        cout_ready, cout_out, m_out = sem("cout_ready"), sem("cout_out"), sem("m_out")
        hb_step, hb_act = sem("hb_step"), sem("hb_act")
        ht_done, ht_prod, ht_hi, ht_lo = (sem(s) for s in ("ht_done", "ht_prod", "ht_hi", "ht_lo"))
        ob_done, br_done, ty_step = sem("ob_done"), sem("br_done"), sem("ty_step")
        out_done = sem("out_done")

        F1 = 0
        INA = FFN_PAIRS
        INB = INA + INA_PAIRS
        OB = INB + INB_PAIRS
        YS = OB + OB_PAIRS
        OS = YS + Y_PAIRS
        F2 = OS + O_PAIRS

        def fills(l, pair):
            return l * BUF + pair // 2 + 1

        def filled(l, pair):
            return l * PAIRS + pair + 2

        def row_of(n):
            return 32 * (n % 2) + n // 2

        def steps_before(l, n):
            return l * NUM_STEPS + (n // 2) * (NUM_FWD + NUM_BWD) + (n % 2) * NUM_FWD

        def at_views(dst, c):
            src = pa[:, c % 2, :]
            if c == LCH:
                return src.rearrange("p (f t) -> p f t", f=4), dst[:, 0:4, NLAT:NTOK]
            w = GRID_W // LCH
            return (src.rearrange("p (f c r) -> p f c r", f=4, r=ROWS),
                    dst[:, 0:4, 0:NLAT].rearrange("p f (r c) -> p f c r", r=ROWS)[:, :, c * w:(c + 1) * w, :])

        settled = sem("settled")

        def settle(eng):
            eng.sem_inc(settled, 1)

        block = ctx.enter_context(nc.Block())

        @block.sync
        def _(sp):
            sp.dma_start(x[:], io["x"]).then_inc(x_upd, X_IN)
            for s in range(2):
                sp.sem_inc(raw_free[s], 1)

            def load(s, l, use, src):
                sp.wait_ge(raw_free[s], l * USES[s] + use + 1)
                sp.dma_start(w_raw[:, s, 0:src.shape[-1]], src).then_inc(landed[s], 16)

            def stream(l, pairs, use, src):
                with sp.Fori(0, pairs) as i:
                    for s in range(2):
                        load(s, l, use[s] + i, src[l, bass.ds(i * 2 + s, 1), :, :].rearrange("a p n -> p (a n)"))

            def ffn(l, use, up, dn, dn_last):
                for f, n in enumerate(FF_PARTS):
                    first = sum(FF_PARTS[:f])
                    stream(l, n, [u + first + 4 * f for u in use], up[:, 2 * first:2 * (first + n)])
                    src = dn[:, f * KT:(f + 1) * KT] if f < 2 else dn_last
                    stream(l, KT // 2, [u + first + n + 4 * f for u in use], src)

            with sp.Fori(0, DEPTH) as l:
                stream(l, ADA_PAIRS, (0, 0), io["w_ada"])
                A = ADA_PAIRS
                ffn(l, (A, A), io["up1"], io["dn1a"], io["dn1b"])
                load(0, l, A + INA, io["wg"][bass.ds(l, 1)].rearrange("a p n -> p (a n)"))
                stream(l, INA_PAIRS, (A + INA + 1, A + INA), io["w_in"][:, 0:12])
                for s in range(2):
                    load(s, l, A + INB + 1 - s, io["w_in"][bass.ds(l, 1), 12 + s].rearrange("a p n -> p (a n)"))
                sp.wait_ge(h_lo_ready, l * H_TILES + KT + 1)
                for h in range(H_A):
                    if h >= 2:
                        sp.wait_ge(s_taken, l * NUNIT + (h - 1) * CH)
                    sp.dma_start(bias[:, 3 * (h % 2):3 * (h % 2) + 3, :],
                                 io["bias"][bass.ds(l, 1), h].rearrange("a p k n -> p (a k) n")
                                 ).then_inc(bias_in[h % 2], 16)
                with sp.Fori(1, INB_PAIRS) as i:
                    for s in range(2):
                        load(s, l, A + INB + 1 - s + i,
                             io["w_in"][l, bass.ds(i * 2 + 12 + s, 1), :, :].rearrange("a p n -> p (a n)"))
                stream(l, OB_PAIRS, (A + OB + 1, A + OB), io["w_in"][:, 24:28])
                with sp.Fori(0, KT) as d:
                    for s in range(2):
                        load(s, l, d * 2 + (A + YS + 1 - s),
                             io["w_in"][l, bass.ds(d * 2 + 28 + s, 1), :, :].rearrange("a p n -> p (a n)"))
                    for s in range(2):
                        load(s, l, d * 2 + (A + YS + 2 - s),
                             io["w_pab"][l, bass.ds(d * 2 + s, 1), :, :].rearrange("a p n -> p (a n)"))
                stream(l, O_PAIRS, (A + OS + 1, A + OS), io["w_o"])
                ffn(l, (A + F2 + 1, A + F2), io["up2"], io["dn2a"], io["dn2b"])
            sp.wait_ge(x_upd, X_IN + DEPTH * X_UPD)
            sp.dma_start(io["y"], x[:]).then_inc(out_done, 16)
            sp.wait_ge(out_done, 16)
            sp.wait_ge(kv_out, DEPTH * 32)
            sp.wait_ge(cout_out, DEPTH * 8 * 16)
            sp.wait_ge(m_out, DEPTH * 32)

        @block.gpsimd
        def _(po):
            def split_lo(s, l, n):
                po.wait_ge(hi_ready[s], l * SPLITS[s] + n + 1)
                nc.gpsimd.tensor_tensor(w_lo[:, s, :], w_raw[:, s, :], w_hi[:, s, :].bitcast(F32),
                                        ALU.subtract).then_inc(lo_ready[s], 1)
                po.wait_ge(lo_ready[s], l * SPLITS[s] + n + 1)
                po.sem_inc(raw_free[s], 1)

            with po.Fori(0, DEPTH) as l:
                with po.Fori(0, INA) as i:
                    for s in range(2):
                        split_lo(s, l, i)
                split_lo(0, l, INA)
                with po.Fori(0, INA_PAIRS) as i:
                    for s in range(2):
                        split_lo(s, l, i + INA + 1 - s)
                po.wait_ge(qk_normed, (l + 1) * 8)
                settle(po)
                po.dma_start(io["new_k"][bass.ds(l, 1)].rearrange("a p f t -> p (a f) t"),
                             qkv[:, 4:8, NLAT:NTOK]).then_inc(kv_out, 16)
                po.wait_ge(taken[1], fills(l, INB - 1) + 1)
                settle(po)
                po.dma_start(io["new_v"][bass.ds(l, 1)].rearrange("a p f t -> p (a f) t"),
                             qkv[:, 8:12, NLAT:NTOK]).then_inc(kv_out, 16)
                for s in range(2):
                    split_lo(s, l, INB + 1 - s)
                po.wait_ge(at_done, (l + 1) * CH)
                settle(po)
                po.dma_start(pool[:, 10260:10260 + NTOK + NLAT], io["rope"]).then_inc(rope_in, 16)
                with po.Fori(1, INB_PAIRS) as i:
                    for s in range(2):
                        split_lo(s, l, i + INB + 1 - s)
                for s in range(2):
                    split_lo(s, l, OB + 1 - s)
                po.wait_ge(row_step, l * ROW_STEPS + ROW_M)
                settle(po)
                po.dma_start(io["new_m"][bass.ds(l, 1), 0].rearrange("a h o -> (a h) o"),
                             row_m[0:H_B, NTOK - 1:NTOK]).then_inc(m_out, 16)
                po.dma_start(io["new_m"][bass.ds(l, 1), 1].rearrange("a h o -> (a h) o"),
                             row_m[32:32 + H_B, NLAT:NLAT + 1]).then_inc(m_out, 16)
                for n in range(2 * H_B):
                    if n < 2:
                        po.wait_ge(cols_done, (l + 1) * 2)
                        po.wait_ge(row_step, (l + 1) * ROW_STEPS)
                    else:
                        po.wait_ge(inter_done, l * 8 + n - 1)
                    settle(po)
                    po.dma_start(c_seq[n % 2][:, 0:1, :], io["state_c"][bass.ds(l, 1), :, n, :]
                                 .rearrange("a p n -> p a n")).then_inc(c_in[n % 2], 16)
                    if n >= 1:
                        po.wait_ge(cout_ready, l * 8 + n)
                        settle(po)
                        po.dma_start(io["new_c"][bass.ds(l, 1), :, n - 1, :].rearrange("a p n -> p a n"),
                                     c_out[:, (n - 1) % 2:(n - 1) % 2 + 1, :]).then_inc(cout_out, 16)
                po.wait_ge(cout_ready, l * 8 + 8)
                settle(po)
                po.dma_start(io["new_c"][bass.ds(l, 1), :, 7, :].rearrange("a p n -> p a n"),
                             c_out[:, 1:2, :]).then_inc(cout_out, 16)
                with po.Fori(1, PAIRS - OB) as i:
                    for s in range(2):
                        split_lo(s, l, i + OB + 1 - s)

        @block.scalar
        def _(ac):
            ac.dma_start(const[:], io["const"]).then_inc(const_in, 16)
            ac.dma_start(cond[:], io["cond"]).then_inc(const_in, 16)
            for s in range(2):
                ac.sem_inc(strip_done[s], 1)
                ac.sem_inc(taken[s], 1)
            ac.wait_ge(const_in, 32)
            nc.scalar.activation(cond[:], cond[:], ACT.Silu).then_inc(cond_ready, 1)

            def split_hi(s, l, n):
                ac.wait_ge(strip_done[s], l * SPLITS[s] + n + 1)
                ac.wait_ge(landed[s], (l * USES[s] + n) * 16 + 16 * (ADA_PAIRS + 1))
                nc.scalar.activation(w_hi[:, s, :], w_raw[:, s, :], ACT.Copy).then_inc(hi_ready[s], 1)

            def norm(l, i):
                n, done = (l * 3 + i) * KT, X_IN + l * X_UPD + (0, 3 * KT, 4 * KT)[i]
                for k in range(KT):
                    if i == 0 and k == 0:
                        ac.wait_ge(x_upd, done)
                    if i > 0:
                        ac.wait_ge(x_upd, done - KT + k + 1)
                    if k >= 2:
                        ac.wait_ge(sq_used, n + k - 1)
                    nc.scalar.activation(sq[:, k % 2, :], x[:, k, :], ACT.Square).then_inc(sq_ready, 1)
                ac.wait_ge(sq_used, n + KT)
                nc.scalar.activation(rstd[:, 0:NLAT], m1[:], ACT.Ln, bias=eps).then_inc(ln_done, 1)
                nc.scalar.activation(rstd[:, NLAT:NTOK], m2[:, 0:NCTX], ACT.Ln, bias=eps).then_inc(ln_done, 1)
                ac.wait_ge(ln_done, (l * 3 + i) * 2 + 2)
                nc.scalar.activation(rstd, rstd, ACT.Exp, scale=-0.5).then_inc(rstd_ready, 1)
                m = l * H_TILES + (0, KT, 3 * KT)[i]
                for k in range(KT):
                    ac.wait_ge(h_mod, (n + k + 1) * 2)
                    nc.scalar.activation(h_hi[:, k, :], hx[:, k % 2, :], ACT.Copy).then_inc(h_hi_ready, 1)

            def ffn(l, base, split, j, last):
                for f, n in enumerate(FF_PARTS):
                    first = sum(FF_PARTS[:f])
                    at = base + first + 4 * f
                    with ac.Fori(0, n // 2) as q:
                        for b in range(2):
                            for s in range(2):
                                split_hi(s, l, q * 2 + (at + b + 1 + (split if s == 0 else 0)))
                            ac.wait_ge(strip_done[1], q * 2 + filled(l, at + b))
                            nc.scalar.activation(sg[:, b, 0:NLAT], bank[b][:, 0, :], ACT.Silu)
                            nc.scalar.activation(sg[:, b, NLAT:NTOK], bank[b][:, 2, 0:P], ACT.Silu)\
                                .then_inc(silu_done, 1)
                            ac.wait_ge(taken[b], q + (fills(l, at + b) + 1))
                            nc.scalar.activation(g_hi[:, bass.ds(q * 2 + b, 1), :],
                                                 gt[:, b:b + 1, :], ACT.Copy).then_inc(g_hi_ready, 1)
                    at += n
                    pairs = KT // 2 - (1 if last and f == 2 else 0)
                    with ac.Fori(0, pairs) as i:
                        for s in range(2):
                            split_hi(s, l, i + (at + 1 + (split if s == 0 else 0)))

            def q_rs(l, t):
                nc.scalar.activation(qrs[:, 0:NLAT], m1[:], ACT.Ln, bias=eps).then_inc(qln_done, 1)
                nc.scalar.activation(qrs[:, NLAT:NTOK], m2[:, 0:NCTX], ACT.Ln, bias=eps).then_inc(qln_done, 1)
                ac.wait_ge(qln_done, (l * 8 + t) * 2 + 2)
                nc.scalar.activation(qrs[:, 0:NTOK], qrs[:, 0:NTOK], ACT.Exp, scale=-0.5).then_inc(qrs_ready, 1)

            with ac.Fori(0, DEPTH) as l:
                ac.wait_ge(x_upd, l * X_UPD + X_IN)
                ac.dma_start(par[:], io["par"][bass.ds(l, 1)].rearrange("a p n -> p (a n)")).then_inc(par_in, 16)
                ac.dma_start(cache_v, io["cache_v"][bass.ds(l, 1)].rearrange("a p n -> p (a n)")).then_inc(par_in, 16)
                ac.dma_start(cache_k, io["cache_k"][bass.ds(l, 1)].rearrange("a p f n -> p (a f) n")).then_inc(par_in, 16)
                for s in range(2):
                    split_hi(s, l, 0)
                norm(l, 0)
                ffn(l, F1, 0, 0, False)
                norm(l, 1)
                split_hi(0, l, INA + 1)
                with ac.Fori(0, INA_PAIRS) as i:
                    for s in range(2):
                        split_hi(s, l, i + (INA + 1 + 1 - s))
                for t in range(8):
                    n = l * 8 + t
                    ac.wait_ge(taken[(t // 2) % 2], fills(l, INA + t // 2) + 1)
                    if t >= 2:
                        ac.wait_ge(qss_done, n - 1)
                    nc.scalar.activation(qsq[:, t % 2, :], qkv[:, t, :], ACT.Square).then_inc(qsq_ready, 1)
                    if t >= 1:
                        ac.wait_ge(qss_done, n)
                        ac.wait_ge(qk_normed, n - 1) if t >= 2 else None
                        q_rs(l, t - 1)
                ac.wait_ge(qss_done, l * 8 + 8)
                ac.wait_ge(qk_normed, l * 8 + 7)
                q_rs(l, 7)
                for i in range(8):
                    ac.wait_ge(vt_done, l * 8 + i + 1)
                    nc.scalar.activation(v_tok[:, i, :], (pa if i % 2 == 0 else pb)[:, 2, :], ACT.Copy)\
                        .then_inc(vt_taken, 1)
                for u in range(NUNIT + 1):
                    n = l * NUNIT + u
                    if u < NUNIT:
                        lo, hi = (0, 384) if u % CH < LCH else (WIN, 384)
                        ac.wait_ge(s_taken, n + 1)
                        if u >= 2:
                            ac.wait_ge(pt_done, n - 1)
                        nc.scalar.activation(p_att[:, u % 2, lo:hi], s_neg[:, u % 2, lo:hi], ACT.Exp, scale=-1.0,
                                             bias=stat[:, 0, u:u + 1], accum_out=stat[:, 1, u:u + 1])\
                            .then_inc(p_ready, 1)
                    if u >= 1:
                        v = u - 1
                        lo, hi = (0, 384) if v % CH < LCH else (WIN, 384)
                        ac.wait_ge(pt_done, n)
                        if v >= 2:
                            ac.wait_ge(pv_done, n - 2)
                        src = (pa[:, 2, :], pb[:, 0, :])[v % 2]
                        nc.scalar.activation(p_t[:, v % 2, lo:hi], src[:, lo:hi], ACT.Copy).then_inc(pt_taken, 1)
                for c in range(CH):
                    ac.wait_ge(at_done, l * CH + c + 1)
                    src, dst = at_views(g_hi, c)
                    nc.scalar.activation(dst, src, ACT.Copy).then_inc(at_hi, 1)
                with ac.Fori(0, INB_PAIRS) as i:
                    for s in range(2):
                        split_hi(s, l, i + (INB + 1 + 1 - s))
                fr = slice(FROW, FROW + ROWP)
                ac.wait_ge(row_step, l * ROW_STEPS + ROW_ABS)
                nc.scalar.activation(row_exp[fr, :], row_exp[fr, :], ACT.Exp, scale=-1.0).then_inc(row_act, 1)
                ac.wait_ge(row_act, l * 2 + 1)
                nc.scalar.activation(row_exp[fr, :], row_exp[fr, :], ACT.Ln, bias=1.0).then_inc(row_act, 1)
                for c in range(CH):
                    ac.wait_ge(va_done, l * CH + c + 1)
                    nc.scalar.activation(v_aug[:, c, :, 0:HD_B], (pb[:, 1, :], pb[:, 2, :])[c % 2]
                                         .rearrange("p (h d) -> p h d", h=H_B), ACT.Copy).then_inc(va_taken, 1)
                ac.wait_ge(cols_done, l * 2 + 2)
                nc.scalar.activation(col[:, 0, :], m1[:, 0:180], ACT.Copy).then_inc(cols_ready, 1)
                nc.scalar.activation(col[:, 1, :], m1[:, 180:360], ACT.Exp).then_inc(cols_ready, 1)
                nc.scalar.activation(small[:, 8:48], m1[:, 360:400], ACT.Exp).then_inc(cols_ready, 1)
                nc.scalar.activation(col[:, 2, :], m2[:, 0:180], ACT.Exp).then_inc(cols_ready, 1)
                nc.scalar.activation(col[:, 3, :], m2[:, 180:360], ACT.Exp, scale=-1.0).then_inc(cols_ready, 1)
                ac.wait_ge(cols_ready, l * 5 + 5)
                for n in range(2 * H_B):
                    h, back = n // 2, n % 2
                    ac.wait_ge(mb_taken, (l * 8 + n + 1) * 2)
                    for c in range(CH):
                        nc.scalar.activation(wt[:, c * P:(c + 1) * P], wt[:, c * P:(c + 1) * P], ACT.Exp, scale=-1.0,
                                             bias=gcols[:, 0, c, 32 * back + h:32 * back + h + 1]).then_inc(wt_ready, 1)
                ac.wait_ge(hb_step, l * 3 + 2)
                nc.scalar.activation(hss, hss, ACT.Ln, scale=1.0 / HD_B, bias=eps).then_inc(hb_act, 1)
                ac.wait_ge(hb_act, l * 2 + 1)
                nc.scalar.activation(hss, hss, ACT.Exp, scale=-0.5).then_inc(hb_act, 1)
                for p in range(OB_PAIRS):
                    for s in range(2):
                        split_hi(s, l, OB + p + 1 + 1 - s)
                    ac.wait_ge(strip_done[1], filled(l, OB + p))
                    nc.scalar.activation(ob_sig[:, 2 * p:2 * p + 2, 0:NLAT], lat(p), ACT.Sigmoid).then_inc(ob_done, 1)
                    nc.scalar.activation(ob_sig[:, 2 * p:2 * p + 2, NLAT:NTOK], cx(p), ACT.Sigmoid)\
                        .then_inc(taken[p], 1)
                    ac.wait_ge(taken[p], fills(l, OB + p) + 1)
                    for t in range(2 * p, 2 * p + 2):
                        nc.scalar.activation(ob_sig[:, t, :], ob_sig[:, t, :], ACT.Copy,
                                             scale=par[:, P_GHN + t:P_GHN + t + 1]).then_inc(ob_done, 1)
                for c in range(CH):
                    ac.wait_ge(ht_prod, l * CH + c + 1)
                    nc.scalar.activation(g_hi[:, 4:8, c * P:(c + 1) * P],
                                         hbt[:, c % 2, :].rearrange("p (f t) -> p f t", f=4), ACT.Copy).then_inc(ht_hi, 1)
                with ac.Fori(0, KT) as d:
                    for s in range(2):
                        split_hi(s, l, d * 2 + (YS + 1 + 1 - s))
                    ac.wait_ge(strip_done[1], d * 2 + filled(l, YS))
                    ac.wait_ge(taken[1], d + fills(l, YS + 1))
                    nc.scalar.activation(br_sig[:, :, 0:NLAT], lat(0), ACT.Sigmoid).then_inc(br_done, 1)
                    nc.scalar.activation(br_sig[:, :, NLAT:NTOK], cx(0), ACT.Sigmoid).then_inc(taken[0], 1)
                    for s in range(2):
                        split_hi(s, l, d * 2 + (YS + 2 + 1 - s))
                for k in range(KT):
                    ac.wait_ge(ty_step, (l * KT + k + 1) * 2 + 1)
                    nc.scalar.activation(h_hi[:, k, :], y[:, k, :], ACT.Copy).then_inc(h_hi_ready, 1)
                with ac.Fori(0, O_PAIRS) as i:
                    for s in range(2):
                        split_hi(s, l, i + (OS + 1 + 1 - s))
                norm(l, 2)
                ffn(l, F2, 1, 1, True)


        @block.tensor
        def _(pe):
            def strip(s, l, n, out_lat, out_ctx, xh, xl, tiles, ready=None):
                pe.wait_ge(lo_ready[s], l * SPLITS[s] + n + 1)
                for k, t in enumerate(tiles):
                    if ready is not None:
                        pe.wait_ge(h_lo_ready, ready + (k + 1))
                    w = slice(k * P, (k + 1) * P)
                    for j, (a, b) in enumerate(((w_hi, xh), (w_hi, xl), (w_lo, xh))):
                        first, last = k == 0 and j == 0, k == len(tiles) - 1 and j == 2
                        nc.tensor.matmul(out_lat, a[:, s, w], b[:, t, 0:NLAT], start=first, stop=last)
                        mm = nc.tensor.matmul(out_ctx, a[:, s, w], b[:, t, NLAT:NTOK], start=first, stop=last)
                mm.then_inc(strip_done[s], 1)

            def pair(l, at, pos, xh, xl, tiles, ready=None, extra=0, q=0, tiles1=None):
                b = at % 2
                pe.wait_ge(taken[b], q + fills(l, at))
                for s in range(2):
                    strip(s, l, q * 2 + (at + (extra if s == 0 else 0)), bank[b][:, s, :],
                          bank[b][:, 2, s * P:(s + 1) * P], xh, xl, tiles1 if s and tiles1 else tiles,
                          ready if s == 0 else None)

            def pairs(l, at, count, xh, xl, tiles, ready=None, extra=0):
                settle(pe)
                with pe.Fori(0, count // 2) as q:
                    for b in range(2):
                        pair(l, at + b, b, xh, xl, tiles, ready, extra, q)

            def norm(l, i):
                n = (l * 3 + i) * KT
                for k in range(KT):
                    pe.wait_ge(sq_ready, n + k + 1)
                    nc.tensor.matmul(m1[:], mean_ones, sq[:, k % 2, 0:NLAT], start=k == 0, stop=k == KT - 1)
                    nc.tensor.matmul(m2[:, 0:NCTX], mean_ones, sq[:, k % 2, NLAT:NTOK],
                                     start=k == 0, stop=k == KT - 1).then_inc(sq_used, 1)

            def ffn(l, base, extra, j):
                for f, n in enumerate(FF_PARTS):
                    at = base + sum(FF_PARTS[:f]) + 4 * f
                    pairs(l, at, n, h_hi, h_lo, range(KT), l * H_TILES + (0, 3 * KT)[j], extra)
                    pe.wait_ge(g_lo_ready, (l * 2 + j) * (D_FF // P) + sum(FF_PARTS[:f + 1]) + 2)
                    pairs(l, at + n, KT // 2, g_hi, g_lo, range(n), None, extra)

            pe.wait_ge(const_in, 32)
            pe.wait_ge(cond_ready, 1)
            with pe.Fori(0, DEPTH) as l:
                with pe.Fori(0, ADA_PAIRS) as i:
                    for s in range(2):
                        pe.wait_ge(landed[s], (l * USES[s] + i) * 16 + 16)
                        for k in range(KT):
                            mm = nc.tensor.matmul(m1[:, bass.ds(i * 4 + 2 * s, 2)], w_raw[:, s, k * P:(k + 1) * P],
                                                  cond[:, k, :], start=k == 0, stop=k == KT - 1)
                        mm.then_inc(raw_free[s], 1)
                pe.wait_ge(mods, l * 7 + 1)
                norm(l, 0)
                ffn(l, F1, 0, 0)
                norm(l, 1)
                pe.wait_ge(h_lo_ready, l * H_TILES + KT + 1)
                strip(0, l, INA, m1[:], m2[:, 0:NCTX], h_hi, h_lo, range(KT), l * H_TILES + KT)
                pairs(l, INA, INA_PAIRS, h_hi, h_lo, range(KT), None, 1)
                pe.wait_ge(gate_taken, l * 2 + 2)
                for t in range(8):
                    n = l * 8 + t
                    pe.wait_ge(qsq_ready, n + 1)
                    if t >= 1:
                        pe.wait_ge(qln_done, n * 2)
                    nc.tensor.matmul(m1[:], head_ones, qsq[:, t % 2, 0:NLAT], start=True, stop=True)
                    nc.tensor.matmul(m2[:, 0:NCTX], head_ones, qsq[:, t % 2, NLAT:NTOK], start=True, stop=True)\
                        .then_inc(qss_done, 1)
                pe.wait_ge(taken[0], fills(l, INB - 2) + 1)
                pe.wait_ge(taken[1], fills(l, INB - 1) + 1)
                for i in range(8):
                    if i >= 2:
                        pe.wait_ge(vt_taken, l * 8 + i - 1)
                    t0 = 64 * i if i < 7 else NLAT
                    for f in range(4):
                        mm = nc.tensor.transpose((pa if i % 2 == 0 else pb)[:, 2, f * P:(f + 1) * P],
                                                 qkv[:, 8 + f, t0:t0 + P], ident)
                    mm.then_inc(vt_done, 1)
                pe.wait_ge(qk_normed, l * 8 + 8)
                pe.wait_ge(par_in, l * 48 + 48)

                def scores(u):
                    h, qb = u // CH, u % CH
                    n, hp = l * NUNIT + u, slice(64 * (h % 2), 64 * (h % 2) + 64)
                    if u >= 2:
                        pe.wait_ge(s_taken, n - 1)
                    out = pa[:, u % 2, :]
                    q = qkv[hp, h // 2, qb * P:(qb + 1) * P]
                    if qb < LCH:
                        nc.tensor.matmul(out[:, 0:WIN], q, qkv[hp, 4 + h // 2, QB_KEY[qb]:QB_KEY[qb] + WIN],
                                         start=True, stop=True)
                    k = cache_k[hp, h // 2, :] if qb < LCH else qkv[hp, 4 + h // 2, NLAT:NTOK]
                    nc.tensor.matmul(out[:, WIN:384], q, k, start=True, stop=True).then_inc(s_done, 1)

                def parts(u):
                    return range(3) if u % CH < LCH else range(2, 3)

                def turn(u):
                    n = l * NUNIT + u
                    pe.wait_ge(p_ready, n + 1)
                    if u == 0:
                        pe.wait_ge(vt_taken, l * 8 + 8)
                    if u >= 2:
                        pe.wait_ge(pt_taken, n - 1)
                    out = (pa[:, 2, :], pb[:, 0, :])[u % 2]
                    for j in parts(u):
                        mm = nc.tensor.transpose(out[:, j * P:(j + 1) * P], p_att[:, u % 2, j * P:(j + 1) * P], ident)
                    mm.then_inc(pt_done, 1)

                def weighted(u):
                    h, qb, n = u // CH, u % CH, l * NUNIT + u
                    pe.wait_ge(pt_taken, n + 1)
                    if u >= 2:
                        pe.wait_ge(att_ready, n - 1)
                    hd = slice(h * HD_A, (h + 1) * HD_A)
                    w = QB_KEY[qb] // 64 if qb < LCH else 0
                    values = (v_tok[:, w, hd], v_tok[:, w + 2, hd], cache_v[:, hd] if qb < LCH else v_tok[:, 7, hd])
                    js = list(parts(u))
                    for j in js:
                        mm = nc.tensor.matmul(pb[:, 1 + u % 2, 0:HD_A], p_t[:, u % 2, j * P:(j + 1) * P], values[j],
                                              start=j == js[0], stop=j == js[-1])
                    mm.then_inc(pv_done, 1)

                for u in range(NUNIT + 2):
                    if u < NUNIT:
                        scores(u)
                    if 1 <= u <= NUNIT:
                        turn(u - 1)
                    if u >= 2:
                        weighted(u - 2)
                pe.wait_ge(att_ready, l * NUNIT + NUNIT)
                for c in range(CH):
                    if c >= 2:
                        pe.wait_ge(at_lo, l * CH + c - 1)
                    for f in range(4):
                        mm = nc.tensor.transpose(pa[:, c % 2, f * P:(f + 1) * P], att[:, c, f * P:(f + 1) * P], ident)
                    mm.then_inc(at_done, 1)
                pe.wait_ge(at_lo, l * CH + CH)
                pairs(l, INB, INB_PAIRS, h_hi, h_lo, range(KT), None, 1)
                pe.wait_ge(taken[0], fills(l, OB - 2) + 1)
                pe.wait_ge(taken[1], fills(l, OB - 1) + 1)
                for t in range(8):
                    if t >= 2:
                        pe.wait_ge(rope_step, l * 24 + 3 * (t - 2) + 1)
                    nc.tensor.matmul(pa[:, t % 2, :], rot, qkv[:, t, 0:NLAT], start=True, stop=True)\
                        .then_inc(rot_done, 1)
                pe.wait_ge(rope_step, l * 24 + 24)
                for c in range(CH):
                    if c >= 2:
                        pe.wait_ge(kt_taken, l * CH + c - 1)
                    for h in range(H_B):
                        mm = nc.tensor.transpose((pa[:, 2, :], pb[:, 0, :])[c % 2][:, h * P:(h + 1) * P],
                                                 qkv[:, 4 + h, c * P:(c + 1) * P], ident)
                    mm.then_inc(kt_done, 1)
                for c in range(CH):
                    if c >= 2:
                        pe.wait_ge(va_taken, l * CH + c - 1)
                    for h in range(H_B):
                        mm = nc.tensor.transpose((pb[:, 1, :], pb[:, 2, :])[c % 2][:, h * P:(h + 1) * P],
                                                 qkv[:, 8 + h, c * P:(c + 1) * P], ident)
                    mm.then_inc(va_done, 1)
                pe.wait_ge(row_step, l * ROW_STEPS + ROW_STEPS)
                settle(pe)
                rows = slice(0, ROWP)
                for out, pairs_ in ((m1, (row_g, row_a)), (m2, (row_w, row_m))):
                    for j, r in enumerate(pairs_):
                        for c in range(CH):
                            at = (j * CH + c) * ROWP
                            mm = nc.tensor.transpose(out[:, at:at + ROWP], r[rows, c * P:(c + 1) * P],
                                                     ident[rows, 0:ROWP])
                    if out is m1:
                        for n in range(2 * H_B):
                            e = P - 1 if n % 2 == 0 else 0
                            pick = ident[rows, row_of(n):row_of(n) + 1].broadcast_to([ROWP, P])
                            ends = row_a[rows, :].rearrange("p (c t) -> p c t", t=P)[:, :, e]
                            mm = nc.tensor.matmul(m1[:, 360 + n * CH:360 + (n + 1) * CH], pick, ends, start=True, stop=True)
                    mm.then_inc(cols_done, 1)
                pe.wait_ge(kt_taken, l * CH + CH)
                pe.wait_ge(va_taken, l * CH + CH)
                pe.wait_ge(ones_set, l + 1)
                pe.wait_ge(cols_ready, l * 5 + 5)
                for n in range(2 * H_B):
                    h, g = n // 2, l * 8 + n
                    order = range(LCH) if n % 2 == 0 else range(LCH - 1, -1, -1)
                    rest = 1 if n % 2 == 0 else 0
                    if n >= 1:
                        pe.wait_ge(num_step, steps_before(l, n - 1) + 5)
                        pe.wait_ge(cout_ready, g)
                    if n % 2 == 0:
                        for c in range(CH):
                            cc = slice(c * P, (c + 1) * P)
                            out = pa[:, 0, cc] if c < LCH else pa[:, 1, 0:P]
                            mm = nc.tensor.matmul(out, qkv[:, 4 + h, cc], qkv[:, h, cc], start=True, stop=True)
                        mm.then_inc(kq_done, 1)
                    pick = ident[rows, row_of(n):row_of(n) + 1].broadcast_to([ROWP, P])
                    nc.tensor.matmul(pa[:, 2, :], pick, row_m_rel[rows, 0:NLAT], start=True, stop=True)
                    nc.tensor.matmul(pb[:, 0, 0:P], pick, row_m_rel[rows, NLAT:NTOK], start=True, stop=True)\
                        .then_inc(mb_done, 1)
                    pe.wait_ge(kw_ready, g + 1)
                    for j, c in enumerate(order[0:3]):
                        nc.tensor.matmul(m1[:, j * VW:(j + 1) * VW], kw[:, c, :], v_aug[:, c, h, :], start=True, stop=True)
                    nc.tensor.matmul(pb[:, 2, 2 * VW:3 * VW], kw[:, LCH, :], v_aug[:, LCH, h, :], start=True, stop=True)\
                        .then_inc(upd_done, 1)
                    pe.wait_ge(c_in[n % 2], (l * 4 + n // 2) * 16 + 16)
                    pe.wait_ge(mb_taken, g * 2 + 2)
                    c0 = order[0]
                    nc.tensor.matmul(pb[:, 0, P:P + VW], qkv[:, h, c0 * P:(c0 + 1) * P], c_seq[n % 2][:, 0, :],
                                     start=True, stop=True)
                    pe.wait_ge(st_ready, g * 2 + 2)
                    for c in range(CH):
                        out = pb[:, 1, c * VW:(c + 1) * VW] if c < 3 else pb[:, 2, (c - 3) * VW:(c - 2) * VW]
                        mm = nc.tensor.matmul(out, st[:, c * P:(c + 1) * P], v_aug[:, c, h, :], start=True, stop=True)
                    mm.then_inc(intra_done, 1)
                    for j in range(1, LCH):
                        c = order[j]
                        pe.wait_ge(c_step, g * 3 + j)
                        mm = nc.tensor.matmul(m2[:, (c - rest) * VW:(c - rest + 1) * VW], qkv[:, h, c * P:(c + 1) * P],
                                              c_seq[n % 2][:, j, :], start=True, stop=True)
                    mm.then_inc(inter_done, 1)
                pe.wait_ge(num_step, l * NUM_STEPS + NUM_STEPS)
                pe.wait_ge(cout_ready, l * 8 + 8)
                for p in range(OB_PAIRS):
                    pair(l, OB + p, p, h_hi, h_lo, range(KT), None, 1)
                pe.wait_ge(hb_step, l * 3 + 3)
                for c in range(CH):
                    if c >= 2:
                        pe.wait_ge(ht_prod, l * CH + c - 1)
                    for f in range(H_B):
                        mm = nc.tensor.transpose((m1, m2)[c % 2][:, f * P:(f + 1) * P], hb[:, c, f * P:(f + 1) * P], ident)
                    mm.then_inc(ht_done, 1)
                with pe.Fori(0, KT) as d:
                    pair(l, YS, 0, h_hi, h_lo, range(KT), None, 1, d)
                    pe.wait_ge(ht_lo, l * CH + CH)
                    pair(l, YS + 1, 1, g_hi, g_lo, range(4), None, 1, d, tiles1=range(4, 8))
                pairs(l, OS, O_PAIRS, h_hi, h_lo, range(KT), l * H_TILES + 2 * KT, 1)
                norm(l, 2)
                ffn(l, F2, 1, 1)

        @block.vector
        def _(dv):
            dv.sem_inc(g_lo_ready, 2)
            dv.sem_inc(ty_step, 1)
            dv.wait_ge(const_in, 32)

            def norm(l, i):
                n, m = (l * 3 + i) * KT, l * H_TILES + (0, KT, 3 * KT)[i]
                dv.wait_ge(rstd_ready, l * 3 + i + 1)

                def low(k):
                    dv.wait_ge(h_hi_ready, m + k + 1)
                    nc.vector.tensor_tensor(h_lo[:, k, :], hx[:, k % 2, :], h_hi[:, k, :].bitcast(F32), ALU.subtract)\
                        .then_inc(h_lo_ready, 1)

                for k in range(KT):
                    if k >= 2:
                        dv.wait_ge(h_lo_ready, m + k - 1)
                    nc.vector.tensor_tensor(hx[:, k % 2, :], x[:, k, :], rstd, ALU.mult).then_inc(h_scaled, 1)
                    dv.wait_ge(h_scaled, n + k + 1)
                    for g, cols in ((0, slice(0, NLAT)), (1, slice(NLAT, NTOK))):
                        nc.vector.tensor_scalar(hx[:, k % 2, cols], hx[:, k % 2, cols], mod_a[:, i, k, g:g + 1],
                                                mod[:, 3 * i * KT + k, g:g + 1], ALU.mult, ALU.add).then_inc(h_mod, 1)
                    if k >= 1:
                        low(k - 1)
                low(KT - 1)

            def add_to_x(l, at, done, which, q=0):
                b = at % 2
                dv.wait_ge(strip_done[1], q * 2 + filled(l, at))
                dv.wait_ge(x_upd, done)
                for s in range(2):
                    t = done_tile(q, b, s)
                    for g, cols, ps in ((0, slice(0, NLAT), bank[b][:, s:s + 1, :]),
                                        (1, slice(NLAT, NTOK), bank[b][:, 2:3, s * P:(s + 1) * P])):
                        ins = nc.vector.scalar_tensor_tensor(x[:, t, cols], ps, gate_at(which, t, g), x[:, t, cols],
                                                             ALU.mult, ALU.add)
                    ins.then_inc(x_upd, 1)
                dv.wait_ge(x_upd, done + 2)
                dv.sem_inc(taken[b], 1)

            def done_tile(q, b, s):
                return bass.ds(q * 4 + (2 * b + s), 1)

            def gate_at(which, t, g):
                return gate[:, which, t, g]

            def add_pairs(l, at, done, which):
                with dv.Fori(0, KT // 4) as q:
                    for b in range(2):
                        add_to_x(l, at + b, q * 4 + (done + 2 * b), which, q)

            def ffn(l, base, j):
                for f, n in enumerate(FF_PARTS):
                    first = sum(FF_PARTS[:f])
                    at = base + first + 4 * f
                    with dv.Fori(0, n // 2) as q:
                        for b in range(2):
                            done = q * 2 + (l * 2 + j) * (D_FF // P) + (first + b)
                            dv.wait_ge(silu_done, done + 1)
                            dv.wait_ge(g_lo_ready, done + 1)
                            nc.vector.tensor_tensor(gt[:, b, 0:NLAT], sg[:, b, 0:NLAT], bank[b][:, 1, :], ALU.mult)
                            nc.vector.tensor_tensor(gt[:, b, NLAT:NTOK], sg[:, b, NLAT:NTOK], bank[b][:, 2, P:2 * P],
                                                    ALU.mult).then_inc(taken[b], 1)
                            dv.wait_ge(g_hi_ready, done + 1)
                            nc.vector.tensor_tensor(g_lo[:, bass.ds(q * 2 + b, 1), :], gt[:, b:b + 1, :],
                                                    g_hi[:, bass.ds(q * 2 + b, 1), :].bitcast(F32), ALU.subtract)\
                                .then_inc(g_lo_ready, 1)
                    add_pairs(l, at + n, X_IN + l * X_UPD + (0, 4 * KT)[j] + f * KT, 2 * j)

            with dv.Fori(0, DEPTH) as l:
                for s in range(2):
                    dv.wait_ge(raw_free[s], l * USES[s] + ADA_PAIRS + 1)
                dv.wait_ge(par_in, l * 48 + 48)
                dv.wait_ge(x_upd, X_IN + l * X_UPD)
                nc.vector.tensor_tensor(mod[:], m1[:, 0:2 * N_MOD * KT].rearrange("p (j g) -> p j g", g=2),
                                        par[:, P_BADA:P_BADA + N_MOD * KT, None].broadcast_to([P, N_MOD * KT, 2]),
                                        ALU.add).then_inc(mods, 1)
                dv.wait_ge(mods, l * 7 + 1)
                for i in range(3):
                    nc.vector.scalar_tensor_tensor(
                        mod_a[:, i], mod[:, (3 * i + 1) * KT:(3 * i + 2) * KT, :], 1.0,
                        par[:, P_GN + i * KT:P_GN + (i + 1) * KT, None].broadcast_to([P, KT, 2]),
                        ALU.add, ALU.mult).then_inc(mods, 1)
                    nc.vector.tensor_scalar(gate[:, i], mod[:, (3 * i + 2) * KT:(3 * i + 3) * KT, :],
                                            1.0 if i == 1 else 0.5, None, ALU.mult).then_inc(mods, 1)
                dv.wait_ge(mods, l * 7 + 7)
                norm(l, 0)
                ffn(l, F1, 0)
                norm(l, 1)
                gr = slice(0, FROW + ROWP)
                dv.wait_ge(strip_done[0], l * SPLITS[0] + INA + 2)
                nc.vector.tensor_scalar(row_gate[gr, 0:NLAT], m1[gr, :], par[gr, P_BG:P_BG + 1], None, ALU.add)\
                    .then_inc(gate_taken, 1)
                nc.vector.tensor_scalar(row_gate[gr, NLAT:NTOK], m2[gr, 0:NCTX], par[gr, P_BG:P_BG + 1], None, ALU.add)\
                    .then_inc(gate_taken, 1)
                nc.vector.tensor_scalar(small[:, 73:74], par[:, P_GQK:P_GQK + 1], HD_A ** -0.5, None, ALU.mult)\
                    .then_inc(gq, 1)
                with dv.Fori(0, INA_PAIRS // 2) as q:
                    for b in range(2):
                        dv.wait_ge(strip_done[1], q * 2 + filled(l, INA + b))
                        for s in range(2):
                            nc.vector.tensor_copy(by_column(qkv[:, bass.ds(q * 4 + (2 * b + s), 1), 0:NLAT]
                                                            .rearrange("p a n -> p (a n)")),
                                                  by_row(bank[b][:, s, :]))
                        nc.vector.tensor_copy(qkv[:, bass.ds(q * 4 + 2 * b, 2), NLAT:NTOK], cx(b)).then_inc(taken[b], 1)
                dv.wait_ge(gq, l + 1)
                for t in range(8):
                    dv.wait_ge(qrs_ready, l * 8 + t + 1)
                    g = small[:, 73:74] if t < 4 else par[:, P_GQK + 1:P_GQK + 2]
                    nc.vector.scalar_tensor_tensor(qkv[:, t, :], qkv[:, t, :], g, qrs[:, 0:NTOK], ALU.mult, ALU.mult)\
                        .then_inc(qk_normed, 1)
                for u in range(NUNIT + 2):
                    n = l * NUNIT + u
                    if u < NUNIT:
                        h, qb = u // CH, u % CH
                        if qb == 0:
                            dv.wait_ge(bias_in[h % 2], (l * 4 + h // 2) * 16 + 16)
                        dv.wait_ge(s_done, n + 1)
                        if u >= 2:
                            dv.wait_ge(p_ready, n - 1)
                        lo, kind = (0, QB_KIND[qb]) if qb < LCH else (WIN, 0)
                        settle(dv)
                        nc.vector.tensor_tensor_reduce(s_neg[:, u % 2, lo:384], pa[:, u % 2, lo:384],
                                                       bias[:, 3 * (h % 2) + kind, lo:384], -1.0, 3.0e38,
                                                       ALU.add, ALU.min, stat[:, 0, u:u + 1]).then_inc(s_taken, 1)
                    if 1 <= u <= NUNIT:
                        dv.wait_ge(p_ready, n)
                        nc.vector.reciprocal(stat[:, 2, u - 1:u], stat[:, 1, u - 1:u]).then_inc(rinv_ready, 1)
                    if u >= 2:
                        v = u - 2
                        if v == 0:
                            dv.wait_ge(kv_out, l * 32 + 32)
                        dv.wait_ge(pv_done, n - 1)
                        dv.wait_ge(rinv_ready, n - 1)
                        nc.vector.tensor_scalar(att[:, v % CH, (v // CH) * HD_A:(v // CH + 1) * HD_A],
                                                pb[:, 1 + v % 2, 0:HD_A], stat[:, 2, v:v + 1], None, ALU.mult)\
                            .then_inc(att_ready, 1)
                for c in range(CH):
                    dv.wait_ge(at_hi, l * CH + c + 1)
                    src, dst = at_views(g_lo, c)
                    nc.vector.tensor_tensor(dst, src, at_views(g_hi, c)[1].bitcast(F32), ALU.subtract).then_inc(at_lo, 1)
                with dv.Fori(0, INB_PAIRS // 2) as q:
                    for b in range(2):
                        dv.wait_ge(strip_done[1], q * 2 + filled(l, INB + b))
                        nc.vector.tensor_copy(qkv[:, bass.ds(q * 4 + 2 * b, 2), 0:NLAT], lat(b))
                        nc.vector.tensor_copy(qkv[:, bass.ds(q * 4 + 2 * b, 2), NLAT:NTOK], cx(b)).then_inc(taken[b], 1)
                dv.wait_ge(rope_in, l * 16 + 16)
                for t in range(8):
                    r, sc = l * 24 + 3 * t, 1.0 if t < 4 else HD_B ** -0.5
                    dv.wait_ge(rot_done, l * 8 + t + 1)
                    if t >= 2:
                        dv.wait_ge(rope_step, r - 3)
                    nc.vector.scalar_tensor_tensor(rtmp[:, t % 2, :], pa[:, t % 2, :], sc, sin, ALU.mult, ALU.mult)\
                        .then_inc(rope_step, 1)
                    if t == 0:
                        dv.wait_ge(taken[0], fills(l, OB - 2) + 1)
                        dv.wait_ge(taken[1], fills(l, OB - 1) + 1)
                    nc.vector.scalar_tensor_tensor(qkv[:, t, :], qkv[:, t, :], sc, cos, ALU.mult, ALU.mult)\
                        .then_inc(rope_step, 1)
                    dv.wait_ge(rope_step, r + 2)
                    nc.vector.tensor_tensor(qkv[:, t, 0:NLAT], qkv[:, t, 0:NLAT], rtmp[:, t % 2, :], ALU.add)\
                        .then_inc(rope_step, 1)
                dv.wait_ge(rope_step, l * 24 + 24)
                at = [l * ROW_STEPS]

                def step(ins):
                    ins.then_inc(row_step, 1)
                    at[0] = at[0] + 1
                    dv.wait_ge(row_step, at[0])

                fr, r0, rb = slice(FROW, FROW + ROWP), slice(0, ROWP), slice(32, ROWP)
                v = nc.vector
                step(v.scalar_tensor_tensor(row_exp[fr, :], row_gate[fr, :], -1.0, row_gate[fr, :], ALU.mult, ALU.max))
                v.memset(v_aug[:, :, :, HD_B:VW], 1.0).then_inc(ones_set, 1)
                for c in range(CH):
                    dv.wait_ge(kt_done, l * CH + c + 1)
                    v.tensor_copy(k_tok[:, c, :], (pa[:, 2, :], pb[:, 0, :])[c % 2]).then_inc(kt_taken, 1)
                dv.wait_ge(row_act, l * 2 + 2)
                step(v.scalar_tensor_tensor(row_lf[r0, :], row_gate[fr, :], 0.0, row_exp[fr, :], ALU.min, ALU.subtract))
                step(v.tensor_tensor_scan(row_b[r0, :], reset[r0, :], row_lf[r0, :], 0.0, ALU.mult, ALU.add))
                step(v.tensor_tensor_scan(row_b[rb, NTOK - 1::-1], reset[rb, NTOK - 1::-1], row_lf[rb, NTOK - 1::-1],
                                          0.0, ALU.mult, ALU.add))
                m0 = par[:, P_M0:P_M0 + 1]
                step(v.tensor_tensor_scan(row_m[r0, 0:NLAT], row_lf[r0, 0:NLAT], row_gate[r0, 0:NLAT], m0[r0], ALU.add, ALU.max))
                step(v.tensor_tensor_scan(row_m[r0, NLAT:NTOK], row_lf[r0, NLAT:NTOK], row_gate[r0, NLAT:NTOK], 0.0,
                                          ALU.add, ALU.max))
                step(v.tensor_tensor_scan(row_m[rb, NLAT - 1::-1], row_lf[rb, NLAT - 1::-1], row_gate[rb, NLAT - 1::-1],
                                          m0[rb], ALU.add, ALU.max))
                step(v.tensor_tensor_scan(row_m[rb, NTOK - 1:NLAT - 1:-1], row_lf[rb, NTOK - 1:NLAT - 1:-1],
                                          row_gate[rb, NTOK - 1:NLAT - 1:-1], 0.0, ALU.add, ALU.max))
                step(v.tensor_tensor(row_m_rel[r0, :], row_m[r0, :], row_b[r0, :], ALU.subtract))
                step(v.tensor_tensor(row_g[r0, :], row_gate[r0, :], row_b[r0, :], ALU.subtract))
                step(v.tensor_copy(mprev[r0, 0:1], m0[r0]))
                step(v.tensor_copy(mprev[r0, 1:LCH], row_m[r0, P - 1:(LCH - 1) * P:P]))
                step(v.memset(mprev[r0, LCH:CH], 0.0))
                step(v.tensor_copy(mprev[rb, 0:LCH - 1], row_m[rb, P:(LCH - 1) * P + 1:P]))
                step(v.tensor_copy(mprev[rb, LCH - 1:LCH], m0[rb]))

                def chunks(ap):
                    return ap.rearrange("p (c t) -> p c t", t=P)

                step(v.tensor_tensor(chunks(row_a[r0, :]), mprev[r0, 0:CH, None].broadcast_to([ROWP, CH, P]),
                                     chunks(row_m_rel[r0, :]), ALU.subtract))
                step(v.tensor_tensor(chunks(row_w[r0, :]), chunks(row_g[r0, :]),
                                     chunks(row_m_rel[r0, :])[:, :, P - 1:P].broadcast_to([ROWP, CH, P]), ALU.subtract))
                step(v.tensor_tensor(chunks(row_w[rb, :]), chunks(row_g[rb, :]),
                                     chunks(row_m_rel[rb, :])[:, :, 0:1].broadcast_to([ROWP - 32, CH, P]), ALU.subtract))
                dv.wait_ge(kt_taken, l * CH + CH)
                dv.wait_ge(cols_ready, l * 5 + 5)
                for n in range(2 * H_B):
                    h, back, g, r = n // 2, n % 2, l * 8 + n, row_of(n)
                    order = range(LCH) if back == 0 else range(LCH - 1, -1, -1)
                    rest = 1 - back
                    mk = mask[:, back:back + 1, :]
                    dv.wait_ge(mb_done, g + 1)
                    if n >= 1:
                        dv.wait_ge(st_ready, g * 2)
                    v.tensor_tensor(chunks(wt[:, 0:NLAT]), chunks(pa[:, 2, :]), mk.broadcast_to([P, LCH, P]), ALU.add)\
                        .then_inc(mb_taken, 1)
                    v.tensor_tensor(wt[:, NLAT:NTOK], pb[:, 0, 0:P], mask[:, back, :], ALU.add).then_inc(mb_taken, 1)
                    if n >= 1:
                        dv.wait_ge(upd_done, g)
                    v.tensor_tensor(kw, k_tok[:, :, h * P:(h + 1) * P],
                                    gcols[:, 2, :, r:r + 1].broadcast_to([P, CH, P]), ALU.mult).then_inc(kw_ready, 1)
                    dv.wait_ge(upd_done, g + 1)
                    dv.wait_ge(c_in[n % 2], (l * 4 + n // 2) * 16 + 16)
                    for j in range(3):
                        if j >= 1:
                            dv.wait_ge(c_step, g * 3 + j)
                        v.scalar_tensor_tensor(c_seq[n % 2][:, j + 1, :], c_seq[n % 2][:, j, :], dec[:, n, order[j]:order[j] + 1],
                                               m1[:, j * VW:(j + 1) * VW], ALU.mult, ALU.add).then_inc(c_step, 1)
                    dv.wait_ge(wt_ready, (g + 1) * CH)
                    dv.wait_ge(kq_done, l * 4 + h + 1)
                    if n >= 1:
                        dv.wait_ge(intra_done, g)
                    v.tensor_tensor(st[:, 0:NLAT], wt[:, 0:NLAT], pa[:, 0, :], ALU.mult).then_inc(st_ready, 1)
                    v.tensor_tensor(st[:, NLAT:NTOK], wt[:, NLAT:NTOK], pa[:, 1, 0:P], ALU.mult).then_inc(st_ready, 1)
                    s0 = steps_before(l, n)
                    dv.wait_ge(intra_done, g + 1)
                    dv.wait_ge(inter_done, g + 1)
                    if n >= 1:
                        dv.wait_ge(num_step, s0)
                    c0 = order[0]
                    v.tensor_tensor(num[:, rest:rest + 3, :], m2[:, 0:3 * VW].rearrange("p (c d) -> p c d", d=VW),
                                    gcols[:, 1, rest:rest + 3, r:r + 1].broadcast_to([P, 3, VW]), ALU.mult).then_inc(num_step, 1)
                    v.tensor_scalar(num[:, c0, :], pb[:, 0, P:P + VW], gcols[:, 1, c0, r:r + 1], None, ALU.mult)\
                        .then_inc(num_step, 1)
                    dv.wait_ge(num_step, s0 + 2)
                    v.tensor_tensor(num[:, 0:3, :], num[:, 0:3, :], pb[:, 1, 0:3 * VW].rearrange("p (c d) -> p c d", d=VW),
                                    ALU.add).then_inc(num_step, 1)
                    v.tensor_tensor(num[:, 3, :], num[:, 3, :], pb[:, 2, 0:VW], ALU.add).then_inc(num_step, 1)
                    v.tensor_copy(num[:, LCH, :], pb[:, 2, VW:2 * VW]).then_inc(num_step, 1)
                    if n >= 2:
                        dv.wait_ge(cout_out, (g - 1) * 16)
                    else:
                        dv.wait_ge(ones_set, l + 1)
                    v.tensor_copy(c_out[:, n % 2, :], pb[:, 2, 2 * VW:3 * VW]).then_inc(cout_ready, 1)
                    dv.wait_ge(num_step, s0 + 5)
                    v.scalar_tensor_tensor(den, num[:, :, HD_B], -1.0, gcols[:, 3, :, r], ALU.mult, ALU.max)\
                        .then_inc(num_step, 1)
                    dv.wait_ge(num_step, s0 + 6)
                    v.tensor_tensor(den, den, num[:, :, HD_B], ALU.max).then_inc(num_step, 1)
                    dv.wait_ge(num_step, s0 + 7)
                    v.reciprocal(den, den).then_inc(num_step, 1)
                    dv.wait_ge(num_step, s0 + 8)
                    out = hb[:, :, h * P:(h + 1) * P] if back == 0 else hnum[:, :, 0:HD_B]
                    if n == 0:
                        dv.wait_ge(m_out, l * 32 + 32)
                    v.tensor_tensor(out, num[:, :, 0:HD_B], den[:, :, None].broadcast_to([P, CH, HD_B]), ALU.mult)\
                        .then_inc(num_step, 1)
                    if back:
                        dv.wait_ge(num_step, s0 + 9)
                        hh = hb[:, :, h * P:(h + 1) * P]
                        v.tensor_tensor(hh, hh, out, ALU.add).then_inc(num_step, 1)
                dv.wait_ge(num_step, l * NUM_STEPS + NUM_STEPS)
                v.tensor_tensor(hsq, hb, hb, ALU.mult).then_inc(hb_step, 1)
                dv.wait_ge(hb_step, l * 3 + 1)
                v.tensor_reduce(hss, pool[:, 10260:12820].rearrange("p (a b) -> p a b", b=P), AX_X, ALU.add)\
                    .then_inc(hb_step, 1)
                dv.wait_ge(hb_act, l * 2 + 2)
                hb20 = pool[:, 12820:15380].rearrange("p (a b) -> p a b", b=P)
                v.tensor_tensor(hb20, hb20, hss[:, :, None].broadcast_to([P, CH * H_B, P]), ALU.mult).then_inc(hb_step, 1)
                dv.wait_ge(hb_step, l * 3 + 3)

                def h_low(c):
                    dv.wait_ge(ht_hi, l * CH + c + 1)
                    v.tensor_tensor(g_lo[:, 4:8, c * P:(c + 1) * P], hbt[:, c % 2, :].rearrange("p (f t) -> p f t", f=4),
                                    g_hi[:, 4:8, c * P:(c + 1) * P].bitcast(F32), ALU.subtract).then_inc(ht_lo, 1)

                dv.wait_ge(ob_done, l * 6 + 6)
                for c in range(CH):
                    dv.wait_ge(ht_done, l * CH + c + 1)
                    if c >= 2:
                        dv.wait_ge(ht_lo, l * CH + c - 1)
                    v.tensor_tensor(hbt[:, c % 2, :].rearrange("p (f t) -> p f t", f=4),
                                    (m1, m2)[c % 2][:, 0:512].rearrange("p (f t) -> p f t", f=4),
                                    ob_sig[:, :, c * P:(c + 1) * P], ALU.mult).then_inc(ht_prod, 1)
                    if c >= 1:
                        h_low(c - 1)
                h_low(CH - 1)
                dv.wait_ge(cout_out, (l + 1) * 2 * H_B * 16)
                settle(dv)
                with dv.Fori(0, KT) as d:
                    dv.wait_ge(strip_done[1], d * 2 + filled(l, YS + 1))
                    dv.wait_ge(taken[0], d + fills(l, YS) + 1)
                    dv.wait_ge(ty_step, (l * KT + d) * 2 + 1)
                    v.tensor_tensor(ty[:, :, 0:NLAT], lat(1), br_sig[:, :, 0:NLAT], ALU.mult).then_inc(ty_step, 1)
                    v.tensor_tensor(ty[:, :, NLAT:NTOK], cx(1), br_sig[:, :, NLAT:NTOK], ALU.mult).then_inc(taken[1], 1)
                    dv.wait_ge(taken[1], d + (fills(l, YS + 1) + 1))
                    v.tensor_tensor(y[:, bass.ds(d, 1), :], ty[:, 0:1, :], ty[:, 1:2, :], ALU.add).then_inc(ty_step, 1)
                for k in range(KT):
                    dv.wait_ge(h_hi_ready, l * H_TILES + 2 * KT + k + 1)
                    v.tensor_tensor(h_lo[:, k, :], y[:, k, :], h_hi[:, k, :].bitcast(F32), ALU.subtract).then_inc(h_lo_ready, 1)
                add_pairs(l, OS, X_IN + l * X_UPD + 3 * KT, 1)
                norm(l, 2)
                ffn(l, F2, 1)


def kernel(x_prompt, x_sample, cache_k, cache_v, state_C, state_n, state_m, c, c_ctx,
           w_ada, b_ada, g_norm, w_up1, w_dn1, w_in, b_gates, g_qn, g_kn, rpb, g_hn,
           w_pa, w_pb, w_o, w_up2, w_dn2):
    import numpy as np
    import concourse.bacc as bacc
    from concourse.bass_utils import run_bass_kernel_spmd

    A = np.asarray
    f32 = np.float32

    def strips(w):
        w = A(w)
        l, k, n = w.shape
        return w.reshape(l, k // P, P, n // P, P).transpose(0, 3, 2, 1, 4).reshape(l, n // P, P, k)

    def columns(v, tiles):
        v = A(v)
        return v.reshape(v.shape[0], -1, tiles, P).transpose(0, 3, 1, 2).reshape(v.shape[0], P, -1)

    def interleave(a, b):
        return np.stack([a, b], axis=2).reshape(a.shape[0], -1, *a.shape[2:])

    def up(w):
        s = strips(w)
        return interleave(s[:, :D_FF // P], s[:, D_FF // P:])

    def down(w):
        w, out, r = A(w), [], 0
        for n in FF_PARTS:
            out.append(strips(w[:, r:r + n * P]))
            r += n * P
        return np.concatenate(out[:2], axis=1), out[2]

    win = A(w_in)
    aw, bw = 3 * H_A * HD_A, 4 * H_B * HD_B
    s_main, s_br = strips(win[:, :, :aw + bw]), strips(win[:, :, aw + bw + 4 * H_B:])
    w_in_s = np.concatenate([s_main, interleave(s_br[:, :KT], s_br[:, KT:])], axis=1)
    gate_at = [(0, 0), (FROW, 1), (32, 2), (FROW + 32, 3)]
    wg = np.zeros((DEPTH, D_MODEL, P), f32)
    for to, j in gate_at:
        wg[:, :, to:to + H_B] = win[:, :, aw + bw + j * H_B:aw + bw + (j + 1) * H_B]
    par = np.zeros((DEPTH, P, N_PAR), f32)
    par[:, :, P_BADA:P_GN] = columns(b_ada, N_MOD * KT)
    par[:, :, P_GN:P_GQK] = columns(g_norm, KT)
    par[:, :, P_GQK] = np.tile(A(g_qn), (1, 2))
    par[:, :, P_GQK + 1] = np.tile(A(g_kn), (1, 2))
    par[:, :, P_GHN:P_BG] = columns(g_hn, H_B)
    for to, j in gate_at:
        par[:, to:to + H_B, P_BG] = A(b_gates)[:, j * H_B:(j + 1) * H_B]
    par[:, 0:H_B, P_M0] = A(state_m)[0, :, 0]
    par[:, 32:32 + H_B, P_M0] = A(state_m)[0, :, 1]

    const = np.zeros((P, N_CONST), f32)
    i = np.arange(P)
    const[:, C_ID:C_ID + P] = np.eye(P)
    const[:, C_BO:C_BO + P] = (i[:, None] // HD_A == i[None] // HD_A) / HD_A
    const[:, C_ON:C_ON + P] = 1.0 / D_MODEL
    half = HD_B // 2
    for m in range(half):
        const[m + half, C_ROT + m] = -1.0
        const[m, C_ROT + m + half] = 1.0
    const[:, C_MASK:C_MASK + P] = np.where(i[:, None] <= i[None], 0.0, 1e30)
    const[:, C_MASK + P:C_MASK + 2 * P] = np.where(i[:, None] >= i[None], 0.0, 1e30)
    t = np.arange(NTOK)
    const[:, C_RESET:C_RESET + NTOK] = (t % P != 0)
    const[32:, C_RESET:C_RESET + NTOK] = (t % P != P - 1)
    const[:, C_EPS] = EPS
    nf = half // 2
    inv = f32(10000.0) ** (-np.arange(nf, dtype=f32) / f32(nf))
    tl = np.arange(NLAT)
    ang = np.concatenate([(tl // GRID_W).astype(f32)[:, None] * inv, (tl % GRID_W).astype(f32)[:, None] * inv], axis=1)
    rope = np.zeros((P, NTOK + NLAT), f32)
    rope[:, :NLAT] = np.tile(np.cos(ang).T, (2, 1))
    rope[:, NLAT:NTOK] = 1.0
    rope[:, NTOK:] = np.tile(np.sin(ang).T, (2, 1))

    qc, qr = i[:, None] // ROWS, i[:, None] % ROWS
    kc, kr = np.arange(WIN)[None] // ROWS, np.arange(WIN)[None] % ROWS
    rp = A(rpb)
    bias = np.zeros((DEPTH, H_A, P, 3, 3 * P), f32)
    for kind, qb in enumerate((0, 1, 3)):
        cq, ck = qc + 16 * qb, kc + QB_KEY[qb] // ROWS
        start = np.clip(cq - 8, 0, GRID_W - 16)
        ok = (ck >= start) & (ck < start + 16)
        dr, dc = np.broadcast_to(kr - qr + 7, ok.shape), np.clip(ck - cq + 15, 0, 30)
        bias[:, :, :, kind, :WIN] = np.where(ok[None, None], rp[:, :, dr, dc], f32(-1e30))

    ff1, ff1b = down(w_dn1)
    ff2, ff2b = down(w_dn2)
    xs = np.concatenate([A(x_sample)[0], A(x_prompt)[0]], axis=0)
    sc, sn = A(state_C)[0], A(state_n)[0]
    state = np.concatenate([sc.transpose(0, 4, 2, 1, 3), sn.transpose(0, 3, 2, 1)[..., None]], axis=4)
    arrays = {
        "x": xs.T.reshape(KT, P, NTOK).transpose(1, 0, 2),
        "cond": np.stack([A(c)[0].reshape(KT, P).T, A(c_ctx).reshape(KT, P).T], axis=2),
        "const": const, "rope": rope, "par": par, "bias": bias,
        "cache_k": A(cache_k)[0].reshape(DEPTH, P, 4, P).transpose(0, 3, 2, 1),
        "cache_v": A(cache_v)[0].reshape(DEPTH, P, H_A * HD_A),
        "state_c": state.reshape(DEPTH, P, 2 * H_B, VW),
        "w_ada": strips(w_ada), "up1": up(w_up1), "dn1a": ff1, "dn1b": ff1b, "wg": strips(wg)[:, 0],
        "w_in": w_in_s, "w_pab": interleave(strips(w_pa), strips(w_pb)), "w_o": strips(w_o),
        "up2": up(w_up2), "dn2a": ff2, "dn2b": ff2b,
    }
    outs = {"y": (P, KT, NTOK), "new_k": (DEPTH, P, 4, NCTX), "new_v": (DEPTH, P, 4, NCTX),
            "new_c": (DEPTH, P, 2 * H_B, VW), "new_m": (DEPTH, 2, H_B, 1)}
    nc = bacc.Bacc("TRN2", target_bir_lowering=False, num_devices=1)
    io, feed = {}, {}
    for name, a in arrays.items():
        a = np.ascontiguousarray(a)
        feed[f"in_{name}"] = a
        io[name] = nc.dram_tensor(f"in_{name}", a.shape, F32, kind="ExternalInput").ap()
    for name, shape in outs.items():
        io[name] = nc.dram_tensor(f"out_{name}", shape, F32, kind="ExternalOutput").ap()
    build(nc, io)
    r = run_bass_kernel_spmd(nc, [feed], core_ids=[0]).results[0]
    yt = r["out_y"].transpose(2, 1, 0).reshape(NTOK, D_MODEL)

    def cache(a):
        return a.transpose(0, 3, 2, 1).reshape(1, DEPTH, NCTX, H_A, HD_A)

    nc_ = r["out_new_c"].reshape(DEPTH, P, H_B, 2, VW)
    return (np.ascontiguousarray(yt[NLAT:])[None], np.ascontiguousarray(yt[:NLAT])[None],
            cache(r["out_new_k"]), cache(r["out_new_v"]),
            nc_[..., :HD_B].transpose(0, 3, 2, 4, 1)[None], nc_[..., HD_B].transpose(0, 3, 2, 1)[None],
            r["out_new_m"].reshape(1, DEPTH, 2, H_B))
```

```python
from contextlib import ExitStack

import concourse.bass as bass
from concourse import mybir

F32 = mybir.dt.float32
F32R = mybir.dt.float32r
ACT = mybir.ActivationFunctionType
ALU = mybir.AluOpType
AX_X = mybir.AxisListType.X

P = 128
D_MODEL = 1024
KT = D_MODEL // P
DEPTH = 2
GRID_W = 64
NLAT = 512
NCTX = 128
NTOK = NLAT + NCTX
ROWS = NLAT // GRID_W
H_A, HD_A = 8, 64
H_B, HD_B = 4, 128
D_FF = 2816
N_MOD = 9
EPS = 1e-6
T1 = 384
T2 = NTOK - T1
R1 = T1 // GRID_W
CH = NTOK // P
LCH = NLAT // P
FF_PARTS = (8, 8, 6)
assert sum(FF_PARTS) * P == D_FF
VW = HD_B + 1
ROWP = 36
FROW = 64
QB_KEY = (0, 64, 192, 256)
QB_KIND = (0, 1, 1, 2)
WIN = 256
NUNIT = H_A * CH

C_ID, C_SEL, C_ON, C_ROT, C_MASK, C_RESET = 0, 128, 256, 384, 512, 768
C_EPS = C_RESET + NTOK
C_ONE = C_EPS + 1
N_CONST = C_ONE + 1
P_GQK, P_GHN, P_BG, P_M0 = 0, 2, 6, 7
N_PAR = 8

ROW_STEPS, ROW_ABS, ROW_M = 18, 1, 8
NUM_FWD, NUM_BWD = 9, 10
NUM_STEPS = H_B * (NUM_FWD + NUM_BWD)

JOBS = N_MOD // 3
JOB_W = 3 * D_MODEL
JOB_PARTS = JOB_W // 1024
JOB_T = JOB_W // P

FFN_PAIRS = D_FF // P + 3 * KT // 2
INA_PAIRS, INB_PAIRS, YA_PAIRS, OB_PAIRS, YB_PAIRS, O_PAIRS = 6, 6, KT, 2, KT, KT // 2
MIX_PAIRS = INA_PAIRS + INB_PAIRS + YA_PAIRS + OB_PAIRS + YB_PAIRS + O_PAIRS
PAIRS = 2 * FFN_PAIRS + MIX_PAIRS
SPLITS = (PAIRS + 1, PAIRS)
BUF = PAIRS // 2
X_UPD = 2 * 3 * KT + KT
X_IN = 16
H_TILES = 4 * KT


def build(nc, io):
    with ExitStack() as ctx:
        def sb(name, shape, dt=F32):
            return ctx.enter_context(nc.sbuf_tensor(name, shape, dt))

        def shared(name, shape):
            with nc.sbuf_tensor(name + "32", shape, F32) as scratch:
                pass
            return sb(name, shape, F32R), scratch

        def sem(name):
            return ctx.enter_context(nc.semaphore(name))

        x = sb("x", [P, KT, NTOK])
        h_hi = sb("h_hi", [P, KT, NTOK], F32R)
        h_lo = sb("h_lo", [P, KT, NTOK], F32R)
        g_hi, g_hi32 = shared("g_hi", [P, 8, NTOK])
        g_lo, g_lo32 = shared("g_lo", [P, 8, NTOK])
        w_raw = sb("w_raw", [P, 2, 1024])
        w_hi = sb("w_hi", [P, 2, 1024], F32R)
        w_lo = sb("w_lo", [P, 2, 1024], F32R)
        with nc.sbuf_tensor("b_hi", [P, H_B, NTOK], F32R) as b_hi, nc.sbuf_tensor("b_lo", [P, H_B, NTOK], F32R) as b_lo:
            pass
        pool = sb("pool", [P, 19328])
        const = sb("const", [P, N_CONST])
        par = sb("par", [P, N_PAR])
        cond = sb("cond", [P, KT, 2])
        job_par = sb("job_par", [P, JOBS * DEPTH * (JOB_T + KT)])
        mod = sb("mod", [P, N_MOD * KT, 2])
        mod_a = sb("mod_a", [P, 3, KT, 2])
        gate = sb("gate", [P, 3, KT, 2])
        stat = sb("stat", [P, 3, NUNIT])
        small = sb("small", [P, 80])
        eps = const[:, C_EPS:C_EPS + 1]

        def area(at, *shape):
            n = 1
            for s in shape:
                n *= s
            a = pool[:, at:at + n]
            if len(shape) == 2:
                return a.rearrange("p (a b) -> p a b", b=shape[1])
            if len(shape) == 3:
                return a.rearrange("p (a b c) -> p a b c", b=shape[1], c=shape[2])
            return a

        hx, sq, rstd = area(0, 2, NTOK), area(2 * NTOK, 2, NTOK), area(4 * NTOK, NTOK)
        sg, gt, ssum = area(5 * NTOK, 2, NTOK), area(7 * NTOK, 2, NTOK), area(9 * NTOK, NTOK)
        ada_acc, ada_w = area(6400, 2, JOB_W), area(6400 + 2 * JOB_W, JOB_PARTS, 1024)
        ada_w0 = area(6400 + 2 * JOB_W, 2, JOB_W)
        qkv = area(0, 12, NTOK)
        att = area(8 * NTOK, CH, H_A * HD_A)
        v_tok = area(7680, 8, 512)
        cache_v, cache_k = area(11776, 512), area(12288, 4, P)
        bias = area(12800, 6, 384)
        s_neg, p_att, p_t = area(15104, 2, 384), area(15872, 2, 384), area(16640, 2, 384)
        qsq, qrs = area(15104, 2, NTOK), area(16384, 1024)
        head_pick = area(18304, 1024)
        wt, st, hnum = area(5120, NTOK), area(5760, NTOK), area(6400, CH, VW)
        c_out = area(7045, 2, VW)
        v_aug = area(7680, CH, H_B, VW)
        k_tok = area(10260, CH, 512)
        cos, sin = area(10260, NTOK), area(10900, NLAT)
        hb = area(12820, CH, 512)
        num, kw = area(15380, CH, VW), area(16025, CH, P)
        col = area(16665, 4, CH * ROWP)
        row_gate, row_m_rel = area(17408, NTOK), area(18048, NTOK)
        row_exp, row_lf, row_b, row_m = (area(12820 + i * NTOK, NTOK) for i in range(4))
        row_g, row_a, row_w = area(15380, NTOK), area(16020, NTOK), area(18688, NTOK)
        rtmp = area(12820, 2, NLAT)
        c_seq = [area(17408, LCH, VW), area(18688, LCH, VW)]
        hsq = area(10260, CH, 512)
        ob_sig = area(5120, H_B, NTOK)
        br_sig, ty = area(7680, 2, NTOK), area(8960, 2, NTOK)
        hbt = area(10260, 2, 512)

        ident, one = const[:, C_ID:C_ID + P], const[:, C_ONE:C_ONE + 1]
        head_sel = const[:, C_SEL:C_SEL + P].rearrange("p (t r) -> p t r", r=16)
        mean_ones = const[:, C_ON:C_ON + P]
        rot = const[:, C_ROT:C_ROT + P]
        mask = const[:, C_MASK:C_MASK + 2 * P].rearrange("p (a b) -> p a b", b=P)
        reset = const[:, C_RESET:C_RESET + NTOK]
        mprev, dec = small[:, 0:8], small[:, 8:48].rearrange("p (a b) -> p a b", b=CH)
        hss, den = small[:, 48:68], small[:, 68:73]
        gcols = col.rearrange("p k (c r) -> p k c r", r=ROWP)

        bank = [ctx.enter_context(nc.psum_tensor(f"pair{b}", [P, 3, 512], F32)) for b in range(2)]
        m1 = ctx.enter_context(nc.psum_tensor("m1", [P, 512], F32))
        m2 = ctx.enter_context(nc.psum_tensor("m2", [P, 512], F32))
        pa, pb = bank

        def y(d):
            return (g_hi32 if d < 4 else g_lo32)[:, 4 + d % 4, :]

        def piece1(b):
            return bank[b][:, 0:2, 0:T1]

        def piece2(b):
            return bank[b][:, 2, :].rearrange("p (a b) -> p a b", b=T2)

        def by_column(ap):
            return ap.rearrange("p (c r) -> p r c", r=ROWS)

        def by_row(ap):
            return ap.rearrange("p (r c) -> p r c", c=GRID_W)

        const_in = sem("const_in")
        par_in = sem("par_in")
        x_upd = sem("x_upd")
        landed = [sem("landed0"), sem("landed1")]
        raw_free = [sem("raw_free0"), sem("raw_free1")]
        hi_ready = [sem("hi_ready0"), sem("hi_ready1")]
        lo_ready = [sem("lo_ready0"), sem("lo_ready1")]
        strip_done = [sem("strip_done0"), sem("strip_done1")]
        taken = [sem("taken0"), sem("taken1")]
        cond_ready = sem("cond_ready")
        first_in = [sem(f"first_in{j}") for j in range(2 * JOB_PARTS)]
        ada_in = [sem(f"ada_in{j}") for j in range(JOB_PARTS)]
        first_dv, first_pe = sem("first_dv"), sem("first_pe")
        ada_step = sem("ada_step")
        acc_zeroed, ada_summed, mods = sem("acc_zeroed"), sem("ada_summed"), sem("mods")
        sq_ready, ssum_step, ms_done = sem("sq_ready"), sem("ssum_step"), sem("ms_done")
        ln_done, rstd_ready = sem("ln_done"), sem("rstd_ready")
        h_scaled, h_hi_ready, h_lo_ready = (sem(s) for s in ("h_scaled", "h_hi_ready", "h_lo_ready"))
        cache_in, pick_in = sem("cache_in"), sem("pick_in")
        silu_done, g_hi_ready, g_lo_ready = (sem(s) for s in ("silu_done", "g_hi_ready", "g_lo_ready"))
        gate_taken = sem("gate_taken")
        qsq_ready, qss_done, qln_done, qrs_ready = (sem(s) for s in ("qsq_ready", "qss_done", "qln_done", "qrs_ready"))
        q_rms_done, qk_normed = sem("q_rms_done"), sem("qk_normed")
        vt_done, vt_taken = sem("vt_done"), sem("vt_taken")
        bias_in = [sem("bias_in0"), sem("bias_in1")]
        s_done, s_taken, p_ready, pt_done, pt_taken = (sem(s) for s in ("s_done", "s_taken", "p_ready", "pt_done", "pt_taken"))
        pv_done, rinv_ready, att_ready = sem("pv_done"), sem("rinv_ready"), sem("att_ready")
        at_done, at_hi, at_lo = sem("at_done"), sem("at_hi"), sem("at_lo")
        kv_out, rope_in = sem("kv_out"), sem("rope_in")
        gq = sem("gq")
        rot_done, rope_step = sem("rot_done"), sem("rope_step")
        kt_done, kt_taken, va_done, va_taken, ones_set = (sem(s) for s in ("kt_done", "kt_taken", "va_done", "va_taken", "ones_set"))
        row_step, row_act = sem("row_step"), sem("row_act")
        cols_done, cols_ready = sem("cols_done"), sem("cols_ready")
        c_in = [sem("c_in0"), sem("c_in1")]
        kq_done, mb_done, mb_taken, wt_ready, st_ready, kw_ready, upd_done = (sem(s) for s in (
            "kq_done", "mb_done", "mb_taken", "wt_ready", "st_ready", "kw_ready", "upd_done"))
        intra_done, inter_done, c_step, num_step = sem("intra_done"), sem("inter_done"), sem("c_step"), sem("num_step")
        cout_ready, cout_out, m_out = sem("cout_ready"), [sem("cout_out0"), sem("cout_out1")], sem("m_out")
        hb_step, hb_act = sem("hb_step"), sem("hb_act")
        ht_done, ht_prod, ht_hi, ht_lo = (sem(s) for s in ("ht_done", "ht_prod", "ht_hi", "ht_lo"))
        ob_done, ga_done, br_done, ty_step = sem("ob_done"), sem("ga_done"), sem("br_done"), sem("ty_step")
        out_done = sem("out_done")

        F1 = 0
        INA = FFN_PAIRS
        INB = INA + INA_PAIRS
        YA = INB + INB_PAIRS
        OB = YA + YA_PAIRS
        YB = OB + OB_PAIRS
        OS = YB + YB_PAIRS
        F2 = OS + O_PAIRS

        def fills(l, pair):
            return l * BUF + pair // 2 + 1

        def filled(l, pair):
            return l * PAIRS + pair + 2

        def ada_steps(l, j):
            return l * (JOBS * KT) + (j + 1) * KT

        def q_rms_out(t):
            return (m1[:, 0:T1], m2[:, 0:T2]) if t % 2 == 0 else (pa[:, 0, 0:T1], pa[:, 1, 0:T2])

        def row_of(n):
            return 32 * (n % 2) + n // 2

        def steps_before(l, n):
            return l * NUM_STEPS + (n // 2) * (NUM_FWD + NUM_BWD) + (n % 2) * NUM_FWD

        def at_views(dst, c):
            src = pa[:, c % 2, :]
            if c == LCH:
                return src.rearrange("p (f t) -> p f t", f=4), dst[:, 0:4, NLAT:NTOK]
            w = GRID_W // LCH
            return (src.rearrange("p (f c r) -> p f c r", f=4, r=ROWS),
                    dst[:, 0:4, 0:NLAT].rearrange("p f (r c) -> p f c r", r=ROWS)[:, :, c * w:(c + 1) * w, :])

        settled = sem("settled")

        def settle(eng):
            eng.sem_inc(settled, 1)

        block = ctx.enter_context(nc.Block())

        @block.sync
        def _(sp):
            for s in range(2):
                sp.sem_inc(raw_free[s], 1)

            def load(s, l, use, src):
                sp.wait_ge(raw_free[s], l * SPLITS[s] + use + 1)
                sp.dma_start(w_raw[:, s, 0:src.shape[-1]], src).then_inc(landed[s], 16)

            def stream(l, pairs, use, src):
                with sp.Fori(0, pairs) as i:
                    for s in range(2):
                        load(s, l, use[s] + i, src[l, bass.ds(i * 2 + s, 1), :, :].rearrange("a p n -> p (a n)"))

            def ada(n, at):
                for j in range(JOB_PARTS):
                    sp.wait_ge(ada_step, n * JOB_PARTS + (j + 1))
                    sp.dma_start(ada_w[:, j:j + 1, :], io["w_ada"][bass.ds(at, 1), :, j * 1024:(j + 1) * 1024]
                                 .rearrange("a p n -> p a n")).then_inc(ada_in[j], 16)

            def ffn(l, use, up, dn, dn_last, jobs):
                for f, n in enumerate(FF_PARTS):
                    first = sum(FF_PARTS[:f])
                    part, before = up[:, 2 * first:2 * (first + n)], [u + first + 4 * f for u in use]
                    if f < len(jobs):
                        with sp.Fori(0, KT) as i:
                            for s in range(2):
                                load(s, l, before[s] + i, part[l, bass.ds(i * 2 + s, 1), :, :]
                                     .rearrange("a p n -> p (a n)"))
                            ada(i + ada_steps(l, jobs[f]), i + (l * (JOBS * KT) + jobs[f] * KT))
                    else:
                        stream(l, n, before, part)
                    src = dn[:, f * KT:(f + 1) * KT] if f < 2 else dn_last
                    stream(l, KT // 2, [u + first + n + 4 * f for u in use], src)

            for k in range(KT):
                for j in range(JOB_PARTS):
                    if k >= 2:
                        if j < JOB_PARTS - 1:
                            sp.wait_ge(first_dv, (k - 2) * (JOB_PARTS - 1) + (j + 1))
                        else:
                            sp.wait_ge(first_pe, k - 1)
                    cols = slice(j * 1024, (j + 1) * 1024)
                    sp.dma_start(ada_w0[:, k % 2, cols], io["w_ada"][(DEPTH * JOBS - 1) * KT + k, :, cols]
                                 ).then_inc(first_in[k % 2 * JOB_PARTS + j], 16)
            with sp.Fori(0, DEPTH) as l:
                ffn(l, (0, 0), io["up1"], io["dn1a"], io["dn1b"], (0, 1))
                stream(l, INA_PAIRS, (INA, INA), io["w_in"][:, 0:12])
                load(0, l, INB, io["wg"][bass.ds(l, 1)].rearrange("a p n -> p (a n)"))
                for s in range(2):
                    load(s, l, INB + 1 - s, io["w_in"][bass.ds(l, 1), 12 + s].rearrange("a p n -> p (a n)"))
                sp.wait_ge(h_lo_ready, l * H_TILES + KT + 1)
                sp.wait_ge(mods, l * (3 * JOBS) + 9)
                for h in range(H_A):
                    if h >= 2:
                        sp.wait_ge(s_taken, l * NUNIT + (h - 1) * CH)
                    sp.dma_start(bias[:, 3 * (h % 2):3 * (h % 2) + 3, :],
                                 io["bias"][bass.ds(l, 1), h].rearrange("a p k n -> p (a k) n")
                                 ).then_inc(bias_in[h % 2], 16)
                with sp.Fori(1, INB_PAIRS) as i:
                    for s in range(2):
                        load(s, l, INB + 1 - s + i,
                             io["w_in"][l, bass.ds(i * 2 + 12 + s, 1), :, :].rearrange("a p n -> p (a n)"))

                def gated(first, gate_strips, out_strips):
                    with sp.Fori(0, KT) as d:
                        load(0, l, d + (first + 1), io["w_in"][l, bass.ds(d + gate_strips, 1), :, :].rearrange("a p n -> p (a n)"))
                        load(1, l, d + first, io["w_pab"][l, bass.ds(d + out_strips, 1), :, :].rearrange("a p n -> p (a n)"))

                gated(YA, 28, 0)
                stream(l, OB_PAIRS, (OB + 1, OB), io["w_in"][:, 24:28])
                gated(YB, 28 + KT, KT)
                stream(l, O_PAIRS, (OS + 1, OS), io["w_o"])
                sp.wait_ge(ht_lo, (l + 1) * CH)
                settle(sp)
                ffn(l, (F2 + 1, F2), io["up2"], io["dn2a"], io["dn2b"], (2,))
            sp.wait_ge(x_upd, X_IN + DEPTH * X_UPD)
            sp.dma_start(io["y"], x[:]).then_inc(out_done, 16)
            sp.wait_ge(out_done, 16)
            sp.wait_ge(kv_out, DEPTH * 32)
            for j in range(2):
                sp.wait_ge(cout_out[j], DEPTH * H_B * 16)
            sp.wait_ge(m_out, DEPTH * 32)

        @block.gpsimd
        def _(po):
            def split_lo(s, l, n):
                po.wait_ge(hi_ready[s], l * SPLITS[s] + n + 1)
                nc.gpsimd.tensor_tensor(w_lo[:, s, :], w_raw[:, s, :], w_hi[:, s, :].bitcast(F32),
                                        ALU.subtract).then_inc(lo_ready[s], 1)
                po.wait_ge(lo_ready[s], l * SPLITS[s] + n + 1)
                po.sem_inc(raw_free[s], 1)

            with po.Fori(0, DEPTH) as l:
                with po.Fori(0, INB) as i:
                    for s in range(2):
                        split_lo(s, l, i)
                split_lo(0, l, INB)
                po.wait_ge(qk_normed, (l + 1) * 8)
                settle(po)
                po.dma_start(io["new_k"][bass.ds(l, 1)].rearrange("a p f t -> p (a f) t"),
                             qkv[:, 4:8, NLAT:NTOK]).then_inc(kv_out, 16)
                po.wait_ge(taken[1], fills(l, INB - 1) + 1)
                settle(po)
                po.dma_start(io["new_v"][bass.ds(l, 1)].rearrange("a p f t -> p (a f) t"),
                             qkv[:, 8:12, NLAT:NTOK]).then_inc(kv_out, 16)
                for s in range(2):
                    split_lo(s, l, INB + 1 - s)
                po.wait_ge(at_done, (l + 1) * CH)
                settle(po)
                po.dma_start(pool[:, 10260:10260 + NTOK + NLAT], io["rope"]).then_inc(rope_in, 16)
                with po.Fori(1, INB_PAIRS) as i:
                    for s in range(2):
                        split_lo(s, l, i + INB + 1 - s)
                for s in range(2):
                    split_lo(s, l, YA + 1 - s)
                po.wait_ge(row_step, l * ROW_STEPS + ROW_M)
                settle(po)
                po.dma_start(io["new_m"][bass.ds(l, 1), 0].rearrange("a h o -> (a h) o"),
                             row_m[0:H_B, NTOK - 1:NTOK]).then_inc(m_out, 16)
                po.dma_start(io["new_m"][bass.ds(l, 1), 1].rearrange("a h o -> (a h) o"),
                             row_m[32:32 + H_B, NLAT:NLAT + 1]).then_inc(m_out, 16)
                po.wait_ge(cols_done, (l + 1) * 2)
                po.wait_ge(row_step, (l + 1) * ROW_STEPS)

                def load_state(n):
                    settle(po)
                    po.dma_start(c_seq[n % 2][:, 0:1, :], io["state_c"][bass.ds(l, 1), :, n, :]
                                 .rearrange("a p n -> p a n")).then_inc(c_in[n % 2], 16)

                def store_state(n):
                    po.wait_ge(cout_ready, l * 8 + n + 1)
                    settle(po)
                    po.dma_start(io["new_c"][bass.ds(l, 1), :, n, :].rearrange("a p n -> p a n"),
                                 c_out[:, n % 2:n % 2 + 1, :]).then_inc(cout_out[n % 2], 16)

                load_state(0)
                load_state(1)
                for n in range(2 * H_B):
                    if 1 <= n < 2 * H_B - 1:
                        po.wait_ge(inter_done, l * 8 + n)
                        load_state(n + 1)
                    if n >= 1:
                        store_state(n - 1)
                    for s in range(2):
                        split_lo(s, l, YA + n + 2 - s)
                store_state(2 * H_B - 1)
                with po.Fori(1, PAIRS - OB) as i:
                    for s in range(2):
                        split_lo(s, l, i + OB + 1 - s)

        @block.scalar
        def _(ac):
            ac.dma_start(const[:], io["const"]).then_inc(const_in, 16)
            ac.dma_start(cond[:], io["cond"]).then_inc(const_in, 16)
            ac.dma_start(job_par[:], io["job_par"]).then_inc(const_in, 16)
            ac.dma_start(x[:], io["x"]).then_inc(x_upd, X_IN)
            for s in range(2):
                ac.sem_inc(strip_done[s], 1)
                ac.sem_inc(taken[s], 1)
            ac.wait_ge(const_in, 48)
            nc.scalar.activation(cond[:], cond[:], ACT.Silu).then_inc(cond_ready, 1)

            def split_hi(s, l, n):
                ac.wait_ge(strip_done[s], l * SPLITS[s] + n + 1)
                ac.wait_ge(landed[s], (l * SPLITS[s] + n) * 16 + 16)
                nc.scalar.activation(w_hi[:, s, :], w_raw[:, s, :], ACT.Copy).then_inc(hi_ready[s], 1)

            def squares(n, done, pair):
                for k in (2 * pair, 2 * pair + 1):
                    if done is not None:
                        ac.wait_ge(x_upd, done + (k + 1))
                    if k >= 3:
                        ac.wait_ge(ssum_step, n * (KT - 1) + (k - 2))
                    nc.scalar.activation(sq[:, k % 2, :] if k else ssum, x[:, k, :], ACT.Square).then_inc(sq_ready, 1)

            def norm(l, i):
                n = l * 3 + i
                ac.wait_ge(ms_done, n + 1)
                nc.scalar.activation(rstd[:, 0:T1], m1[:, 0:T1], ACT.Ln, bias=eps).then_inc(ln_done, 1)
                nc.scalar.activation(rstd[:, T1:NTOK], m2[:, 0:T2], ACT.Ln, bias=eps).then_inc(ln_done, 1)
                ac.wait_ge(ln_done, n * 2 + 2)
                nc.scalar.activation(rstd, rstd, ACT.Exp, scale=-0.5).then_inc(rstd_ready, 1)
                for k in range(KT):
                    ac.wait_ge(h_scaled, n * KT + (k + 1))
                    for g, cols in ((0, slice(0, NLAT)), (1, slice(NLAT, NTOK))):
                        ins = nc.scalar.activation(h_hi[:, k, cols], hx[:, k % 2, cols], ACT.Identity,
                                                   bias=mod[:, 3 * i * KT + k, g:g + 1])
                    ins.then_inc(h_hi_ready, 1)

            def last_pairs(l, at, n, done, next_splits=True):
                for i in range(KT // 2):
                    if i < KT // 2 - 1 or next_splits:
                        for s in range(2):
                            split_hi(s, l, at[s] + i)
                    squares(n, done, i)

            def ffn(l, base, split, j, last):
                for f, n in enumerate(FF_PARTS):
                    first = sum(FF_PARTS[:f])
                    at = base + first + 4 * f
                    with ac.Fori(0, n // 2) as q:
                        for b in range(2):
                            for s in range(2):
                                split_hi(s, l, q * 2 + (at + b + 1 + (split if s == 0 else 0)))
                            ac.wait_ge(strip_done[1], q * 2 + filled(l, at + b))
                            nc.scalar.activation(sg[:, b, 0:T1], bank[b][:, 0, 0:T1], ACT.Silu)
                            nc.scalar.activation(sg[:, b, T1:NTOK], bank[b][:, 2, 0:T2], ACT.Silu)\
                                .then_inc(silu_done, 1)
                            ac.wait_ge(taken[b], q + (fills(l, at + b) + 1))
                            nc.scalar.activation(g_hi[:, bass.ds(q * 2 + b, 1), :],
                                                 gt[:, b:b + 1, :], ACT.Copy).then_inc(g_hi_ready, 1)
                    at += n
                    if f < 2:
                        with ac.Fori(0, KT // 2) as i:
                            for s in range(2):
                                split_hi(s, l, i + (at + 1 + (split if s == 0 else 0)))
                    else:
                        last_pairs(l, (at + 1 + split, at + 1), l * 3 + 1 + 2 * j,
                                   l * X_UPD + X_IN + (2, 6)[j] * KT, not last)

            def q_squares(l, pair):
                ac.wait_ge(taken[pair % 2], fills(l, INA + pair) + 1)
                for t in (2 * pair, 2 * pair + 1):
                    if t >= 2:
                        ac.wait_ge(qss_done, l * 8 + (t - 1))
                    nc.scalar.activation(qsq[:, t % 2, :], qkv[:, t, :], ACT.Square).then_inc(qsq_ready, 1)

            def q_rs(l):
                ac.wait_ge(qss_done, l * 8 + 8)
                nc.scalar.activation(qrs[0:16, 0:T1], m1[0:16, 0:T1], ACT.Ln, bias=eps[0:16]).then_inc(qln_done, 1)
                nc.scalar.activation(qrs[0:16, T1:NTOK], m2[0:16, 0:T2], ACT.Ln, bias=eps[0:16]).then_inc(qln_done, 1)
                ac.wait_ge(qln_done, l * 2 + 2)
                nc.scalar.activation(qrs[0:16, 0:NTOK], qrs[0:16, 0:NTOK], ACT.Exp, scale=-0.5).then_inc(qrs_ready, 1)

            ac.wait_ge(x_upd, X_IN)
            for p in range(KT // 2):
                squares(0, None, p)
            with ac.Fori(0, DEPTH) as l:
                ac.wait_ge(x_upd, l * X_UPD + X_IN)
                ac.dma_start(par[:], io["par"][bass.ds(l, 1)].rearrange("a p n -> p (a n)")).then_inc(par_in, 16)
                for s in range(2):
                    split_hi(s, l, 0)
                norm(l, 0)
                ffn(l, F1, 0, 0, False)
                norm(l, 1)
                ac.wait_ge(mods, l * (3 * JOBS) + 9)
                ac.dma_start(head_pick[0:16, :], io["pick"]).then_inc(pick_in, 16)
                ac.dma_start(cache_v, io["cache_v"][bass.ds(l, 1)].rearrange("a p n -> p (a n)")).then_inc(cache_in, 16)
                ac.dma_start(cache_k, io["cache_k"][bass.ds(l, 1)].rearrange("a p f n -> p (a f) n")).then_inc(cache_in, 16)
                for i in range(INA_PAIRS):
                    for s in range(2):
                        split_hi(s, l, INA + 1 + i)
                    if i < 4:
                        q_squares(l, i)
                    if i == 4:
                        q_rs(l)
                split_hi(0, l, INB + 1)
                for i in range(8):
                    ac.wait_ge(vt_done, l * 8 + i + 1)
                    nc.scalar.activation(v_tok[:, i, :], (pa if i % 2 == 0 else pb)[:, 2, :], ACT.Copy)\
                        .then_inc(vt_taken, 1)
                for u in range(NUNIT + 1):
                    n = l * NUNIT + u
                    if u < NUNIT:
                        lo, hi = (0, 384) if u % CH < LCH else (WIN, 384)
                        ac.wait_ge(s_taken, n + 1)
                        if u >= 2:
                            ac.wait_ge(pt_done, n - 1)
                        nc.scalar.activation(p_att[:, u % 2, lo:hi], s_neg[:, u % 2, lo:hi], ACT.Exp, scale=-1.0,
                                             bias=stat[:, 0, u:u + 1], accum_out=stat[:, 1, u:u + 1])\
                            .then_inc(p_ready, 1)
                    if u >= 1:
                        v = u - 1
                        lo, hi = (0, 384) if v % CH < LCH else (WIN, 384)
                        ac.wait_ge(pt_done, n)
                        if v >= 2:
                            ac.wait_ge(pv_done, n - 2)
                        src = (pa[:, 2, :], pb[:, 0, :])[v % 2]
                        nc.scalar.activation(p_t[:, v % 2, lo:hi], src[:, lo:hi], ACT.Copy).then_inc(pt_taken, 1)
                for c in range(CH):
                    ac.wait_ge(at_done, l * CH + c + 1)
                    src, dst = at_views(g_hi, c)
                    nc.scalar.activation(dst, src, ACT.Copy).then_inc(at_hi, 1)
                with ac.Fori(0, INB_PAIRS) as i:
                    for s in range(2):
                        split_hi(s, l, i + (INB + 1 + 1 - s))
                fr = slice(FROW, FROW + ROWP)
                ac.wait_ge(row_step, l * ROW_STEPS + ROW_ABS)
                nc.scalar.activation(row_exp[fr, :], row_exp[fr, :], ACT.Exp, scale=-1.0).then_inc(row_act, 1)
                ac.wait_ge(row_act, l * 2 + 1)
                nc.scalar.activation(row_exp[fr, :], row_exp[fr, :], ACT.Ln, bias=1.0).then_inc(row_act, 1)
                for c in range(CH):
                    ac.wait_ge(va_done, l * CH + c + 1)
                    nc.scalar.activation(v_aug[:, c, :, 0:HD_B], (pb[:, 1, :], pb[:, 2, :])[c % 2]
                                         .rearrange("p (h d) -> p h d", h=H_B), ACT.Copy).then_inc(va_taken, 1)
                ac.wait_ge(cols_done, l * 2 + 2)
                nc.scalar.activation(col[:, 0, :], m1[:, 0:180], ACT.Copy).then_inc(cols_ready, 1)
                nc.scalar.activation(col[:, 1, :], m1[:, 180:360], ACT.Exp).then_inc(cols_ready, 1)
                nc.scalar.activation(small[:, 8:48], m1[:, 360:400], ACT.Exp).then_inc(cols_ready, 1)
                nc.scalar.activation(col[:, 2, :], m2[:, 0:180], ACT.Exp).then_inc(cols_ready, 1)
                nc.scalar.activation(col[:, 3, :], m2[:, 180:360], ACT.Exp, scale=-1.0).then_inc(cols_ready, 1)
                ac.wait_ge(cols_ready, l * 5 + 5)
                for n in range(2 * H_B):
                    h, back = n // 2, n % 2
                    ac.wait_ge(mb_taken, (l * 8 + n + 1) * 2)
                    for c in range(CH):
                        nc.scalar.activation(wt[:, c * P:(c + 1) * P], wt[:, c * P:(c + 1) * P], ACT.Exp, scale=-1.0,
                                             bias=gcols[:, 0, c, 32 * back + h:32 * back + h + 1]).then_inc(wt_ready, 1)
                    ac.wait_ge(strip_done[0], l * SPLITS[0] + (YA + n + 3))
                    nc.scalar.activation(y(n)[:, 0:T1], pb[:, 0, 0:T1], ACT.Sigmoid)
                    nc.scalar.activation(y(n)[:, T1:NTOK], pb[:, 2, 0:T2], ACT.Sigmoid).then_inc(ga_done, 1)
                    for s in range(2):
                        split_hi(s, l, YA + n + 1 + 1 - s)
                ac.wait_ge(hb_step, l * 3 + 2)
                nc.scalar.activation(hss, hss, ACT.Ln, scale=1.0 / HD_B, bias=eps).then_inc(hb_act, 1)
                ac.wait_ge(hb_act, l * 2 + 1)
                nc.scalar.activation(hss, hss, ACT.Exp, scale=-0.5).then_inc(hb_act, 1)
                for j in range(2):
                    ac.wait_ge(cout_out[j], (l + 1) * H_B * 16)
                for p in range(OB_PAIRS):
                    for s in range(2):
                        split_hi(s, l, OB + p + 1 + 1 - s)
                    ac.wait_ge(strip_done[1], filled(l, OB + p))
                    nc.scalar.activation(ob_sig[:, 2 * p:2 * p + 2, 0:T1], piece1(p), ACT.Sigmoid).then_inc(ob_done, 1)
                    nc.scalar.activation(ob_sig[:, 2 * p:2 * p + 2, T1:NTOK], piece2(p), ACT.Sigmoid)\
                        .then_inc(taken[p], 1)
                    ac.wait_ge(taken[p], fills(l, OB + p) + 1)
                    for t in range(2 * p, 2 * p + 2):
                        nc.scalar.activation(ob_sig[:, t, :], ob_sig[:, t, :], ACT.Copy,
                                             scale=par[:, P_GHN + t:P_GHN + t + 1]).then_inc(ob_done, 1)
                for c in range(CH):
                    ac.wait_ge(ht_prod, l * CH + c + 1)
                    nc.scalar.activation(b_hi[:, :, c * P:(c + 1) * P],
                                         hbt[:, c % 2, :].rearrange("p (f t) -> p f t", f=4), ACT.Copy).then_inc(ht_hi, 1)
                with ac.Fori(0, KT // 2) as q:
                    for b in range(2):
                        split_hi(0, l, q * 2 + (YB + b + 2))
                        ac.wait_ge(strip_done[1], q * 2 + filled(l, YB + b))
                        ac.wait_ge(ty_step, (q * 2 + l * KT) * 2 + (2 * b + 1))
                        nc.scalar.activation(br_sig[:, b, 0:T1], bank[b][:, 0, 0:T1], ACT.Sigmoid)
                        nc.scalar.activation(br_sig[:, b, T1:NTOK], bank[b][:, 2, 0:T2], ACT.Sigmoid).then_inc(br_done, 1)
                        split_hi(1, l, q * 2 + (YB + b + 1))
                for k in range(KT):
                    ac.wait_ge(ty_step, (l * KT + KT) * 2 + 1)
                    nc.scalar.activation(h_hi[:, k, :], y(k), ACT.Copy).then_inc(h_hi_ready, 1)
                last_pairs(l, (OS + 2, OS + 1), l * 3 + 2, l * X_UPD + X_IN + 3 * KT)
                norm(l, 2)
                ffn(l, F2, 1, 1, True)


        @block.tensor
        def _(pe):
            def passes(s, k, t, out1, out2, xh, xl, begin, end, shared=False):
                w = slice(k * P, (k + 1) * P)
                for j, (a, b) in enumerate(((w_hi, xh), (w_hi, xl), (w_lo, xh))):
                    first, last = begin and j == 0, end and j == 2
                    nc.tensor.matmul(out1, a[:, s, w], b[:, t, 0:T1], start=first, stop=last)
                    mm = nc.tensor.matmul(out2, a[:, s, w], b[:, t, T1:NTOK], start=first and not (shared and s == 1),
                                          stop=last and not (shared and s == 0))
                return mm

            def strip(s, l, n, out1, out2, xh, xl, tiles):
                pe.wait_ge(lo_ready[s], l * SPLITS[s] + n + 1)
                for k, t in enumerate(tiles):
                    mm = passes(s, k, t, out1, out2, xh, xl, k == 0, k == len(tiles) - 1)
                mm.then_inc(strip_done[s], 1)

            def pair(l, at, pos, xh, xl, tiles, ready=None, extra=0, q=0, tiles1=None):
                b = at % 2
                pe.wait_ge(taken[b], q + fills(l, at))
                out = [(bank[b][:, s, 0:T1], bank[b][:, 2, s * T2:(s + 1) * T2]) for s in range(2)]
                before = [q * 2 + (at + (extra if s == 0 else 0)) for s in range(2)]
                if ready is None:
                    for s in range(2):
                        strip(s, l, before[s], *out[s], xh, xl, tiles1 if s and tiles1 else tiles)
                    return
                for s in range(2):
                    pe.wait_ge(lo_ready[s], l * SPLITS[s] + before[s] + 1)
                for k in tiles:
                    pe.wait_ge(h_lo_ready, ready + (k + 1))
                    for s in range(2):
                        mm = passes(s, k, k, *out[s], xh, xl, k == 0, k == len(tiles) - 1, True)
                        if k == len(tiles) - 1:
                            mm.then_inc(strip_done[s], 1)

            def pairs(l, at, count, xh, xl, tiles, ready=None, extra=0):
                settle(pe)
                if ready is not None:
                    for b in range(2):
                        pair(l, at + b, b, xh, xl, tiles, None if b else ready, extra)
                with pe.Fori(0 if ready is None else 1, count // 2) as q:
                    for b in range(2):
                        pair(l, at + b, b, xh, xl, tiles, None, extra, q)

            def norm(l, i):
                n = l * 3 + i
                pe.wait_ge(ssum_step, n * (KT - 1) + (KT - 1))
                nc.tensor.matmul(m1[:, 0:T1], mean_ones, ssum[:, 0:T1], start=True, stop=True)
                nc.tensor.matmul(m2[:, 0:T2], mean_ones, ssum[:, T1:NTOK], start=True, stop=True).then_inc(ms_done, 1)

            def modulation(job):
                pe.wait_ge(ada_step, job * (KT * JOB_PARTS) + (KT * JOB_PARTS + JOB_PARTS))
                settle(pe)
                sum_partitions(JOB_T)

            def sum_partitions(tiles):
                for t in range(tiles):
                    for g in range(2):
                        mm = nc.tensor.matmul(m1[:, 2 * t + g:2 * t + g + 1], ada_acc[:, g, t * P:(t + 1) * P], one,
                                              start=True, stop=True)
                mm.then_inc(ada_summed, 1)

            def ffn(l, base, extra, j, jobs):
                for f, n in enumerate(FF_PARTS):
                    at = base + sum(FF_PARTS[:f]) + 4 * f
                    pairs(l, at, n, h_hi, h_lo, range(KT), None if f else l * H_TILES + (0, 3 * KT)[j], extra)
                    pe.wait_ge(g_lo_ready, (l * 2 + j) * (D_FF // P) + sum(FF_PARTS[:f + 1]) + 2)
                    pairs(l, at + n, KT // 2, g_hi, g_lo, range(n), None, extra)
                    if f < len(jobs):
                        if f:
                            pe.wait_ge(mods, l * (3 * JOBS) + 3 * jobs[f] + 3)
                        modulation(l * JOBS + (jobs[f] + 1))

            pe.wait_ge(const_in, 48)
            pe.wait_ge(cond_ready, 1)
            j, tiles = JOB_PARTS - 1, JOB_T // JOB_PARTS
            for k in range(KT):
                pe.wait_ge(first_in[k % 2 * JOB_PARTS + j], k // 2 * 16 + 16)
                for t in range(tiles):
                    at = j * tiles + t
                    mm = nc.tensor.matmul(m1[:, 2 * at:2 * at + 2], ada_w0[:, k % 2, at * P:(at + 1) * P], cond[:, k, :],
                                          start=k == 0 and t == 0, stop=k == KT - 1 and t == tiles - 1)
                mm.then_inc(first_pe, 1)
            pe.wait_ge(first_dv, KT * (JOB_PARTS - 1))
            pe.wait_ge(first_pe, KT)
            sum_partitions(j * tiles)
            with pe.Fori(0, DEPTH) as l:
                pe.wait_ge(mods, l * (3 * JOBS) + 3)
                norm(l, 0)
                ffn(l, F1, 0, 0, (0, 1))
                pe.wait_ge(mods, l * (3 * JOBS) + 9)
                norm(l, 1)
                settle(pe)
                for i in range(INA_PAIRS):
                    pair(l, INA + i, i % 2, h_hi, h_lo, range(KT), l * H_TILES + KT if i == 0 else None)
                    for t in range(2 * (i - 1), 2 * i) if 1 <= i <= 4 else ():
                        pe.wait_ge(qsq_ready, l * 8 + t + 1)
                        nc.tensor.matmul(m1[0:16, 0:T1], head_sel[:, t, :], qsq[:, t % 2, 0:T1], start=t == 0, stop=t == 7)
                        nc.tensor.matmul(m2[0:16, 0:T2], head_sel[:, t, :], qsq[:, t % 2, T1:NTOK],
                                         start=t == 0, stop=t == 7).then_inc(qss_done, 1)

                def q_rms(t):
                    if t >= 2:
                        pe.wait_ge(qk_normed, l * 8 + (t - 1))
                    pick, out = head_pick[0:16, t * P:(t + 1) * P], q_rms_out(t)
                    nc.tensor.matmul(out[0], pick, qrs[0:16, 0:T1], start=True, stop=True)
                    nc.tensor.matmul(out[1], pick, qrs[0:16, T1:NTOK], start=True, stop=True).then_inc(q_rms_done, 1)

                pe.wait_ge(qrs_ready, l + 1)
                pe.wait_ge(pick_in, l * 16 + 16)
                pe.wait_ge(taken[0], fills(l, INB - 2) + 1)
                settle(pe)
                q_rms(0)
                q_rms(1)
                pe.wait_ge(taken[1], fills(l, INB - 1) + 1)
                strip(0, l, INB, pb[:, 0, 0:T1], pb[:, 2, 0:T2], h_hi, h_lo, range(KT))
                for i in range(8):
                    if i < 6:
                        q_rms(i + 2)
                    if i == 1:
                        pe.wait_ge(gate_taken, l * 2 + 2)
                    if i >= 2:
                        pe.wait_ge(vt_taken, l * 8 + i - 1)
                    t0 = 64 * i if i < 7 else NLAT
                    for f in range(4):
                        mm = nc.tensor.transpose((pa if i % 2 == 0 else pb)[:, 2, f * P:(f + 1) * P],
                                                 qkv[:, 8 + f, t0:t0 + P], ident)
                    mm.then_inc(vt_done, 1)
                pe.wait_ge(qk_normed, l * 8 + 8)
                pe.wait_ge(cache_in, l * 32 + 32)

                def scores(u):
                    h, qb = u // CH, u % CH
                    n, hp = l * NUNIT + u, slice(64 * (h % 2), 64 * (h % 2) + 64)
                    if u >= 2:
                        pe.wait_ge(s_taken, n - 1)
                    out = pa[:, u % 2, :]
                    q = qkv[hp, h // 2, qb * P:(qb + 1) * P]
                    if qb < LCH:
                        nc.tensor.matmul(out[:, 0:WIN], q, qkv[hp, 4 + h // 2, QB_KEY[qb]:QB_KEY[qb] + WIN],
                                         start=True, stop=True)
                    k = cache_k[hp, h // 2, :] if qb < LCH else qkv[hp, 4 + h // 2, NLAT:NTOK]
                    nc.tensor.matmul(out[:, WIN:384], q, k, start=True, stop=True).then_inc(s_done, 1)

                def parts(u):
                    return range(3) if u % CH < LCH else range(2, 3)

                def turn(u):
                    n = l * NUNIT + u
                    pe.wait_ge(p_ready, n + 1)
                    if u == 0:
                        pe.wait_ge(vt_taken, l * 8 + 8)
                    if u >= 2:
                        pe.wait_ge(pt_taken, n - 1)
                    out = (pa[:, 2, :], pb[:, 0, :])[u % 2]
                    for j in parts(u):
                        mm = nc.tensor.transpose(out[:, j * P:(j + 1) * P], p_att[:, u % 2, j * P:(j + 1) * P], ident)
                    mm.then_inc(pt_done, 1)

                def weighted(u):
                    h, qb, n = u // CH, u % CH, l * NUNIT + u
                    pe.wait_ge(pt_taken, n + 1)
                    if u >= 2:
                        pe.wait_ge(att_ready, n - 1)
                    hd = slice(h * HD_A, (h + 1) * HD_A)
                    w = QB_KEY[qb] // 64 if qb < LCH else 0
                    values = (v_tok[:, w, hd], v_tok[:, w + 2, hd], cache_v[:, hd] if qb < LCH else v_tok[:, 7, hd])
                    js = list(parts(u))
                    for j in js:
                        mm = nc.tensor.matmul(pb[:, 1 + u % 2, 0:HD_A], p_t[:, u % 2, j * P:(j + 1) * P], values[j],
                                              start=j == js[0], stop=j == js[-1])
                    mm.then_inc(pv_done, 1)

                for u in range(NUNIT + 2):
                    if u < NUNIT:
                        scores(u)
                    if 1 <= u <= NUNIT:
                        turn(u - 1)
                    if u >= 2:
                        weighted(u - 2)
                pe.wait_ge(att_ready, l * NUNIT + NUNIT)
                for c in range(CH):
                    if c >= 2:
                        pe.wait_ge(at_lo, l * CH + c - 1)
                    for f in range(4):
                        mm = nc.tensor.transpose(pa[:, c % 2, f * P:(f + 1) * P], att[:, c, f * P:(f + 1) * P], ident)
                    mm.then_inc(at_done, 1)
                pe.wait_ge(at_lo, l * CH + CH)
                pairs(l, INB, INB_PAIRS, h_hi, h_lo, range(KT), None, 1)
                pe.wait_ge(taken[0], fills(l, YA - 2) + 1)
                pe.wait_ge(taken[1], fills(l, YA - 1) + 1)
                for t in range(8):
                    if t >= 2:
                        pe.wait_ge(rope_step, l * 24 + 3 * (t - 2) + 1)
                    nc.tensor.matmul(pa[:, t % 2, :], rot, qkv[:, t, 0:NLAT], start=True, stop=True)\
                        .then_inc(rot_done, 1)
                pe.wait_ge(rope_step, l * 24 + 24)
                for c in range(CH):
                    if c >= 2:
                        pe.wait_ge(kt_taken, l * CH + c - 1)
                    for h in range(H_B):
                        mm = nc.tensor.transpose((pa[:, 2, :], pb[:, 0, :])[c % 2][:, h * P:(h + 1) * P],
                                                 qkv[:, 4 + h, c * P:(c + 1) * P], ident)
                    mm.then_inc(kt_done, 1)
                for c in range(CH):
                    if c >= 2:
                        pe.wait_ge(va_taken, l * CH + c - 1)
                    for h in range(H_B):
                        mm = nc.tensor.transpose((pb[:, 1, :], pb[:, 2, :])[c % 2][:, h * P:(h + 1) * P],
                                                 qkv[:, 8 + h, c * P:(c + 1) * P], ident)
                    mm.then_inc(va_done, 1)
                pe.wait_ge(row_step, l * ROW_STEPS + ROW_STEPS)
                settle(pe)
                rows = slice(0, ROWP)
                for out, pairs_ in ((m1, (row_g, row_a)), (m2, (row_w, row_m))):
                    for j, r in enumerate(pairs_):
                        for c in range(CH):
                            at = (j * CH + c) * ROWP
                            mm = nc.tensor.transpose(out[:, at:at + ROWP], r[rows, c * P:(c + 1) * P],
                                                     ident[rows, 0:ROWP])
                    if out is m1:
                        for n in range(2 * H_B):
                            e = P - 1 if n % 2 == 0 else 0
                            pick = ident[rows, row_of(n):row_of(n) + 1].broadcast_to([ROWP, P])
                            ends = row_a[rows, :].rearrange("p (c t) -> p c t", t=P)[:, :, e]
                            mm = nc.tensor.matmul(m1[:, 360 + n * CH:360 + (n + 1) * CH], pick, ends, start=True, stop=True)
                    mm.then_inc(cols_done, 1)
                pe.wait_ge(kt_taken, l * CH + CH)
                pe.wait_ge(va_taken, l * CH + CH)
                pe.wait_ge(ones_set, l + 1)
                pe.wait_ge(cols_ready, l * 5 + 5)
                def ya_gate(n, ks):
                    at = YA + n
                    if ks[0] == 0:
                        pe.wait_ge(lo_ready[0], l * SPLITS[0] + (at + 2))
                        if n >= 1:
                            pe.wait_ge(taken[(at - 1) % 2], fills(l, at - 1) + 1)
                        settle(pe)
                    for k in ks:
                        mm = passes(0, k, k, pb[:, 0, 0:T1], pb[:, 2, 0:T2], h_hi, h_lo, k == 0, k == KT - 1)
                    if ks[-1] == KT - 1:
                        mm.then_inc(strip_done[0], 1)

                def ya_out(n):
                    pe.wait_ge(ga_done, l * KT + n + 1)
                    strip(1, l, YA + n, pb[:, 1, 0:T1], pb[:, 2, T2:2 * T2], g_hi, g_lo, range(4))

                inter = pa[:, 2, 0:3 * VW]
                for n in range(2 * H_B):
                    h, g = n // 2, l * 8 + n
                    order = range(LCH) if n % 2 == 0 else range(LCH - 1, -1, -1)
                    rest = 1 if n % 2 == 0 else 0
                    if n >= 1:
                        pe.wait_ge(num_step, steps_before(l, n - 1) + 5)
                        pe.wait_ge(cout_ready, g)
                    if n % 2 == 0:
                        for c in range(CH):
                            cc = slice(c * P, (c + 1) * P)
                            out = pa[:, 0, cc] if c < LCH else pa[:, 1, 0:P]
                            mm = nc.tensor.matmul(out, qkv[:, 4 + h, cc], qkv[:, h, cc], start=True, stop=True)
                        mm.then_inc(kq_done, 1)
                    pick = ident[rows, row_of(n):row_of(n) + 1].broadcast_to([ROWP, P])
                    nc.tensor.matmul(pa[:, 2, :], pick, row_m_rel[rows, 0:NLAT], start=True, stop=True)
                    nc.tensor.matmul(pa[:, 1, P:2 * P], pick, row_m_rel[rows, NLAT:NTOK], start=True, stop=True)\
                        .then_inc(mb_done, 1)
                    ya_gate(n, range(0, KT // 2))
                    pe.wait_ge(kw_ready, g + 1)
                    for j, c in enumerate(order[0:3]):
                        nc.tensor.matmul(m1[:, j * VW:(j + 1) * VW], kw[:, c, :], v_aug[:, c, h, :], start=True, stop=True)
                    nc.tensor.matmul(m2[:, 2 * VW:3 * VW], kw[:, LCH, :], v_aug[:, LCH, h, :], start=True, stop=True)\
                        .then_inc(upd_done, 1)
                    ya_gate(n, range(KT // 2, KT))
                    pe.wait_ge(mb_taken, g * 2 + 2)
                    pe.wait_ge(c_step, g * 3 + 3)
                    pe.wait_ge(st_ready, g * 2 + 2)
                    for c in range(CH):
                        out = m1[:, c * VW:(c + 1) * VW] if c < 3 else m2[:, (c - 3) * VW:(c - 2) * VW]
                        mm = nc.tensor.matmul(out, st[:, c * P:(c + 1) * P], v_aug[:, c, h, :], start=True, stop=True)
                    mm.then_inc(intra_done, 1)
                    pe.wait_ge(c_in[n % 2], (l * 4 + n // 2) * 16 + 16)
                    for j in range(LCH):
                        c = order[j]
                        out = inter[:, (c - rest) * VW:(c - rest + 1) * VW] if j else pa[:, 1, 2 * P:2 * P + VW]
                        mm = nc.tensor.matmul(out, qkv[:, h, c * P:(c + 1) * P], c_seq[n % 2][:, j, :], start=True, stop=True)
                    mm.then_inc(inter_done, 1)
                    ya_out(n)
                pe.wait_ge(num_step, l * NUM_STEPS + NUM_STEPS)
                pe.wait_ge(cout_ready, l * 8 + 8)
                for p in range(OB_PAIRS):
                    pair(l, OB + p, p, h_hi, h_lo, range(KT), None, 1)
                pe.wait_ge(hb_step, l * 3 + 3)
                for c in range(CH):
                    if c >= 2:
                        pe.wait_ge(ht_prod, l * CH + c - 1)
                    for f in range(H_B):
                        mm = nc.tensor.transpose((m1, m2)[c % 2][:, f * P:(f + 1) * P], hb[:, c, f * P:(f + 1) * P], ident)
                    mm.then_inc(ht_done, 1)
                with pe.Fori(0, KT // 2) as q:
                    for b in range(2):
                        pe.wait_ge(taken[b], q + fills(l, YB + b))
                        strip(0, l, q * 2 + (YB + b + 1), bank[b][:, 0, 0:T1], bank[b][:, 2, 0:T2], h_hi, h_lo, range(KT))
                        pe.wait_ge(ht_lo, l * CH + CH)
                        strip(1, l, q * 2 + (YB + b), bank[b][:, 1, 0:T1], bank[b][:, 2, T2:2 * T2], b_hi, b_lo, range(4))
                pairs(l, OS, O_PAIRS, h_hi, h_lo, range(KT), l * H_TILES + 2 * KT, 1)
                norm(l, 2)
                ffn(l, F2, 1, 1, (2,))

        @block.vector
        def _(dv):
            dv.sem_inc(g_lo_ready, 2)
            dv.sem_inc(ty_step, 1)
            dv.wait_ge(const_in, 48)

            def norm(l, i):
                n, m = (l * 3 + i) * KT, l * H_TILES + (0, KT, 3 * KT)[i]
                both = ((0, slice(0, NLAT)), (1, slice(NLAT, NTOK)))
                dv.wait_ge(rstd_ready, l * 3 + i + 1)

                def low(k):
                    dv.wait_ge(h_hi_ready, m + k + 1)
                    for g, cols in both:
                        ins = nc.vector.scalar_tensor_tensor(h_lo[:, k, cols], hx[:, k % 2, cols],
                                                             mod[:, 3 * i * KT + k, g:g + 1],
                                                             h_hi[:, k, cols].bitcast(F32), ALU.add, ALU.subtract)
                    ins.then_inc(h_lo_ready, 1)

                for k in range(KT):
                    if k >= 2:
                        dv.wait_ge(h_lo_ready, m + k - 1)
                    for g, cols in both:
                        ins = nc.vector.scalar_tensor_tensor(hx[:, k % 2, cols], x[:, k, cols], mod_a[:, i, k, g:g + 1],
                                                             rstd[:, cols], ALU.mult, ALU.mult)
                    ins.then_inc(h_scaled, 1)
                    if k >= 1:
                        low(k - 1)
                low(KT - 1)

            def sum_squares(n, pair):
                for k in (2 * pair, 2 * pair + 1):
                    if k == 0:
                        continue
                    dv.wait_ge(sq_ready, n * KT + (k + 1))
                    if k >= 2:
                        dv.wait_ge(ssum_step, n * (KT - 1) + (k - 1))
                    nc.vector.tensor_tensor(ssum, ssum, sq[:, k % 2, :], ALU.add).then_inc(ssum_step, 1)

            def zero_acc(job):
                nc.vector.memset(ada_acc, 0.0).then_inc(acc_zeroed, 1)
                dv.wait_ge(acc_zeroed, job + 1)

            def ada(n, k):
                for j in range(JOB_PARTS):
                    dv.wait_ge(ada_in[j], n * 16 + (16 - 16 * KT))
                    dv.wait_ge(ada_step, n * JOB_PARTS + (j + 1))
                    for g in range(2):
                        cols = slice(j * 1024, (j + 1) * 1024)
                        ins = nc.vector.scalar_tensor_tensor(ada_acc[:, g:g + 1, cols], ada_w[:, j:j + 1, :],
                                                             cond[:, bass.ds(k, 1), g:g + 1].rearrange("p a b -> p (a b)"),
                                                             ada_acc[:, g:g + 1, cols], ALU.mult, ALU.add)
                    ins.then_inc(ada_step, 1)

            def modulation(job, i, at):
                dv.wait_ge(ada_summed, job + 1)
                nc.vector.tensor_tensor(mod[:, i * JOB_T:(i + 1) * JOB_T, :],
                                        m1[:, 0:2 * JOB_T].rearrange("p (j g) -> p j g", g=2),
                                        job_par[:, bass.ds(at, JOB_T), None].broadcast_to([P, JOB_T, 2]),
                                        ALU.add).then_inc(mods, 1)
                dv.wait_ge(mods, job * 3 + 1)
                nc.vector.scalar_tensor_tensor(
                    mod_a[:, i], mod[:, (3 * i + 1) * KT:(3 * i + 2) * KT, :], 1.0,
                    job_par[:, bass.ds(at + JOB_T, KT), None].broadcast_to([P, KT, 2]), ALU.add, ALU.mult).then_inc(mods, 1)
                nc.vector.tensor_scalar(gate[:, i], mod[:, (3 * i + 2) * KT:(3 * i + 3) * KT, :],
                                        1.0 if i == 1 else 0.5, None, ALU.mult).then_inc(mods, 1)
                dv.wait_ge(mods, job * 3 + 3)

            def add_to_x(l, at, done, which, q=0):
                b = at % 2
                dv.wait_ge(strip_done[1], q * 2 + filled(l, at))
                dv.wait_ge(x_upd, done)
                for s in range(2):
                    t = done_tile(q, b, s)
                    end = s * T2 + NLAT - T1
                    for g, cols, ps in ((0, slice(0, T1), bank[b][:, s:s + 1, 0:T1]),
                                        (0, slice(T1, NLAT), bank[b][:, 2:3, s * T2:end]),
                                        (1, slice(NLAT, NTOK), bank[b][:, 2:3, end:(s + 1) * T2])):
                        ins = nc.vector.scalar_tensor_tensor(x[:, t, cols], ps, gate_at(which, t, g), x[:, t, cols],
                                                             ALU.mult, ALU.add)
                    ins.then_inc(x_upd, 1)
                dv.wait_ge(x_upd, done + 2)
                dv.sem_inc(taken[b], 1)

            def done_tile(q, b, s):
                return bass.ds(q * 4 + (2 * b + s), 1)

            def gate_at(which, t, g):
                return gate[:, which, t, g]

            def add_pairs(l, at, done, which, n=None):
                if n is not None:
                    for p in range(KT // 2):
                        if p >= 1:
                            sum_squares(n, p - 1)
                        add_to_x(l, at + p % 2, done + 2 * p, which, p // 2)
                    sum_squares(n, KT // 2 - 1)
                    return
                settle(dv)
                with dv.Fori(0, KT // 4) as q:
                    for b in range(2):
                        add_to_x(l, at + b, q * 4 + (done + 2 * b), which, q)

            def ffn(l, base, j, jobs):
                step = JOB_T + KT
                for f, n in enumerate(FF_PARTS):
                    first = sum(FF_PARTS[:f])
                    at = base + first + 4 * f
                    if f < len(jobs):
                        zero_acc(l * JOBS + (jobs[f] + 1))
                    settle(dv)
                    with dv.Fori(0, n // 2) as q:
                        for b in range(2):
                            if f < len(jobs):
                                ada(q * 2 + (b + ada_steps(l, jobs[f])), q * 2 + b)
                            done = q * 2 + (l * 2 + j) * (D_FF // P) + (first + b)
                            dv.wait_ge(silu_done, done + 1)
                            dv.wait_ge(g_lo_ready, done + 1)
                            nc.vector.tensor_tensor(gt[:, b, 0:T1], sg[:, b, 0:T1], bank[b][:, 1, 0:T1], ALU.mult)
                            nc.vector.tensor_tensor(gt[:, b, T1:NTOK], sg[:, b, T1:NTOK], bank[b][:, 2, T2:2 * T2],
                                                    ALU.mult).then_inc(taken[b], 1)
                            dv.wait_ge(g_hi_ready, done + 1)
                            nc.vector.tensor_tensor(g_lo[:, bass.ds(q * 2 + b, 1), :], gt[:, b:b + 1, :],
                                                    g_hi[:, bass.ds(q * 2 + b, 1), :].bitcast(F32), ALU.subtract)\
                                .then_inc(g_lo_ready, 1)
                    add_pairs(l, at + n, l * X_UPD + (X_IN + (0, 4 * KT)[j] + f * KT), 2 * j,
                              l * 3 + 1 + 2 * j if f == 2 else None)
                    if f < len(jobs):
                        job = jobs[f]
                        modulation(l * JOBS + (job + 1), (job + 1) % JOBS, l * (JOBS * step) + job * step)

            zero_acc(0)
            dv.wait_ge(cond_ready, 1)
            for k in range(KT):
                for j in range(JOB_PARTS - 1):
                    dv.wait_ge(first_in[k % 2 * JOB_PARTS + j], k // 2 * 16 + 16)
                    if k >= 1:
                        dv.wait_ge(first_dv, (k - 1) * (JOB_PARTS - 1) + (j + 1))
                    cols = slice(j * 1024, (j + 1) * 1024)
                    for g in range(2):
                        ins = nc.vector.scalar_tensor_tensor(ada_acc[:, g, cols], ada_w0[:, k % 2, cols], cond[:, k, g:g + 1],
                                                             ada_acc[:, g, cols], ALU.mult, ALU.add)
                    ins.then_inc(first_dv, 1)
            modulation(0, 0, (DEPTH * JOBS - 1) * (JOB_T + KT))
            dv.sem_inc(ada_step, JOB_PARTS * (KT + 1))
            for p in range(KT // 2):
                sum_squares(0, p)
            with dv.Fori(0, DEPTH) as l:
                norm(l, 0)
                ffn(l, F1, 0, (0, 1))
                norm(l, 1)
                dv.wait_ge(par_in, l * 16 + 16)
                settle(dv)
                nc.vector.tensor_scalar(small[:, 73:74], par[:, P_GQK:P_GQK + 1], HD_A ** -0.5, None, ALU.mult)\
                    .then_inc(gq, 1)
                settle(dv)
                with dv.Fori(0, INA_PAIRS // 2) as q:
                    for b in range(2):
                        dv.wait_ge(strip_done[1], q * 2 + filled(l, INA + b))
                        for s in range(2):
                            dst = by_column(qkv[:, bass.ds(q * 4 + (2 * b + s), 1), 0:NLAT].rearrange("p a n -> p (a n)"))
                            end = s * T2 + NLAT - T1
                            nc.vector.tensor_copy(dst[:, 0:R1, :], by_row(bank[b][:, s, 0:T1]))
                            nc.vector.tensor_copy(dst[:, R1:ROWS, :], by_row(bank[b][:, 2, s * T2:end]))
                        nc.vector.tensor_copy(qkv[:, bass.ds(q * 4 + 2 * b, 2), NLAT:NTOK],
                                              piece2(b)[:, :, NLAT - T1:T2]).then_inc(taken[b], 1)
                dv.wait_ge(gq, l + 1)

                def q_norm(t):
                    dv.wait_ge(q_rms_done, l * 8 + t + 1)
                    g, out = small[:, 73:74] if t < 4 else par[:, P_GQK + 1:P_GQK + 2], q_rms_out(t)
                    nc.vector.scalar_tensor_tensor(qkv[:, t, 0:T1], qkv[:, t, 0:T1], g, out[0], ALU.mult, ALU.mult)
                    nc.vector.scalar_tensor_tensor(qkv[:, t, T1:NTOK], qkv[:, t, T1:NTOK], g, out[1], ALU.mult, ALU.mult)\
                        .then_inc(qk_normed, 1)

                for t in range(3):
                    q_norm(t)
                gr = slice(0, FROW + ROWP)
                dv.wait_ge(strip_done[0], l * SPLITS[0] + INB + 2)
                nc.vector.tensor_scalar(row_gate[gr, 0:T1], pb[gr, 0, 0:T1], par[gr, P_BG:P_BG + 1], None, ALU.add)\
                    .then_inc(gate_taken, 1)
                nc.vector.tensor_scalar(row_gate[gr, T1:NTOK], pb[gr, 2, 0:T2], par[gr, P_BG:P_BG + 1], None, ALU.add)\
                    .then_inc(gate_taken, 1)
                for t in range(3, 8):
                    q_norm(t)
                for u in range(NUNIT + 2):
                    n = l * NUNIT + u
                    if u < NUNIT:
                        h, qb = u // CH, u % CH
                        if qb == 0:
                            dv.wait_ge(bias_in[h % 2], (l * 4 + h // 2) * 16 + 16)
                        dv.wait_ge(s_done, n + 1)
                        if u >= 2:
                            dv.wait_ge(p_ready, n - 1)
                        lo, kind = (0, QB_KIND[qb]) if qb < LCH else (WIN, 0)
                        settle(dv)
                        nc.vector.tensor_tensor_reduce(s_neg[:, u % 2, lo:384], pa[:, u % 2, lo:384],
                                                       bias[:, 3 * (h % 2) + kind, lo:384], -1.0, 3.0e38,
                                                       ALU.add, ALU.min, stat[:, 0, u:u + 1]).then_inc(s_taken, 1)
                    if 1 <= u <= NUNIT:
                        dv.wait_ge(p_ready, n)
                        nc.vector.reciprocal(stat[:, 2, u - 1:u], stat[:, 1, u - 1:u]).then_inc(rinv_ready, 1)
                    if u >= 2:
                        v = u - 2
                        if v == 0:
                            dv.wait_ge(kv_out, l * 32 + 32)
                        dv.wait_ge(pv_done, n - 1)
                        dv.wait_ge(rinv_ready, n - 1)
                        nc.vector.tensor_scalar(att[:, v % CH, (v // CH) * HD_A:(v // CH + 1) * HD_A],
                                                pb[:, 1 + v % 2, 0:HD_A], stat[:, 2, v:v + 1], None, ALU.mult)\
                            .then_inc(att_ready, 1)
                for c in range(CH):
                    dv.wait_ge(at_hi, l * CH + c + 1)
                    src, dst = at_views(g_lo, c)
                    nc.vector.tensor_tensor(dst, src, at_views(g_hi, c)[1].bitcast(F32), ALU.subtract).then_inc(at_lo, 1)
                with dv.Fori(0, INB_PAIRS // 2) as q:
                    for b in range(2):
                        dv.wait_ge(strip_done[1], q * 2 + filled(l, INB + b))
                        nc.vector.tensor_copy(qkv[:, bass.ds(q * 4 + 2 * b, 2), 0:T1], piece1(b))
                        nc.vector.tensor_copy(qkv[:, bass.ds(q * 4 + 2 * b, 2), T1:NTOK], piece2(b)).then_inc(taken[b], 1)
                dv.wait_ge(rope_in, l * 16 + 16)
                for t in range(8):
                    r, sc = l * 24 + 3 * t, 1.0 if t < 4 else HD_B ** -0.5
                    dv.wait_ge(rot_done, l * 8 + t + 1)
                    if t >= 2:
                        dv.wait_ge(rope_step, r - 3)
                    nc.vector.scalar_tensor_tensor(rtmp[:, t % 2, :], pa[:, t % 2, :], sc, sin, ALU.mult, ALU.mult)\
                        .then_inc(rope_step, 1)
                    if t == 0:
                        dv.wait_ge(taken[0], fills(l, YA - 2) + 1)
                        dv.wait_ge(taken[1], fills(l, YA - 1) + 1)
                    nc.vector.scalar_tensor_tensor(qkv[:, t, :], qkv[:, t, :], sc, cos, ALU.mult, ALU.mult)\
                        .then_inc(rope_step, 1)
                    dv.wait_ge(rope_step, r + 2)
                    nc.vector.tensor_tensor(qkv[:, t, 0:NLAT], qkv[:, t, 0:NLAT], rtmp[:, t % 2, :], ALU.add)\
                        .then_inc(rope_step, 1)
                dv.wait_ge(rope_step, l * 24 + 24)
                at = [l * ROW_STEPS]

                def step(ins):
                    ins.then_inc(row_step, 1)
                    at[0] = at[0] + 1
                    dv.wait_ge(row_step, at[0])

                fr, r0, rb = slice(FROW, FROW + ROWP), slice(0, ROWP), slice(32, ROWP)
                v = nc.vector
                step(v.scalar_tensor_tensor(row_exp[fr, :], row_gate[fr, :], -1.0, row_gate[fr, :], ALU.mult, ALU.max))
                v.memset(v_aug[:, :, :, HD_B:VW], 1.0).then_inc(ones_set, 1)
                for c in range(CH):
                    dv.wait_ge(kt_done, l * CH + c + 1)
                    v.tensor_copy(k_tok[:, c, :], (pa[:, 2, :], pb[:, 0, :])[c % 2]).then_inc(kt_taken, 1)
                dv.wait_ge(row_act, l * 2 + 2)
                step(v.scalar_tensor_tensor(row_lf[r0, :], row_gate[fr, :], 0.0, row_exp[fr, :], ALU.min, ALU.subtract))
                step(v.tensor_tensor_scan(row_b[r0, :], reset[r0, :], row_lf[r0, :], 0.0, ALU.mult, ALU.add))
                step(v.tensor_tensor_scan(row_b[rb, NTOK - 1::-1], reset[rb, NTOK - 1::-1], row_lf[rb, NTOK - 1::-1],
                                          0.0, ALU.mult, ALU.add))
                m0 = par[:, P_M0:P_M0 + 1]
                step(v.tensor_tensor_scan(row_m[r0, 0:NLAT], row_lf[r0, 0:NLAT], row_gate[r0, 0:NLAT], m0[r0], ALU.add, ALU.max))
                step(v.tensor_tensor_scan(row_m[r0, NLAT:NTOK], row_lf[r0, NLAT:NTOK], row_gate[r0, NLAT:NTOK], 0.0,
                                          ALU.add, ALU.max))
                step(v.tensor_tensor_scan(row_m[rb, NLAT - 1::-1], row_lf[rb, NLAT - 1::-1], row_gate[rb, NLAT - 1::-1],
                                          m0[rb], ALU.add, ALU.max))
                step(v.tensor_tensor_scan(row_m[rb, NTOK - 1:NLAT - 1:-1], row_lf[rb, NTOK - 1:NLAT - 1:-1],
                                          row_gate[rb, NTOK - 1:NLAT - 1:-1], 0.0, ALU.add, ALU.max))
                step(v.tensor_tensor(row_m_rel[r0, :], row_m[r0, :], row_b[r0, :], ALU.subtract))
                step(v.tensor_tensor(row_g[r0, :], row_gate[r0, :], row_b[r0, :], ALU.subtract))
                step(v.tensor_copy(mprev[r0, 0:1], m0[r0]))
                step(v.tensor_copy(mprev[r0, 1:LCH], row_m[r0, P - 1:(LCH - 1) * P:P]))
                step(v.memset(mprev[r0, LCH:CH], 0.0))
                step(v.tensor_copy(mprev[rb, 0:LCH - 1], row_m[rb, P:(LCH - 1) * P + 1:P]))
                step(v.tensor_copy(mprev[rb, LCH - 1:LCH], m0[rb]))

                def chunks(ap):
                    return ap.rearrange("p (c t) -> p c t", t=P)

                step(v.tensor_tensor(chunks(row_a[r0, :]), mprev[r0, 0:CH, None].broadcast_to([ROWP, CH, P]),
                                     chunks(row_m_rel[r0, :]), ALU.subtract))
                step(v.tensor_tensor(chunks(row_w[r0, :]), chunks(row_g[r0, :]),
                                     chunks(row_m_rel[r0, :])[:, :, P - 1:P].broadcast_to([ROWP, CH, P]), ALU.subtract))
                step(v.tensor_tensor(chunks(row_w[rb, :]), chunks(row_g[rb, :]),
                                     chunks(row_m_rel[rb, :])[:, :, 0:1].broadcast_to([ROWP - 32, CH, P]), ALU.subtract))
                dv.wait_ge(kt_taken, l * CH + CH)
                dv.wait_ge(cols_ready, l * 5 + 5)

                def ya(n):
                    dv.wait_ge(strip_done[1], filled(l, YA + n))
                    dv.wait_ge(ga_done, l * KT + n + 1)
                    v.tensor_tensor(y(n)[:, 0:T1], y(n)[:, 0:T1], pb[:, 1, 0:T1], ALU.mult)
                    v.tensor_tensor(y(n)[:, T1:NTOK], y(n)[:, T1:NTOK], pb[:, 2, T2:2 * T2], ALU.mult)\
                        .then_inc(taken[(YA + n) % 2], 1)

                for n in range(2 * H_B):
                    h, back, g, r = n // 2, n % 2, l * 8 + n, row_of(n)
                    order = range(LCH) if back == 0 else range(LCH - 1, -1, -1)
                    rest = 1 - back
                    mk = mask[:, back:back + 1, :]
                    if n >= 1:
                        ya(n - 1)
                    dv.wait_ge(mb_done, g + 1)
                    if n >= 1:
                        dv.wait_ge(st_ready, g * 2)
                    v.tensor_tensor(chunks(wt[:, 0:NLAT]), chunks(pa[:, 2, :]), mk.broadcast_to([P, LCH, P]), ALU.add)\
                        .then_inc(mb_taken, 1)
                    v.tensor_tensor(wt[:, NLAT:NTOK], pa[:, 1, P:2 * P], mask[:, back, :], ALU.add).then_inc(mb_taken, 1)
                    if n >= 1:
                        dv.wait_ge(upd_done, g)
                    v.tensor_tensor(kw, k_tok[:, :, h * P:(h + 1) * P],
                                    gcols[:, 2, :, r:r + 1].broadcast_to([P, CH, P]), ALU.mult).then_inc(kw_ready, 1)
                    dv.wait_ge(upd_done, g + 1)
                    dv.wait_ge(c_in[n % 2], (l * 4 + n // 2) * 16 + 16)
                    for j in range(3):
                        if j >= 1:
                            dv.wait_ge(c_step, g * 3 + j)
                        v.scalar_tensor_tensor(c_seq[n % 2][:, j + 1, :], c_seq[n % 2][:, j, :], dec[:, n, order[j]:order[j] + 1],
                                               m1[:, j * VW:(j + 1) * VW], ALU.mult, ALU.add).then_inc(c_step, 1)
                    dv.wait_ge(wt_ready, (g + 1) * CH)
                    dv.wait_ge(kq_done, l * 4 + h + 1)
                    if n >= 1:
                        dv.wait_ge(intra_done, g)
                    v.tensor_tensor(st[:, 0:NLAT], wt[:, 0:NLAT], pa[:, 0, :], ALU.mult).then_inc(st_ready, 1)
                    v.tensor_tensor(st[:, NLAT:NTOK], wt[:, NLAT:NTOK], pa[:, 1, 0:P], ALU.mult).then_inc(st_ready, 1)
                    s0 = steps_before(l, n)
                    dv.wait_ge(intra_done, g + 1)
                    dv.wait_ge(inter_done, g + 1)
                    if n >= 1:
                        dv.wait_ge(num_step, s0)
                    c0 = order[0]
                    v.tensor_tensor(num[:, rest:rest + 3, :], pa[:, 2, 0:3 * VW].rearrange("p (c d) -> p c d", d=VW),
                                    gcols[:, 1, rest:rest + 3, r:r + 1].broadcast_to([P, 3, VW]), ALU.mult).then_inc(num_step, 1)
                    v.tensor_scalar(num[:, c0, :], pa[:, 1, 2 * P:2 * P + VW], gcols[:, 1, c0, r:r + 1], None, ALU.mult)\
                        .then_inc(num_step, 1)
                    dv.wait_ge(num_step, s0 + 2)
                    v.tensor_tensor(num[:, 0:3, :], num[:, 0:3, :], m1[:, 0:3 * VW].rearrange("p (c d) -> p c d", d=VW),
                                    ALU.add).then_inc(num_step, 1)
                    v.tensor_tensor(num[:, 3, :], num[:, 3, :], m2[:, 0:VW], ALU.add).then_inc(num_step, 1)
                    v.tensor_copy(num[:, LCH, :], m2[:, VW:2 * VW]).then_inc(num_step, 1)
                    if n >= 2:
                        dv.wait_ge(cout_out[n % 2], (l * H_B + n // 2) * 16)
                    else:
                        dv.wait_ge(ones_set, l + 1)
                    v.tensor_copy(c_out[:, n % 2, :], m2[:, 2 * VW:3 * VW]).then_inc(cout_ready, 1)
                    dv.wait_ge(num_step, s0 + 5)
                    v.scalar_tensor_tensor(den, num[:, :, HD_B], -1.0, gcols[:, 3, :, r], ALU.mult, ALU.max)\
                        .then_inc(num_step, 1)
                    dv.wait_ge(num_step, s0 + 6)
                    v.tensor_tensor(den, den, num[:, :, HD_B], ALU.max).then_inc(num_step, 1)
                    dv.wait_ge(num_step, s0 + 7)
                    v.reciprocal(den, den).then_inc(num_step, 1)
                    dv.wait_ge(num_step, s0 + 8)
                    out = hb[:, :, h * P:(h + 1) * P] if back == 0 else hnum[:, :, 0:HD_B]
                    if n == 0:
                        dv.wait_ge(m_out, l * 32 + 32)
                    v.tensor_tensor(out, num[:, :, 0:HD_B], den[:, :, None].broadcast_to([P, CH, HD_B]), ALU.mult)\
                        .then_inc(num_step, 1)
                    if back:
                        dv.wait_ge(num_step, s0 + 9)
                        hh = hb[:, :, h * P:(h + 1) * P]
                        v.tensor_tensor(hh, hh, out, ALU.add).then_inc(num_step, 1)
                ya(2 * H_B - 1)
                dv.wait_ge(num_step, l * NUM_STEPS + NUM_STEPS)
                v.tensor_tensor(hsq, hb, hb, ALU.mult).then_inc(hb_step, 1)
                dv.wait_ge(hb_step, l * 3 + 1)
                v.tensor_reduce(hss, pool[:, 10260:12820].rearrange("p (a b) -> p a b", b=P), AX_X, ALU.add)\
                    .then_inc(hb_step, 1)
                dv.wait_ge(hb_act, l * 2 + 2)
                hb20 = pool[:, 12820:15380].rearrange("p (a b) -> p a b", b=P)
                v.tensor_tensor(hb20, hb20, hss[:, :, None].broadcast_to([P, CH * H_B, P]), ALU.mult).then_inc(hb_step, 1)
                dv.wait_ge(hb_step, l * 3 + 3)

                def h_low(c):
                    dv.wait_ge(ht_hi, l * CH + c + 1)
                    v.tensor_tensor(b_lo[:, :, c * P:(c + 1) * P], hbt[:, c % 2, :].rearrange("p (f t) -> p f t", f=4),
                                    b_hi[:, :, c * P:(c + 1) * P].bitcast(F32), ALU.subtract).then_inc(ht_lo, 1)

                dv.wait_ge(ob_done, l * 6 + 6)
                for c in range(CH):
                    dv.wait_ge(ht_done, l * CH + c + 1)
                    if c >= 2:
                        dv.wait_ge(ht_lo, l * CH + c - 1)
                    v.tensor_tensor(hbt[:, c % 2, :].rearrange("p (f t) -> p f t", f=4),
                                    (m1, m2)[c % 2][:, 0:512].rearrange("p (f t) -> p f t", f=4),
                                    ob_sig[:, :, c * P:(c + 1) * P], ALU.mult).then_inc(ht_prod, 1)
                    if c >= 1:
                        h_low(c - 1)
                h_low(CH - 1)
                for half, mem in enumerate((g_hi32, g_lo32)):
                    settle(dv)
                    with dv.Fori(0, 2) as q:
                        for b in range(2):
                            at, ys = half * 4 + b, mem[:, bass.ds(q * 2 + (4 + b), 1), :]
                            dv.wait_ge(strip_done[1], q * 2 + filled(l, YB + at))
                            dv.wait_ge(br_done, q * 2 + (l * KT + (at + 1)))
                            dv.wait_ge(ty_step, (q * 2 + l * KT) * 2 + (2 * at + 1))
                            v.tensor_tensor(ty[:, b, 0:T1], bank[b][:, 1, 0:T1], br_sig[:, b, 0:T1], ALU.mult).then_inc(ty_step, 1)
                            v.tensor_tensor(ty[:, b, T1:NTOK], bank[b][:, 2, T2:2 * T2], br_sig[:, b, T1:NTOK], ALU.mult)\
                                .then_inc(taken[b], 1)
                            dv.wait_ge(taken[b], q + (fills(l, YB + at) + 1))
                            v.tensor_tensor(ys, ys, ty[:, b:b + 1, :], ALU.add).then_inc(ty_step, 1)
                for k in range(KT):
                    dv.wait_ge(h_hi_ready, l * H_TILES + 2 * KT + k + 1)
                    v.tensor_tensor(h_lo[:, k, :], y(k), h_hi[:, k, :].bitcast(F32), ALU.subtract).then_inc(h_lo_ready, 1)
                add_pairs(l, OS, l * X_UPD + (X_IN + 3 * KT), 1, l * 3 + 2)
                norm(l, 2)
                ffn(l, F2, 1, (2,))


def kernel(x_prompt, x_sample, cache_k, cache_v, state_C, state_n, state_m, c, c_ctx,
           w_ada, b_ada, g_norm, w_up1, w_dn1, w_in, b_gates, g_qn, g_kn, rpb, g_hn,
           w_pa, w_pb, w_o, w_up2, w_dn2):
    import numpy as np
    import concourse.bacc as bacc
    from concourse.bass_utils import run_bass_kernel_spmd

    A = np.asarray
    f32 = np.float32

    def strips(w):
        w = A(w)
        l, k, n = w.shape
        return w.reshape(l, k // P, P, n // P, P).transpose(0, 3, 2, 1, 4).reshape(l, n // P, P, k)

    def columns(v, tiles):
        v = A(v)
        return v.reshape(v.shape[0], -1, tiles, P).transpose(0, 3, 1, 2).reshape(v.shape[0], P, -1)

    def interleave(a, b):
        return np.stack([a, b], axis=2).reshape(a.shape[0], -1, *a.shape[2:])

    def up(w):
        s = strips(w)
        return interleave(s[:, :D_FF // P], s[:, D_FF // P:])

    def down(w):
        w, out, r = A(w), [], 0
        for n in FF_PARTS:
            out.append(strips(w[:, r:r + n * P]))
            r += n * P
        return np.concatenate(out[:2], axis=1), out[2]

    win = A(w_in)
    aw, bw = 3 * H_A * HD_A, 4 * H_B * HD_B
    s_main, s_br = strips(win[:, :, :aw + bw]), strips(win[:, :, aw + bw + 4 * H_B:])
    w_in_s = np.concatenate([s_main, s_br], axis=1)
    gate_at = [(0, 0), (FROW, 1), (32, 2), (FROW + 32, 3)]
    wg = np.zeros((DEPTH, D_MODEL, P), f32)
    for to, j in gate_at:
        wg[:, :, to:to + H_B] = win[:, :, aw + bw + j * H_B:aw + bw + (j + 1) * H_B]
    par = np.zeros((DEPTH, P, N_PAR), f32)
    par[:, :, P_GQK] = np.tile(A(g_qn), (1, 2))
    par[:, :, P_GQK + 1] = np.tile(A(g_kn), (1, 2))
    par[:, :, P_GHN:P_BG] = columns(g_hn, H_B)
    for to, j in gate_at:
        par[:, to:to + H_B, P_BG] = A(b_gates)[:, j * H_B:(j + 1) * H_B]
    par[:, 0:H_B, P_M0] = A(state_m)[0, :, 0]
    par[:, 32:32 + H_B, P_M0] = A(state_m)[0, :, 1]

    ba = A(b_ada).reshape(DEPTH * JOBS, JOB_T, P)
    gn = A(g_norm).reshape(DEPTH * JOBS, KT, P)
    job_par = np.roll(np.concatenate([ba, gn], axis=1), -1, axis=0).reshape(-1, P).T
    ada = A(w_ada).reshape(DEPTH, KT, P, JOBS, JOB_W).transpose(0, 3, 1, 2, 4).reshape(DEPTH * JOBS, KT, P, JOB_W)
    ada = np.roll(ada, -1, axis=0).reshape(-1, P, JOB_W)

    const = np.zeros((P, N_CONST), f32)
    i = np.arange(P)
    const[:, C_ID:C_ID + P] = np.eye(P)
    const[:, C_SEL:C_SEL + P] = (i[None] % 16 == 2 * (i[None] // 16) + i[:, None] // HD_A) / HD_A
    pick = (np.arange(16)[:, None] == np.arange(1024)[None] // HD_A).astype(f32)
    const[:, C_ON:C_ON + P] = 1.0 / D_MODEL
    half = HD_B // 2
    for m in range(half):
        const[m + half, C_ROT + m] = -1.0
        const[m, C_ROT + m + half] = 1.0
    const[:, C_MASK:C_MASK + P] = np.where(i[:, None] <= i[None], 0.0, 1e30)
    const[:, C_MASK + P:C_MASK + 2 * P] = np.where(i[:, None] >= i[None], 0.0, 1e30)
    t = np.arange(NTOK)
    const[:, C_RESET:C_RESET + NTOK] = (t % P != 0)
    const[32:, C_RESET:C_RESET + NTOK] = (t % P != P - 1)
    const[:, C_EPS] = EPS
    const[:, C_ONE] = 1.0
    nf = half // 2
    inv = f32(10000.0) ** (-np.arange(nf, dtype=f32) / f32(nf))
    tl = np.arange(NLAT)
    ang = np.concatenate([(tl // GRID_W).astype(f32)[:, None] * inv, (tl % GRID_W).astype(f32)[:, None] * inv], axis=1)
    rope = np.zeros((P, NTOK + NLAT), f32)
    rope[:, :NLAT] = np.tile(np.cos(ang).T, (2, 1))
    rope[:, NLAT:NTOK] = 1.0
    rope[:, NTOK:] = np.tile(np.sin(ang).T, (2, 1))

    qc, qr = i[:, None] // ROWS, i[:, None] % ROWS
    kc, kr = np.arange(WIN)[None] // ROWS, np.arange(WIN)[None] % ROWS
    rp = A(rpb)
    bias = np.zeros((DEPTH, H_A, P, 3, 3 * P), f32)
    for kind, qb in enumerate((0, 1, 3)):
        cq, ck = qc + 16 * qb, kc + QB_KEY[qb] // ROWS
        start = np.clip(cq - 8, 0, GRID_W - 16)
        ok = (ck >= start) & (ck < start + 16)
        dr, dc = np.broadcast_to(kr - qr + 7, ok.shape), np.clip(ck - cq + 15, 0, 30)
        bias[:, :, :, kind, :WIN] = np.where(ok[None, None], rp[:, :, dr, dc], f32(-1e30))

    ff1, ff1b = down(w_dn1)
    ff2, ff2b = down(w_dn2)
    xs = np.concatenate([A(x_sample)[0], A(x_prompt)[0]], axis=0)
    sc, sn = A(state_C)[0], A(state_n)[0]
    state = np.concatenate([sc.transpose(0, 4, 2, 1, 3), sn.transpose(0, 3, 2, 1)[..., None]], axis=4)
    arrays = {
        "x": xs.T.reshape(KT, P, NTOK).transpose(1, 0, 2),
        "cond": np.stack([A(c)[0].reshape(KT, P).T, A(c_ctx).reshape(KT, P).T], axis=2),
        "const": const, "pick": pick, "rope": rope, "par": par, "bias": bias,
        "cache_k": A(cache_k)[0].reshape(DEPTH, P, 4, P).transpose(0, 3, 2, 1),
        "cache_v": A(cache_v)[0].reshape(DEPTH, P, H_A * HD_A),
        "state_c": state.reshape(DEPTH, P, 2 * H_B, VW),
        "w_ada": ada, "job_par": job_par, "up1": up(w_up1), "dn1a": ff1, "dn1b": ff1b, "wg": strips(wg)[:, 0],
        "w_in": w_in_s, "w_pab": np.concatenate([strips(w_pa), strips(w_pb)], axis=1), "w_o": strips(w_o),
        "up2": up(w_up2), "dn2a": ff2, "dn2b": ff2b,
    }
    outs = {"y": (P, KT, NTOK), "new_k": (DEPTH, P, 4, NCTX), "new_v": (DEPTH, P, 4, NCTX),
            "new_c": (DEPTH, P, 2 * H_B, VW), "new_m": (DEPTH, 2, H_B, 1)}
    nc = bacc.Bacc("TRN2", target_bir_lowering=False, num_devices=1)
    io, feed = {}, {}
    for name, a in arrays.items():
        a = np.ascontiguousarray(a)
        feed[f"in_{name}"] = a
        io[name] = nc.dram_tensor(f"in_{name}", a.shape, F32, kind="ExternalInput").ap()
    for name, shape in outs.items():
        io[name] = nc.dram_tensor(f"out_{name}", shape, F32, kind="ExternalOutput").ap()
    build(nc, io)
    r = run_bass_kernel_spmd(nc, [feed], core_ids=[0]).results[0]
    yt = r["out_y"].transpose(2, 1, 0).reshape(NTOK, D_MODEL)

    def cache(a):
        return a.transpose(0, 3, 2, 1).reshape(1, DEPTH, NCTX, H_A, HD_A)

    nc_ = r["out_new_c"].reshape(DEPTH, P, H_B, 2, VW)
    return (np.ascontiguousarray(yt[NLAT:])[None], np.ascontiguousarray(yt[:NLAT])[None],
            cache(r["out_new_k"]), cache(r["out_new_v"]),
            nc_[..., :HD_B].transpose(0, 3, 2, 4, 1)[None], nc_[..., HD_B].transpose(0, 3, 2, 1)[None],
            r["out_new_m"].reshape(1, DEPTH, 2, H_B))
```

```python
from contextlib import ExitStack

import concourse.bass as bass
from concourse import mybir

F32 = mybir.dt.float32
F32R = mybir.dt.float32r
ACT = mybir.ActivationFunctionType
ALU = mybir.AluOpType
AX_X = mybir.AxisListType.X

P = 128
D_MODEL = 1024
KT = D_MODEL // P
DEPTH = 2
GRID_W = 64
NLAT = 512
NCTX = 128
NTOK = NLAT + NCTX
ROWS = NLAT // GRID_W
H_A, HD_A = 8, 64
H_B, HD_B = 4, 128
D_FF = 2816
N_MOD = 9
EPS = 1e-6
T1 = 384
T2 = NTOK - T1
R1 = T1 // GRID_W
CH = NTOK // P
LCH = NLAT // P
FF_PARTS = (8, 8, 6)
assert sum(FF_PARTS) * P == D_FF
VW = HD_B + 1
ROWP = 36
FROW = 64
QB_KEY = (0, 64, 192, 256)
QB_KIND = (0, 1, 1, 2)
WIN = 256
NUNIT = H_A * CH

C_ID, C_SEL, C_ON, C_ROT, C_MASK, C_RESET = 0, 128, 256, 384, 512, 768
C_EPS = C_RESET + NTOK
N_CONST = C_EPS + 1
P_GQK, P_GHN, P_BG, P_M0 = 0, 2, 6, 7
N_PAR = 8

ROW_STEPS, ROW_ABS, ROW_M = 18, 1, 8
NUM_FWD, NUM_BWD = 9, 10
NUM_STEPS = H_B * (NUM_FWD + NUM_BWD)

JOBS = N_MOD // 3
JOB_W = 3 * D_MODEL
JOB_PARTS = JOB_W // 1024
JOB_T = JOB_W // P
FIRST_ROUNDS = 2 * (JOB_T - JOB_T // JOB_PARTS) // 4
JOB_ROUNDS = 2 * JOB_T // 4
assert JOB_ROUNDS == 3 * (KT // 2)

FFN_PAIRS = D_FF // P + 3 * KT // 2
INA_PAIRS, INB_PAIRS, YA_PAIRS, OB_PAIRS, YB_PAIRS, O_PAIRS = 6, 6, KT, 2, KT, KT // 2
MIX_PAIRS = INA_PAIRS + INB_PAIRS + YA_PAIRS + OB_PAIRS + YB_PAIRS + O_PAIRS
PAIRS = 2 * FFN_PAIRS + MIX_PAIRS
SPLITS = (PAIRS + 1, PAIRS)
BUF = PAIRS // 2
X_UPD = 2 * 3 * KT + KT
X_IN = 16
Y_EARLY = 4
H_TILES = 4 * KT


def build(nc, io):
    with ExitStack() as ctx:
        def sb(name, shape, dt=F32):
            return ctx.enter_context(nc.sbuf_tensor(name, shape, dt))

        def shared(name, shape):
            with nc.sbuf_tensor(name + "32", shape, F32) as scratch:
                pass
            return sb(name, shape, F32R), scratch

        def sem(name):
            return ctx.enter_context(nc.semaphore(name))

        x = sb("x", [P, KT, NTOK])
        h_hi = sb("h_hi", [P, KT, NTOK], F32R)
        h_lo = sb("h_lo", [P, KT, NTOK], F32R)
        g_hi, g_hi32 = shared("g_hi", [P, 8, NTOK])
        g_lo, g_lo32 = shared("g_lo", [P, 8, NTOK])
        w_raw = sb("w_raw", [P, 2, 1024])
        w_hi = sb("w_hi", [P, 2, 1024], F32R)
        w_lo = sb("w_lo", [P, 2, 1024], F32R)
        with nc.sbuf_tensor("b_hi", [P, H_B, NTOK], F32R) as b_hi, nc.sbuf_tensor("b_lo", [P, H_B, NTOK], F32R) as b_lo:
            pass
        pool = sb("pool", [P, 19328])
        const = sb("const", [P, N_CONST])
        par = sb("par", [P, N_PAR])
        cond = sb("cond", [P, KT, 2])
        job_par = sb("job_par", [P, JOBS * DEPTH * (JOB_T + KT)])
        mod = sb("mod", [P, N_MOD * KT, 2])
        sums = sb("sums", [P, 2 * JOB_T])
        mod_a = sb("mod_a", [P, 3, KT, 2])
        gate = sb("gate", [P, 3, KT, 2])
        stat = sb("stat", [P, 3, NUNIT])
        small = sb("small", [P, 80])
        eps = const[:, C_EPS:C_EPS + 1]

        def area(at, *shape):
            n = 1
            for s in shape:
                n *= s
            a = pool[:, at:at + n]
            if len(shape) == 2:
                return a.rearrange("p (a b) -> p a b", b=shape[1])
            if len(shape) == 3:
                return a.rearrange("p (a b c) -> p a b c", b=shape[1], c=shape[2])
            return a

        hx, sq, rstd = area(0, 2, NTOK), area(2 * NTOK, 2, NTOK), area(4 * NTOK, NTOK)
        sg, gt, ssum = area(5 * NTOK, 2, NTOK), area(7 * NTOK, 2, NTOK), area(9 * NTOK, NTOK)
        ada_acc, ada_w = area(6400, 2, JOB_W), area(6400 + 2 * JOB_W, JOB_PARTS, 1024)
        ada_w0 = area(6400 + 2 * JOB_W, 2, JOB_W)
        qkv = area(0, 12, NTOK)
        att = area(8 * NTOK, CH, H_A * HD_A)
        v_tok = area(7680, 8, 512)
        cache_v, cache_k = area(11776, 512), area(12288, 4, P)
        bias = area(12800, 6, 384)
        s_neg, p_att, p_t = area(15104, 2, 384), area(15872, 2, 384), area(16640, 2, 384)
        qsq, qrs = area(15104, 2, NTOK), area(16384, 1024)
        head_pick = area(18304, 1024)
        wt, st, hnum = area(5120, NTOK), area(5760, NTOK), area(6400, CH, VW)
        c_out = area(7045, 2, VW)
        v_aug = area(7680, CH, H_B, VW)
        k_tok = area(10260, CH, 512)
        cos, sin = area(10260, NTOK), area(10900, NLAT)
        hb = area(12820, CH, 512)
        num, kw = area(15380, CH, VW), area(16025, CH, P)
        col = area(16665, 4, CH * ROWP)
        row_gate, row_m_rel = area(17408, NTOK), area(18048, NTOK)
        row_exp, row_lf, row_b, row_m = (area(12820 + i * NTOK, NTOK) for i in range(4))
        row_g, row_a, row_w = area(15380, NTOK), area(16020, NTOK), area(18688, NTOK)
        rtmp = area(12820, 2, NLAT)
        c_seq = [area(17408, LCH, VW), area(18688, LCH, VW)]
        hsq = area(10260, CH, 512)
        ob_sig = area(5120, H_B, NTOK)
        br_sig, ty = area(7680, 2, NTOK), area(8960, 2, NTOK)
        hbt = area(10260, 2, 512)

        ident = const[:, C_ID:C_ID + P]
        head_sel = const[:, C_SEL:C_SEL + P].rearrange("p (t r) -> p t r", r=16)
        mean_ones = const[:, C_ON:C_ON + P]
        rot = const[:, C_ROT:C_ROT + P]
        mask = const[:, C_MASK:C_MASK + 2 * P].rearrange("p (a b) -> p a b", b=P)
        reset = const[:, C_RESET:C_RESET + NTOK]
        mprev, dec = small[:, 0:8], small[:, 8:48].rearrange("p (a b) -> p a b", b=CH)
        hss, den = small[:, 48:68], small[:, 68:73]
        gcols = col.rearrange("p k (c r) -> p k c r", r=ROWP)

        bank = [ctx.enter_context(nc.psum_tensor(f"pair{b}", [P, 3, 512], F32)) for b in range(2)]
        m1 = ctx.enter_context(nc.psum_tensor("m1", [P, 512], F32))
        m2 = ctx.enter_context(nc.psum_tensor("m2", [P, 512], F32))
        pa, pb = bank

        def y(d):
            return (g_hi32 if d < 4 else g_lo32)[:, 4 + d % 4, :]

        def piece1(b):
            return bank[b][:, 0:2, 0:T1]

        def piece2(b):
            return bank[b][:, 2, :].rearrange("p (a b) -> p a b", b=T2)

        def by_column(ap):
            return ap.rearrange("p (c r) -> p r c", r=ROWS)

        def by_row(ap):
            return ap.rearrange("p (r c) -> p r c", c=GRID_W)

        const_in = sem("const_in")
        par_in = sem("par_in")
        x_upd = sem("x_upd")
        landed = [sem("landed0"), sem("landed1")]
        raw_free = [sem("raw_free0"), sem("raw_free1")]
        hi_ready = [sem("hi_ready0"), sem("hi_ready1")]
        lo_ready = [sem("lo_ready0"), sem("lo_ready1")]
        strip_done = [sem("strip_done0"), sem("strip_done1")]
        taken = [sem("taken0"), sem("taken1")]
        cond_ready = sem("cond_ready")
        first_in = [sem(f"first_in{j}") for j in range(2 * JOB_PARTS)]
        ada_in = [sem(f"ada_in{j}") for j in range(JOB_PARTS)]
        first_dv, first_pe = sem("first_dv"), sem("first_pe")
        first_turned, first_summed = sem("first_turned"), sem("first_summed")
        ada_step = sem("ada_step")
        acc_turned, acc_summed = sem("acc_turned"), sem("acc_summed")
        acc_zeroed, mods = sem("acc_zeroed"), sem("mods")
        sq_ready, ssum_step, ms_done = sem("sq_ready"), sem("ssum_step"), sem("ms_done")
        ln_done, rstd_ready = sem("ln_done"), sem("rstd_ready")
        h_scaled, h_hi_ready, h_lo_ready = (sem(s) for s in ("h_scaled", "h_hi_ready", "h_lo_ready"))
        qrs_zeroed = sem("qrs_zeroed")
        ctx_shifted = sem("ctx_shifted")
        h_lo_ctx = sem("h_lo_ctx")
        cache_in, pick_in = sem("cache_in"), sem("pick_in")
        silu_done, g_hi_ready, g_lo_ready = (sem(s) for s in ("silu_done", "g_hi_ready", "g_lo_ready"))
        gate_taken = sem("gate_taken")
        qsq_ready, qss_done, qln_done, qrs_ready = (sem(s) for s in ("qsq_ready", "qss_done", "qln_done", "qrs_ready"))
        q_rms_done, qk_normed = sem("q_rms_done"), sem("qk_normed")
        vt_done, vt_taken = sem("vt_done"), sem("vt_taken")
        bias_in = [sem("bias_in0"), sem("bias_in1")]
        s_done, s_taken, p_ready, pt_done, pt_taken = (sem(s) for s in ("s_done", "s_taken", "p_ready", "pt_done", "pt_taken"))
        pv_done, rinv_ready, att_ready = sem("pv_done"), sem("rinv_ready"), sem("att_ready")
        at_done, at_hi, at_lo = sem("at_done"), sem("at_hi"), sem("at_lo")
        kv_out, rope_in = sem("kv_out"), sem("rope_in")
        gq = sem("gq")
        rot_done, rope_step = sem("rot_done"), sem("rope_step")
        kt_done, kt_taken, va_done, va_taken, ones_set = (sem(s) for s in ("kt_done", "kt_taken", "va_done", "va_taken", "ones_set"))
        row_step, row_act = sem("row_step"), sem("row_act")
        cols_done, cols_ready = sem("cols_done"), sem("cols_ready")
        c_in = [sem("c_in0"), sem("c_in1")]
        kq_done, mb_done, mb_taken, wt_ready, st_ready, kw_ready, upd_done = (sem(s) for s in (
            "kq_done", "mb_done", "mb_taken", "wt_ready", "st_ready", "kw_ready", "upd_done"))
        intra_done, inter_done, c_step, num_step = sem("intra_done"), sem("inter_done"), sem("c_step"), sem("num_step")
        cout_ready, cout_out, m_out = sem("cout_ready"), [sem("cout_out0"), sem("cout_out1")], sem("m_out")
        hb_step, hb_act = sem("hb_step"), sem("hb_act")
        ht_done, ht_prod, ht_hi, ht_lo = (sem(s) for s in ("ht_done", "ht_prod", "ht_hi", "ht_lo"))
        ob_done, ga_done, br_done, ty_step = sem("ob_done"), sem("ga_done"), sem("br_done"), sem("ty_step")
        out_done = sem("out_done")

        F1 = 0
        INA = FFN_PAIRS
        INB = INA + INA_PAIRS
        YA = INB + INB_PAIRS
        OB = YA + YA_PAIRS
        YB = OB + OB_PAIRS
        OS = YB + YB_PAIRS
        F2 = OS + O_PAIRS

        def fills(l, pair):
            return l * BUF + pair // 2 + 1

        def filled(l, pair):
            return l * PAIRS + pair + 2

        def halves(s, l, n, half):
            return l * (2 * SPLITS[s]) + n * 2 + (half + 1)

        def ada_steps(l, j):
            return l * (JOBS * KT) + (j + 1) * KT

        def first_out(r):
            return (bank[0][:, r % 6, :] if r % 6 < 3 else bank[1][:, r % 6 - 3, :]) if r < 6 else \
                (m2[:], bank[0][:, 0, :])[r - 6]

        def q_rms_out(t):
            return (m1[:, 0:T1], m2[:, 0:T2]) if t % 2 == 0 else (pa[:, 0, 0:T1], pa[:, 1, 0:T2])

        def row_of(n):
            return 32 * (n % 2) + n // 2

        def steps_before(l, n):
            return l * NUM_STEPS + (n // 2) * (NUM_FWD + NUM_BWD) + (n % 2) * NUM_FWD

        def at_views(dst, c):
            src = pa[:, c % 2, :]
            if c == LCH:
                return src.rearrange("p (f t) -> p f t", f=4), dst[:, 0:4, NLAT:NTOK]
            w = GRID_W // LCH
            return (src.rearrange("p (f c r) -> p f c r", f=4, r=ROWS),
                    dst[:, 0:4, 0:NLAT].rearrange("p f (r c) -> p f c r", r=ROWS)[:, :, c * w:(c + 1) * w, :])

        settled = sem("settled")

        def settle(eng):
            eng.sem_inc(settled, 1)

        block = ctx.enter_context(nc.Block())

        @block.sync
        def _(sp):
            for s in range(2):
                sp.sem_inc(raw_free[s], 1)

            def load(s, l, use, src):
                sp.wait_ge(raw_free[s], l * SPLITS[s] + use + 1)
                sp.dma_start(w_raw[:, s, 0:src.shape[-1]], src).then_inc(landed[s], 16)

            def stream(l, pairs, use, src):
                with sp.Fori(0, pairs) as i:
                    for s in range(2):
                        load(s, l, use[s] + i, src[l, bass.ds(i * 2 + s, 1), :, :].rearrange("a p n -> p (a n)"))

            def ada(n, at):
                for j in range(JOB_PARTS):
                    sp.wait_ge(ada_step, n * JOB_PARTS + (j + 1))
                    sp.dma_start(ada_w[:, j:j + 1, :], io["w_ada"][bass.ds(at, 1), :, j * 1024:(j + 1) * 1024]
                                 .rearrange("a p n -> p a n")).then_inc(ada_in[j], 16)

            def ffn(l, use, up, dn, dn_last, jobs):
                for f, n in enumerate(FF_PARTS):
                    first = sum(FF_PARTS[:f])
                    part, before = up[:, 2 * first:2 * (first + n)], [u + first + 4 * f for u in use]
                    if f < len(jobs):
                        with sp.Fori(0, KT) as i:
                            for s in range(2):
                                load(s, l, before[s] + i, part[l, bass.ds(i * 2 + s, 1), :, :]
                                     .rearrange("a p n -> p (a n)"))
                            ada(i + ada_steps(l, jobs[f]), i + (l * (JOBS * KT) + jobs[f] * KT))
                    else:
                        stream(l, n, before, part)
                    src = dn[:, f * KT:(f + 1) * KT] if f < 2 else dn_last
                    stream(l, KT // 2, [u + first + n + 4 * f for u in use], src)

            for k in range(KT):
                for j in range(JOB_PARTS):
                    if k >= 2:
                        if j < JOB_PARTS - 1:
                            sp.wait_ge(first_dv, (k - 2) * (JOB_PARTS - 1) + (j + 1))
                        else:
                            sp.wait_ge(first_pe, k - 1)
                    cols = slice(j * 1024, (j + 1) * 1024)
                    sp.dma_start(ada_w0[:, k % 2, cols], io["w_ada"][(DEPTH * JOBS - 1) * KT + k, :, cols]
                                 ).then_inc(first_in[k % 2 * JOB_PARTS + j], 16)
            with sp.Fori(0, DEPTH) as l:
                ffn(l, (0, 0), io["up1"], io["dn1a"], io["dn1b"], (0, 1))
                stream(l, INA_PAIRS, (INA, INA), io["w_in"][:, 0:12])
                load(0, l, INB, io["wg"][bass.ds(l, 1)].rearrange("a p n -> p (a n)"))
                for s in range(2):
                    load(s, l, INB + 1 - s, io["w_in"][bass.ds(l, 1), 12 + s].rearrange("a p n -> p (a n)"))
                sp.wait_ge(h_lo_ready, l * H_TILES + KT + 1)
                sp.wait_ge(mods, l * (3 * JOBS) + 9)
                for h in range(H_A):
                    if h >= 2:
                        sp.wait_ge(s_taken, l * NUNIT + (h - 1) * CH)
                    sp.dma_start(bias[:, 3 * (h % 2):3 * (h % 2) + 3, :],
                                 io["bias"][bass.ds(l, 1), h].rearrange("a p k n -> p (a k) n")
                                 ).then_inc(bias_in[h % 2], 16)
                with sp.Fori(1, INB_PAIRS) as i:
                    for s in range(2):
                        load(s, l, INB + 1 - s + i,
                             io["w_in"][l, bass.ds(i * 2 + 12 + s, 1), :, :].rearrange("a p n -> p (a n)"))

                def gated(first, gate_strips, out_strips):
                    with sp.Fori(0, KT) as d:
                        load(0, l, d + (first + 1), io["w_in"][l, bass.ds(d + gate_strips, 1), :, :].rearrange("a p n -> p (a n)"))
                        load(1, l, d + first, io["w_pab"][l, bass.ds(d + out_strips, 1), :, :].rearrange("a p n -> p (a n)"))

                gated(YA, 28, 0)
                stream(l, OB_PAIRS, (OB + 1, OB), io["w_in"][:, 24:28])
                gated(YB, 28 + KT, KT)
                stream(l, O_PAIRS, (OS + 1, OS), io["w_o"])
                sp.wait_ge(ht_lo, (l + 1) * CH)
                settle(sp)
                ffn(l, (F2 + 1, F2), io["up2"], io["dn2a"], io["dn2b"], (2,))
            sp.wait_ge(x_upd, X_IN + DEPTH * X_UPD)
            sp.dma_start(io["y"], x[:]).then_inc(out_done, 16)
            sp.wait_ge(out_done, 16)
            sp.wait_ge(kv_out, DEPTH * 32)
            for j in range(2):
                sp.wait_ge(cout_out[j], DEPTH * H_B * 16)
            sp.wait_ge(m_out, DEPTH * 32)

        @block.gpsimd
        def _(po):
            def split_lo(s, l, n):
                for half in range(2):
                    w = slice(half * 512, (half + 1) * 512)
                    po.wait_ge(hi_ready[s], halves(s, l, n, half))
                    nc.gpsimd.tensor_tensor(w_lo[:, s, w], w_raw[:, s, w], w_hi[:, s, w].bitcast(F32),
                                            ALU.subtract).then_inc(lo_ready[s], 1)
                po.wait_ge(lo_ready[s], halves(s, l, n, 1))
                po.sem_inc(raw_free[s], 1)

            def norm(l, i):
                n, m = (l * 3 + i) * KT, l * H_TILES + (0, KT, 3 * KT)[i]
                for k in range(KT):
                    po.wait_ge(h_hi_ready, m + k + 1)
                    settle(po)
                    z = hx[:, k % 2, NLAT:NTOK]
                    nc.gpsimd.tensor_scalar(z, z, mod[:, 3 * i * KT + k, 1:2], None, ALU.add).then_inc(ctx_shifted, 1)
                    po.wait_ge(ctx_shifted, n + (k + 1))
                    nc.gpsimd.tensor_tensor(h_lo[:, k, NLAT:NTOK], z, h_hi[:, k, NLAT:NTOK].bitcast(F32),
                                            ALU.subtract).then_inc(h_lo_ctx, 1)

            for k in range(1, KT):
                po.wait_ge(sq_ready, k + 1)
                if k >= 2:
                    po.wait_ge(ssum_step, k - 1)
                nc.gpsimd.tensor_tensor(ssum, ssum, sq[:, k % 2, :], ALU.add).then_inc(ssum_step, 1)
            with po.Fori(0, DEPTH) as l:
                for s in range(2):
                    split_lo(s, l, 0)
                norm(l, 0)
                with po.Fori(1, INA + 1) as i:
                    for s in range(2):
                        split_lo(s, l, i)
                norm(l, 1)
                with po.Fori(INA + 1, INB) as i:
                    for s in range(2):
                        split_lo(s, l, i)
                split_lo(0, l, INB)
                po.wait_ge(qk_normed, (l + 1) * 8)
                settle(po)
                po.dma_start(io["new_k"][bass.ds(l, 1)].rearrange("a p f t -> p (a f) t"),
                             qkv[:, 4:8, NLAT:NTOK]).then_inc(kv_out, 16)
                po.wait_ge(taken[1], fills(l, INB - 1) + 1)
                settle(po)
                po.dma_start(io["new_v"][bass.ds(l, 1)].rearrange("a p f t -> p (a f) t"),
                             qkv[:, 8:12, NLAT:NTOK]).then_inc(kv_out, 16)
                for s in range(2):
                    split_lo(s, l, INB + 1 - s)
                po.wait_ge(at_done, (l + 1) * CH)
                settle(po)
                po.dma_start(pool[:, 10260:10260 + NTOK + NLAT], io["rope"]).then_inc(rope_in, 16)
                with po.Fori(1, INB_PAIRS) as i:
                    for s in range(2):
                        split_lo(s, l, i + INB + 1 - s)
                for s in range(2):
                    split_lo(s, l, YA + 1 - s)
                po.wait_ge(row_step, l * ROW_STEPS + ROW_M)
                settle(po)
                po.dma_start(io["new_m"][bass.ds(l, 1), 0].rearrange("a h o -> (a h) o"),
                             row_m[0:H_B, NTOK - 1:NTOK]).then_inc(m_out, 16)
                po.dma_start(io["new_m"][bass.ds(l, 1), 1].rearrange("a h o -> (a h) o"),
                             row_m[32:32 + H_B, NLAT:NLAT + 1]).then_inc(m_out, 16)
                po.wait_ge(cols_done, (l + 1) * 2)
                po.wait_ge(row_step, (l + 1) * ROW_STEPS)

                def load_state(n):
                    settle(po)
                    po.dma_start(c_seq[n % 2][:, 0:1, :], io["state_c"][bass.ds(l, 1), :, n, :]
                                 .rearrange("a p n -> p a n")).then_inc(c_in[n % 2], 16)

                def store_state(n):
                    po.wait_ge(cout_ready, l * 8 + n + 1)
                    settle(po)
                    po.dma_start(io["new_c"][bass.ds(l, 1), :, n, :].rearrange("a p n -> p a n"),
                                 c_out[:, n % 2:n % 2 + 1, :]).then_inc(cout_out[n % 2], 16)

                load_state(0)
                load_state(1)
                for n in range(2 * H_B):
                    if 1 <= n < 2 * H_B - 1:
                        po.wait_ge(inter_done, l * 8 + n)
                        load_state(n + 1)
                    if n >= 1:
                        store_state(n - 1)
                    for s in range(2):
                        split_lo(s, l, YA + n + 2 - s)
                store_state(2 * H_B - 1)
                with po.Fori(OB + 1, F2 + 1) as i:
                    for s in range(2):
                        split_lo(s, l, i + (1 - s))
                norm(l, 2)
                with po.Fori(F2 + 1, PAIRS) as i:
                    for s in range(2):
                        split_lo(s, l, i + (1 - s))

        @block.scalar
        def _(ac):
            ac.dma_start(const[:], io["const"]).then_inc(const_in, 16)
            ac.dma_start(cond[:], io["cond"]).then_inc(const_in, 16)
            ac.dma_start(job_par[:], io["job_par"]).then_inc(const_in, 16)
            ac.dma_start(x[:], io["x"]).then_inc(x_upd, X_IN)
            for s in range(2):
                ac.sem_inc(strip_done[s], 1)
                ac.sem_inc(taken[s], 1)
            ac.wait_ge(const_in, 48)
            nc.scalar.activation(cond[:], cond[:], ACT.Silu).then_inc(cond_ready, 1)

            def split_hi(s, l, n):
                ac.wait_ge(strip_done[s], l * SPLITS[s] + n + 1)
                ac.wait_ge(landed[s], (l * SPLITS[s] + n) * 16 + 16)
                for half in range(2):
                    w = slice(half * 512, (half + 1) * 512)
                    nc.scalar.activation(w_hi[:, s, w], w_raw[:, s, w], ACT.Copy).then_inc(hi_ready[s], 1)

            def squares(n, done, pair):
                for k in (2 * pair, 2 * pair + 1):
                    if done is not None:
                        ac.wait_ge(x_upd, done + (k + 1))
                    if k >= 3:
                        ac.wait_ge(ssum_step, n * (KT - 1) + (k - 2))
                    nc.scalar.activation(sq[:, k % 2, :] if k else ssum, x[:, k, :], ACT.Square).then_inc(sq_ready, 1)

            def norm(l, i):
                n = l * 3 + i
                ac.wait_ge(ms_done, n + 1)
                nc.scalar.activation(rstd[:, 0:T1], m1[:, 0:T1], ACT.Ln, bias=eps).then_inc(ln_done, 1)
                nc.scalar.activation(rstd[:, T1:NTOK], m2[:, 0:T2], ACT.Ln, bias=eps).then_inc(ln_done, 1)
                ac.wait_ge(ln_done, n * 2 + 2)
                nc.scalar.activation(rstd, rstd, ACT.Exp, scale=-0.5).then_inc(rstd_ready, 1)
                for k in range(KT):
                    ac.wait_ge(h_scaled, n * KT + (k + 1))
                    for g, cols in ((0, slice(0, NLAT)), (1, slice(NLAT, NTOK))):
                        ins = nc.scalar.activation(h_hi[:, k, cols], hx[:, k % 2, cols], ACT.Identity,
                                                   bias=mod[:, 3 * i * KT + k, g:g + 1])
                    ins.then_inc(h_hi_ready, 1)

            def last_pairs(l, at, n, done, next_splits=True):
                for i in range(KT // 2):
                    if i < KT // 2 - 1 or next_splits:
                        for s in range(2):
                            split_hi(s, l, at[s] + i)
                    squares(n, done, i)

            def ffn(l, base, split, j, last):
                for f, n in enumerate(FF_PARTS):
                    first = sum(FF_PARTS[:f])
                    at = base + first + 4 * f
                    with ac.Fori(0, n // 2) as q:
                        for b in range(2):
                            for s in range(2):
                                split_hi(s, l, q * 2 + (at + b + 1 + (split if s == 0 else 0)))
                            ac.wait_ge(strip_done[1], q * 2 + filled(l, at + b))
                            nc.scalar.activation(sg[:, b, 0:T1], bank[b][:, 0, 0:T1], ACT.Silu)
                            nc.scalar.activation(sg[:, b, T1:NTOK], bank[b][:, 2, 0:T2], ACT.Silu)\
                                .then_inc(silu_done, 1)
                            ac.wait_ge(taken[b], q + (fills(l, at + b) + 1))
                            nc.scalar.activation(g_hi[:, bass.ds(q * 2 + b, 1), :],
                                                 gt[:, b:b + 1, :], ACT.Copy).then_inc(g_hi_ready, 1)
                    at += n
                    if f < 2:
                        with ac.Fori(0, KT // 2) as i:
                            for s in range(2):
                                split_hi(s, l, i + (at + 1 + (split if s == 0 else 0)))
                    else:
                        last_pairs(l, (at + 1 + split, at + 1), l * 3 + 1 + 2 * j,
                                   l * X_UPD + X_IN + (2, 6)[j] * KT, not last)

            def q_squares(l, pair):
                ac.wait_ge(taken[pair % 2], fills(l, INA + pair) + 1)
                for t in (2 * pair, 2 * pair + 1):
                    if t >= 2:
                        ac.wait_ge(qss_done, l * 8 + (t - 1))
                    nc.scalar.activation(qsq[:, t % 2, :], qkv[:, t, :], ACT.Square).then_inc(qsq_ready, 1)

            def q_rs(l):
                ac.wait_ge(qss_done, l * 8 + 8)
                ac.wait_ge(qrs_zeroed, l + 1)
                nc.scalar.activation(qrs[0:16, 0:T1], m1[0:16, 0:T1], ACT.Ln, bias=eps[0:16]).then_inc(qln_done, 1)
                nc.scalar.activation(qrs[0:16, T1:NTOK], m2[0:16, 0:T2], ACT.Ln, bias=eps[0:16]).then_inc(qln_done, 1)
                ac.wait_ge(qln_done, l * 2 + 2)
                nc.scalar.activation(qrs[0:16, 0:NTOK], qrs[0:16, 0:NTOK], ACT.Exp, scale=-0.5).then_inc(qrs_ready, 1)

            ac.wait_ge(x_upd, X_IN)
            for p in range(KT // 2):
                squares(0, None, p)
            with ac.Fori(0, DEPTH) as l:
                ac.wait_ge(x_upd, l * X_UPD + X_IN)
                ac.dma_start(par[:], io["par"][bass.ds(l, 1)].rearrange("a p n -> p (a n)")).then_inc(par_in, 16)
                for s in range(2):
                    split_hi(s, l, 0)
                norm(l, 0)
                ffn(l, F1, 0, 0, False)
                norm(l, 1)
                ac.wait_ge(mods, l * (3 * JOBS) + 9)
                ac.dma_start(head_pick, io["pick"]).then_inc(pick_in, 16)
                ac.dma_start(cache_v, io["cache_v"][bass.ds(l, 1)].rearrange("a p n -> p (a n)")).then_inc(cache_in, 16)
                ac.dma_start(cache_k, io["cache_k"][bass.ds(l, 1)].rearrange("a p f n -> p (a f) n")).then_inc(cache_in, 16)
                for i in range(INA_PAIRS):
                    for s in range(2):
                        split_hi(s, l, INA + 1 + i)
                    if i < 4:
                        q_squares(l, i)
                    if i == 4:
                        q_rs(l)
                split_hi(0, l, INB + 1)
                for i in range(8):
                    ac.wait_ge(vt_done, l * 8 + i + 1)
                    nc.scalar.activation(v_tok[:, i, :], (pa if i % 2 == 0 else pb)[:, 2, :], ACT.Copy)\
                        .then_inc(vt_taken, 1)
                for u in range(NUNIT + 1):
                    n = l * NUNIT + u
                    if u < NUNIT:
                        lo, hi = (0, 384) if u % CH < LCH else (WIN, 384)
                        ac.wait_ge(s_taken, n + 1)
                        if u >= 2:
                            ac.wait_ge(pt_done, n - 1)
                        nc.scalar.activation(p_att[:, u % 2, lo:hi], s_neg[:, u % 2, lo:hi], ACT.Exp, scale=-1.0,
                                             bias=stat[:, 0, u:u + 1], accum_out=stat[:, 1, u:u + 1])\
                            .then_inc(p_ready, 1)
                    if u >= 1:
                        v = u - 1
                        lo, hi = (0, 384) if v % CH < LCH else (WIN, 384)
                        ac.wait_ge(pt_done, n)
                        if v >= 2:
                            ac.wait_ge(pv_done, n - 2)
                        src = (pa[:, 2, :], pb[:, 0, :])[v % 2]
                        nc.scalar.activation(p_t[:, v % 2, lo:hi], src[:, lo:hi], ACT.Copy).then_inc(pt_taken, 1)
                for c in range(CH):
                    ac.wait_ge(at_done, l * CH + c + 1)
                    src, dst = at_views(g_hi, c)
                    nc.scalar.activation(dst, src, ACT.Copy).then_inc(at_hi, 1)
                fr = slice(FROW, FROW + ROWP)
                ac.wait_ge(row_step, l * ROW_STEPS + ROW_ABS)
                nc.scalar.activation(row_exp[fr, :], row_exp[fr, :], ACT.Exp, scale=-1.0).then_inc(row_act, 1)
                ac.wait_ge(row_act, l * 2 + 1)
                nc.scalar.activation(row_exp[fr, :], row_exp[fr, :], ACT.Ln, bias=1.0).then_inc(row_act, 1)
                for i in range(INB_PAIRS - 1):
                    for s in range(2):
                        split_hi(s, l, INB + i + 1 + 1 - s)
                split_hi(0, l, YA + 1)
                ac.wait_ge(cols_done, l * 2 + 2)
                nc.scalar.activation(col[:, 0, :], m1[:, 0:180], ACT.Copy).then_inc(cols_ready, 1)
                nc.scalar.activation(col[:, 1, :], m1[:, 180:360], ACT.Exp).then_inc(cols_ready, 1)
                nc.scalar.activation(small[:, 8:48], m1[:, 360:400], ACT.Exp).then_inc(cols_ready, 1)
                nc.scalar.activation(col[:, 2, :], m2[:, 0:180], ACT.Exp).then_inc(cols_ready, 1)
                nc.scalar.activation(col[:, 3, :], m2[:, 180:360], ACT.Exp, scale=-1.0).then_inc(cols_ready, 1)
                split_hi(1, l, YA)
                for c in range(CH):
                    ac.wait_ge(va_done, l * CH + c + 1)
                    nc.scalar.activation(v_aug[:, c, :, 0:HD_B], (pb[:, 1, :], pb[:, 2, :])[c % 2]
                                         .rearrange("p (h d) -> p h d", h=H_B), ACT.Copy).then_inc(va_taken, 1)
                ac.wait_ge(cols_ready, l * 5 + 5)
                for n in range(2 * H_B):
                    h, back = n // 2, n % 2
                    ac.wait_ge(mb_taken, (l * 8 + n + 1) * 2)
                    for c in range(CH):
                        nc.scalar.activation(wt[:, c * P:(c + 1) * P], wt[:, c * P:(c + 1) * P], ACT.Exp, scale=-1.0,
                                             bias=gcols[:, 0, c, 32 * back + h:32 * back + h + 1]).then_inc(wt_ready, 1)
                    ac.wait_ge(strip_done[0], l * SPLITS[0] + (YA + n + 3))
                    nc.scalar.activation(y(n)[:, 0:T1], pb[:, 0, 0:T1], ACT.Sigmoid)
                    nc.scalar.activation(y(n)[:, T1:NTOK], pb[:, 2, 0:T2], ACT.Sigmoid).then_inc(ga_done, 1)
                    for s in range(2):
                        split_hi(s, l, YA + n + 1 + 1 - s)
                ac.wait_ge(hb_step, l * 3 + 2)
                nc.scalar.activation(hss, hss, ACT.Ln, scale=1.0 / HD_B, bias=eps).then_inc(hb_act, 1)
                ac.wait_ge(hb_act, l * 2 + 1)
                nc.scalar.activation(hss, hss, ACT.Exp, scale=-0.5).then_inc(hb_act, 1)
                for j in range(2):
                    ac.wait_ge(cout_out[j], (l + 1) * H_B * 16)
                for p in range(OB_PAIRS):
                    for s in range(2):
                        split_hi(s, l, OB + p + 1 + 1 - s)
                    ac.wait_ge(strip_done[1], filled(l, OB + p))
                    nc.scalar.activation(ob_sig[:, 2 * p:2 * p + 2, 0:T1], piece1(p), ACT.Sigmoid).then_inc(ob_done, 1)
                    nc.scalar.activation(ob_sig[:, 2 * p:2 * p + 2, T1:NTOK], piece2(p), ACT.Sigmoid)\
                        .then_inc(taken[p], 1)
                    ac.wait_ge(taken[p], fills(l, OB + p) + 1)
                    for t in range(2 * p, 2 * p + 2):
                        nc.scalar.activation(ob_sig[:, t, :], ob_sig[:, t, :], ACT.Copy,
                                             scale=par[:, P_GHN + t:P_GHN + t + 1]).then_inc(ob_done, 1)
                for c in range(CH):
                    ac.wait_ge(ht_prod, l * CH + c + 1)
                    nc.scalar.activation(b_hi[:, :, c * P:(c + 1) * P],
                                         hbt[:, c % 2, :].rearrange("p (f t) -> p f t", f=4), ACT.Copy).then_inc(ht_hi, 1)
                def y_hi(k):
                    nc.scalar.activation(h_hi[:, k, :], y(k), ACT.Copy).then_inc(h_hi_ready, 1)

                def yb(q, b, last=False):
                    split_hi(0, l, q * 2 + (YB + b + 2))
                    if last:
                        ac.wait_ge(ty_step, (l * KT + Y_EARLY) * 2 + 1)
                        for k in range(Y_EARLY):
                            y_hi(k)
                        split_hi(1, l, q * 2 + (YB + b + 1))
                    ac.wait_ge(strip_done[1], q * 2 + filled(l, YB + b))
                    ac.wait_ge(ty_step, (q * 2 + l * KT) * 2 + (2 * b + 1))
                    nc.scalar.activation(br_sig[:, b, 0:T1], bank[b][:, 0, 0:T1], ACT.Sigmoid)
                    nc.scalar.activation(br_sig[:, b, T1:NTOK], bank[b][:, 2, 0:T2], ACT.Sigmoid).then_inc(br_done, 1)
                    if not last:
                        split_hi(1, l, q * 2 + (YB + b + 1))

                with ac.Fori(0, KT // 2 - 1) as q:
                    for b in range(2):
                        yb(q, b)
                yb(KT // 2 - 1, 0)
                yb(KT // 2 - 1, 1, True)
                for k in range(Y_EARLY, KT):
                    ac.wait_ge(ty_step, (l * KT + k + 1) * 2 + 1)
                    y_hi(k)
                last_pairs(l, (OS + 2, OS + 1), l * 3 + 2, l * X_UPD + X_IN + 3 * KT)
                norm(l, 2)
                ffn(l, F2, 1, 1, True)


        @block.tensor
        def _(pe):
            def passes(s, k, t, out1, out2, xh, xl, begin, end, shared=False):
                w = slice(k * P, (k + 1) * P)
                for j, (a, b) in enumerate(((w_hi, xh), (w_hi, xl), (w_lo, xh))):
                    first, last = begin and j == 0, end and j == 2
                    nc.tensor.matmul(out1, a[:, s, w], b[:, t, 0:T1], start=first, stop=last)
                    mm = nc.tensor.matmul(out2, a[:, s, w], b[:, t, T1:NTOK], start=first and not (shared and s == 1),
                                          stop=last and not (shared and s == 0))
                return mm

            def strip(s, l, n, out1, out2, xh, xl, tiles, g_ready=None):
                pe.wait_ge(lo_ready[s], halves(s, l, n, 0))
                for k, t in enumerate(tiles):
                    if k == 4:
                        pe.wait_ge(lo_ready[s], halves(s, l, n, 1))
                    if g_ready is not None and k == len(tiles) - 1:
                        pe.wait_ge(g_lo_ready, g_ready)
                    mm = passes(s, k, t, out1, out2, xh, xl, k == 0, k == len(tiles) - 1)
                mm.then_inc(strip_done[s], 1)

            def pair(l, at, pos, xh, xl, tiles, ready=None, extra=0, q=0, tiles1=None, g_ready=None, between=None,
                     norms=None):
                b = at % 2
                pe.wait_ge(taken[b], q + fills(l, at))
                out = [(bank[b][:, s, 0:T1], bank[b][:, 2, s * T2:(s + 1) * T2]) for s in range(2)]
                before = [q * 2 + (at + (extra if s == 0 else 0)) for s in range(2)]
                if ready is None:
                    for s in range(2):
                        strip(s, l, before[s], *out[s], xh, xl, tiles1 if s and tiles1 else tiles,
                              g_ready if s == 0 else None)
                        if between:
                            between(s)
                    return
                for s in range(2):
                    pe.wait_ge(lo_ready[s], halves(s, l, before[s], 0))
                for k in tiles:
                    for s in range(2) if k == 4 else ():
                        pe.wait_ge(lo_ready[s], halves(s, l, before[s], 1))
                    pe.wait_ge(h_lo_ready, ready + (k + 1))
                    if norms is not None:
                        pe.wait_ge(h_lo_ctx, norms * KT + (k + 1))
                    for s in range(2):
                        mm = passes(s, k, k, *out[s], xh, xl, k == 0, k == len(tiles) - 1, True)
                        if k == len(tiles) - 1:
                            mm.then_inc(strip_done[s], 1)

            def pairs(l, at, count, xh, xl, tiles, ready=None, extra=0, g_ready=None, norms=None):
                settle(pe)
                if ready is not None:
                    for b in range(2):
                        pair(l, at + b, b, xh, xl, tiles, None if b else ready, extra, norms=norms)
                with pe.Fori(0 if ready is None else 1, count // 2) as q:
                    for b in range(2):
                        pair(l, at + b, b, xh, xl, tiles, None, extra, q, g_ready=g_ready)

            def norm(l, i):
                n = l * 3 + i
                pe.wait_ge(taken[0], fills(l, (F1, INA, F2)[i]))
                settle(pe)
                pe.wait_ge(ssum_step, n * (KT - 1) + (KT - 1))
                nc.tensor.matmul(m1[:, 0:T1], mean_ones, ssum[:, 0:T1], start=True, stop=True)
                nc.tensor.matmul(m2[:, 0:T2], mean_ones, ssum[:, T1:NTOK], start=True, stop=True).then_inc(ms_done, 1)

            def turn_sums(job, r):
                if r == 0:
                    pe.wait_ge(ada_step, job * (KT * JOB_PARTS) + (2 * KT * JOB_PARTS + JOB_PARTS))
                    settle(pe)
                if r >= 2:
                    pe.wait_ge(acc_summed, job * JOB_ROUNDS + (r - 1))
                for t in range(4):
                    g, at = divmod(4 * r + t, JOB_T)
                    mm = nc.tensor.transpose((m1, m2)[r % 2][:, t * P:(t + 1) * P], ada_acc[:, g, at * P:(at + 1) * P], ident)
                mm.then_inc(acc_turned, 1)

            def ffn(l, base, extra, j, jobs):
                for f, n in enumerate(FF_PARTS):
                    at = base + sum(FF_PARTS[:f]) + 4 * f
                    pairs(l, at, n, h_hi, h_lo, range(KT), None if f else l * H_TILES + (0, 3 * KT)[j], extra,
                          norms=l * 3 + 2 * j)
                    g_ready = (l * 2 + j) * (D_FF // P) + sum(FF_PARTS[:f + 1]) + 2
                    pe.wait_ge(g_lo_ready, g_ready - 1)
                    if f >= len(jobs):
                        pairs(l, at + n, KT // 2, g_hi, g_lo, range(n), None, extra, g_ready)
                        continue
                    job = l * JOBS + jobs[f]
                    if jobs[f] == 1:
                        pe.wait_ge(acc_summed, job * JOB_ROUNDS)
                    for p in range(KT // 2):
                        def turns(s):
                            for r in ((3 * p,), (3 * p + 1, 3 * p + 2))[s]:
                                turn_sums(job, r)
                        pair(l, at + n + p, p % 2, g_hi, g_lo, range(n), None, extra, g_ready=g_ready if p == 0 else None,
                             between=turns)

            pe.wait_ge(const_in, 48)
            pe.wait_ge(cond_ready, 1)
            j, tiles = JOB_PARTS - 1, JOB_T // JOB_PARTS
            for k in range(KT):
                pe.wait_ge(first_in[k % 2 * JOB_PARTS + j], k // 2 * 16 + 16)
                for t in range(tiles):
                    at = j * tiles + t
                    mm = nc.tensor.matmul(m1[:, 2 * at:2 * at + 2], ada_w0[:, k % 2, at * P:(at + 1) * P], cond[:, k, :],
                                          start=k == 0 and t == 0, stop=k == KT - 1 and t == tiles - 1)
                mm.then_inc(first_pe, 1)
            pe.wait_ge(first_dv, KT * (JOB_PARTS - 1))
            for r in range(FIRST_ROUNDS):
                g, first = divmod(4 * r, j * tiles)
                if r == 7:
                    pe.wait_ge(first_summed, 1)
                for t in range(4):
                    mm = nc.tensor.transpose(first_out(r)[:, t * P:(t + 1) * P],
                                             ada_acc[:, g, (first + t) * P:(first + t + 1) * P], ident)
                mm.then_inc(first_turned, 1)
            with pe.Fori(0, DEPTH) as l:
                pe.wait_ge(mods, l * (3 * JOBS) + 3)
                norm(l, 0)
                ffn(l, F1, 0, 0, (0, 1))
                pe.wait_ge(mods, l * (3 * JOBS) + 9)
                norm(l, 1)
                settle(pe)
                for i in range(INA_PAIRS):
                    pair(l, INA + i, i % 2, h_hi, h_lo, range(KT), l * H_TILES + KT if i == 0 else None,
                         norms=l * 3 + 1)
                    for t in range(2 * (i - 1), 2 * i) if 1 <= i <= 4 else ():
                        pe.wait_ge(qsq_ready, l * 8 + t + 1)
                        nc.tensor.matmul(m1[0:16, 0:T1], head_sel[:, t, :], qsq[:, t % 2, 0:T1], start=t == 0, stop=t == 7)
                        nc.tensor.matmul(m2[0:16, 0:T2], head_sel[:, t, :], qsq[:, t % 2, T1:NTOK],
                                         start=t == 0, stop=t == 7).then_inc(qss_done, 1)

                def q_rms(t):
                    if t >= 2:
                        pe.wait_ge(qk_normed, l * 8 + (t - 1))
                    pick, out = head_pick[:, t * P:(t + 1) * P], q_rms_out(t)
                    nc.tensor.matmul(out[0], pick, qrs[:, 0:T1], start=True, stop=True)
                    nc.tensor.matmul(out[1], pick, qrs[:, T1:NTOK], start=True, stop=True).then_inc(q_rms_done, 1)

                pe.wait_ge(qrs_ready, l + 1)
                pe.wait_ge(pick_in, l * 16 + 16)
                pe.wait_ge(taken[0], fills(l, INB - 2) + 1)
                settle(pe)
                q_rms(0)
                q_rms(1)
                pe.wait_ge(taken[1], fills(l, INB - 1) + 1)
                strip(0, l, INB, pb[:, 0, 0:T1], pb[:, 2, 0:T2], h_hi, h_lo, range(KT))
                for i in range(8):
                    if i < 6:
                        q_rms(i + 2)
                    if i == 1:
                        pe.wait_ge(gate_taken, l * 2 + 2)
                    if i >= 2:
                        pe.wait_ge(vt_taken, l * 8 + i - 1)
                    t0 = 64 * i if i < 7 else NLAT
                    for f in range(4):
                        mm = nc.tensor.transpose((pa if i % 2 == 0 else pb)[:, 2, f * P:(f + 1) * P],
                                                 qkv[:, 8 + f, t0:t0 + P], ident)
                    mm.then_inc(vt_done, 1)
                pe.wait_ge(qk_normed, l * 8 + 8)
                pe.wait_ge(cache_in, l * 32 + 32)

                def scores(u):
                    h, qb = u // CH, u % CH
                    n, hp = l * NUNIT + u, slice(64 * (h % 2), 64 * (h % 2) + 64)
                    if u >= 2:
                        pe.wait_ge(s_taken, n - 1)
                    out = pa[:, u % 2, :]
                    q = qkv[hp, h // 2, qb * P:(qb + 1) * P]
                    if qb < LCH:
                        nc.tensor.matmul(out[:, 0:WIN], q, qkv[hp, 4 + h // 2, QB_KEY[qb]:QB_KEY[qb] + WIN],
                                         start=True, stop=True)
                    k = cache_k[hp, h // 2, :] if qb < LCH else qkv[hp, 4 + h // 2, NLAT:NTOK]
                    nc.tensor.matmul(out[:, WIN:384], q, k, start=True, stop=True).then_inc(s_done, 1)

                def parts(u):
                    return range(3) if u % CH < LCH else range(2, 3)

                def turn(u):
                    n = l * NUNIT + u
                    pe.wait_ge(p_ready, n + 1)
                    if u == 0:
                        pe.wait_ge(vt_taken, l * 8 + 8)
                    if u >= 2:
                        pe.wait_ge(pt_taken, n - 1)
                    out = (pa[:, 2, :], pb[:, 0, :])[u % 2]
                    for j in parts(u):
                        mm = nc.tensor.transpose(out[:, j * P:(j + 1) * P], p_att[:, u % 2, j * P:(j + 1) * P], ident)
                    mm.then_inc(pt_done, 1)

                def weighted(u):
                    h, qb, n = u // CH, u % CH, l * NUNIT + u
                    pe.wait_ge(pt_taken, n + 1)
                    if u >= 2:
                        pe.wait_ge(att_ready, n - 1)
                    hd = slice(h * HD_A, (h + 1) * HD_A)
                    w = QB_KEY[qb] // 64 if qb < LCH else 0
                    values = (v_tok[:, w, hd], v_tok[:, w + 2, hd], cache_v[:, hd] if qb < LCH else v_tok[:, 7, hd])
                    js = list(parts(u))
                    for j in js:
                        mm = nc.tensor.matmul(pb[:, 1 + u % 2, 0:HD_A], p_t[:, u % 2, j * P:(j + 1) * P], values[j],
                                              start=j == js[0], stop=j == js[-1])
                    mm.then_inc(pv_done, 1)

                for u in range(NUNIT + 2):
                    if u < NUNIT:
                        scores(u)
                    if 1 <= u <= NUNIT:
                        turn(u - 1)
                    if u >= 2:
                        weighted(u - 2)
                pe.wait_ge(att_ready, l * NUNIT + NUNIT)
                for c in range(CH):
                    if c >= 2:
                        pe.wait_ge(at_lo, l * CH + c - 1)
                    for f in range(4):
                        mm = nc.tensor.transpose(pa[:, c % 2, f * P:(f + 1) * P], att[:, c, f * P:(f + 1) * P], ident)
                    mm.then_inc(at_done, 1)
                pe.wait_ge(at_lo, l * CH + CH)
                def rotate(t):
                    pe.wait_ge(taken[(t // 2) % 2], fills(l, INB + t // 2) + 1)
                    if t >= 2:
                        pe.wait_ge(rope_step, l * 24 + 3 * (t - 2) + 1)
                    nc.tensor.matmul((m1, m2)[t % 2][:], rot, qkv[:, t, 0:NLAT], start=True, stop=True)\
                        .then_inc(rot_done, 1)

                def gate_columns():
                    for t in (6, 7):
                        pe.wait_ge(rope_step, l * 24 + 3 * t + 1)
                    pe.wait_ge(row_step, l * ROW_STEPS + ROW_STEPS)
                    settle(pe)
                    for out, pairs_ in ((m1, (row_g, row_a)), (m2, (row_w, row_m))):
                        for j, r in enumerate(pairs_):
                            for c in range(CH):
                                at = (j * CH + c) * ROWP
                                mm = nc.tensor.transpose(out[:, at:at + ROWP], r[rows, c * P:(c + 1) * P],
                                                         ident[rows, 0:ROWP])
                        if out is m1:
                            for n in range(2 * H_B):
                                e = P - 1 if n % 2 == 0 else 0
                                pick = ident[rows, row_of(n):row_of(n) + 1].broadcast_to([ROWP, P])
                                ends = row_a[rows, :].rearrange("p (c t) -> p c t", t=P)[:, :, e]
                                mm = nc.tensor.matmul(m1[:, 360 + n * CH:360 + (n + 1) * CH], pick, ends, start=True, stop=True)
                        mm.then_inc(cols_done, 1)
                rows = slice(0, ROWP)
                settle(pe)
                for i in range(INB_PAIRS):
                    def beside(s):
                        if 0 <= 2 * (i - 1) + s < 8:
                            rotate(2 * (i - 1) + s)
                        if (i, s) == (INB_PAIRS - 1, 0):
                            gate_columns()
                    pair(l, INB + i, i % 2, h_hi, h_lo, range(KT), None, 1, between=beside)
                pe.wait_ge(taken[0], fills(l, YA - 2) + 1)
                pe.wait_ge(taken[1], fills(l, YA - 1) + 1)
                pe.wait_ge(rope_step, l * 24 + 24)
                for c in range(CH):
                    if c >= 2:
                        pe.wait_ge(kt_taken, l * CH + c - 1)
                    for h in range(H_B):
                        mm = nc.tensor.transpose((pa[:, 2, :], pb[:, 0, :])[c % 2][:, h * P:(h + 1) * P],
                                                 qkv[:, 4 + h, c * P:(c + 1) * P], ident)
                    mm.then_inc(kt_done, 1)
                for c in range(CH):
                    if c >= 2:
                        pe.wait_ge(va_taken, l * CH + c - 1)
                    for h in range(H_B):
                        mm = nc.tensor.transpose((pb[:, 1, :], pb[:, 2, :])[c % 2][:, h * P:(h + 1) * P],
                                                 qkv[:, 8 + h, c * P:(c + 1) * P], ident)
                    mm.then_inc(va_done, 1)
                pe.wait_ge(kt_taken, l * CH + CH)
                pe.wait_ge(va_taken, l * CH + CH)
                pe.wait_ge(ones_set, l + 1)
                pe.wait_ge(cols_ready, l * 5 + 5)
                def ya_gate(n, ks):
                    at = YA + n
                    if ks[0] == 0:
                        pe.wait_ge(lo_ready[0], halves(0, l, at + 1, 0))
                        if n >= 1:
                            pe.wait_ge(taken[(at - 1) % 2], fills(l, at - 1) + 1)
                        settle(pe)
                    else:
                        pe.wait_ge(lo_ready[0], halves(0, l, at + 1, 1))
                    for k in ks:
                        mm = passes(0, k, k, pb[:, 0, 0:T1], pb[:, 2, 0:T2], h_hi, h_lo, k == 0, k == KT - 1)
                    if ks[-1] == KT - 1:
                        mm.then_inc(strip_done[0], 1)

                def ya_out(n):
                    pe.wait_ge(ga_done, l * KT + n + 1)
                    strip(1, l, YA + n, pb[:, 1, 0:T1], pb[:, 2, T2:2 * T2], g_hi, g_lo, range(4))

                inter = pa[:, 2, 0:3 * VW]
                for n in range(2 * H_B):
                    h, g = n // 2, l * 8 + n
                    order = range(LCH) if n % 2 == 0 else range(LCH - 1, -1, -1)
                    rest = 1 if n % 2 == 0 else 0
                    if n >= 1:
                        pe.wait_ge(num_step, steps_before(l, n - 1) + 5)
                        pe.wait_ge(cout_ready, g)
                    if n % 2 == 0:
                        for c in range(CH):
                            cc = slice(c * P, (c + 1) * P)
                            out = pa[:, 0, cc] if c < LCH else pa[:, 1, 0:P]
                            mm = nc.tensor.matmul(out, qkv[:, 4 + h, cc], qkv[:, h, cc], start=True, stop=True)
                        mm.then_inc(kq_done, 1)
                    pick = ident[rows, row_of(n):row_of(n) + 1].broadcast_to([ROWP, P])
                    nc.tensor.matmul(pa[:, 2, :], pick, row_m_rel[rows, 0:NLAT], start=True, stop=True)
                    nc.tensor.matmul(pa[:, 1, P:2 * P], pick, row_m_rel[rows, NLAT:NTOK], start=True, stop=True)\
                        .then_inc(mb_done, 1)
                    ya_gate(n, range(0, KT // 2))
                    pe.wait_ge(kw_ready, g + 1)
                    for j, c in enumerate(order[0:3]):
                        nc.tensor.matmul(m1[:, j * VW:(j + 1) * VW], kw[:, c, :], v_aug[:, c, h, :], start=True, stop=True)
                    nc.tensor.matmul(m2[:, 2 * VW:3 * VW], kw[:, LCH, :], v_aug[:, LCH, h, :], start=True, stop=True)\
                        .then_inc(upd_done, 1)
                    ya_gate(n, range(KT // 2, KT))
                    pe.wait_ge(mb_taken, g * 2 + 2)
                    pe.wait_ge(c_step, g * 3 + 3)
                    pe.wait_ge(st_ready, g * 2 + 2)
                    for c in range(CH):
                        out = m1[:, c * VW:(c + 1) * VW] if c < 3 else m2[:, (c - 3) * VW:(c - 2) * VW]
                        mm = nc.tensor.matmul(out, st[:, c * P:(c + 1) * P], v_aug[:, c, h, :], start=True, stop=True)
                    mm.then_inc(intra_done, 1)
                    pe.wait_ge(c_in[n % 2], (l * 4 + n // 2) * 16 + 16)
                    for j in range(LCH):
                        c = order[j]
                        out = inter[:, (c - rest) * VW:(c - rest + 1) * VW] if j else pa[:, 1, 2 * P:2 * P + VW]
                        mm = nc.tensor.matmul(out, qkv[:, h, c * P:(c + 1) * P], c_seq[n % 2][:, j, :], start=True, stop=True)
                    mm.then_inc(inter_done, 1)
                    ya_out(n)
                pe.wait_ge(num_step, l * NUM_STEPS + NUM_STEPS)
                pe.wait_ge(cout_ready, l * 8 + 8)
                for p in range(OB_PAIRS):
                    pair(l, OB + p, p, h_hi, h_lo, range(KT), None, 1)
                def yb_gate(q, b):
                    pe.wait_ge(taken[b], q + fills(l, YB + b))
                    strip(0, l, q * 2 + (YB + b + 1), bank[b][:, 0, 0:T1], bank[b][:, 2, 0:T2], h_hi, h_lo, range(KT))

                def yb_out(q, b):
                    strip(1, l, q * 2 + (YB + b), bank[b][:, 1, 0:T1], bank[b][:, 2, T2:2 * T2], b_hi, b_lo, range(4))

                yb_gate(0, 0)
                pe.wait_ge(hb_step, l * 3 + 3)
                for c in range(CH):
                    if c >= 2:
                        pe.wait_ge(ht_prod, l * CH + c - 1)
                    for f in range(H_B):
                        mm = nc.tensor.transpose((m1, m2)[c % 2][:, f * P:(f + 1) * P], hb[:, c, f * P:(f + 1) * P], ident)
                    mm.then_inc(ht_done, 1)
                pe.wait_ge(ht_lo, l * CH + CH)
                yb_out(0, 0)
                yb_gate(0, 1)
                yb_out(0, 1)
                with pe.Fori(1, KT // 2) as q:
                    for b in range(2):
                        yb_gate(q, b)
                        yb_out(q, b)
                pairs(l, OS, O_PAIRS, h_hi, h_lo, range(KT), l * H_TILES + 2 * KT, 1)
                norm(l, 2)
                ffn(l, F2, 1, 1, (2,))

        @block.vector
        def _(dv):
            dv.sem_inc(g_lo_ready, 2)
            dv.sem_inc(ty_step, 1)
            dv.wait_ge(const_in, 48)

            def norm(l, i):
                n, m = (l * 3 + i) * KT, l * H_TILES + (0, KT, 3 * KT)[i]
                both = ((0, slice(0, NLAT)), (1, slice(NLAT, NTOK)))
                dv.wait_ge(rstd_ready, l * 3 + i + 1)

                def low(k):
                    dv.wait_ge(h_hi_ready, m + k + 1)
                    nc.vector.scalar_tensor_tensor(h_lo[:, k, 0:NLAT], hx[:, k % 2, 0:NLAT], mod[:, 3 * i * KT + k, 0:1],
                                                   h_hi[:, k, 0:NLAT].bitcast(F32), ALU.add, ALU.subtract)\
                        .then_inc(h_lo_ready, 1)

                for k in range(KT):
                    if k >= 2:
                        dv.wait_ge(h_lo_ready, m + k - 1)
                        dv.wait_ge(h_lo_ctx, n + k - 1)
                    for g, cols in both:
                        ins = nc.vector.scalar_tensor_tensor(hx[:, k % 2, cols], x[:, k, cols], mod_a[:, i, k, g:g + 1],
                                                             rstd[:, cols], ALU.mult, ALU.mult)
                    ins.then_inc(h_scaled, 1)
                    if k >= 1:
                        low(k - 1)
                low(KT - 1)

            def sum_squares(n, pair):
                for k in (2 * pair, 2 * pair + 1):
                    if k == 0:
                        continue
                    dv.wait_ge(sq_ready, n * KT + (k + 1))
                    if k >= 2:
                        dv.wait_ge(ssum_step, n * (KT - 1) + (k - 1))
                    nc.vector.tensor_tensor(ssum, ssum, sq[:, k % 2, :], ALU.add).then_inc(ssum_step, 1)

            def zero_acc(job):
                nc.vector.memset(ada_acc, 0.0).then_inc(acc_zeroed, 1)
                dv.wait_ge(acc_zeroed, job + 1)

            def ada(n, k):
                for j in range(JOB_PARTS):
                    dv.wait_ge(ada_in[j], n * 16 + (16 - 16 * KT))
                    dv.wait_ge(ada_step, n * JOB_PARTS + (j + 1))
                    for g in range(2):
                        cols = slice(j * 1024, (j + 1) * 1024)
                        ins = nc.vector.scalar_tensor_tensor(ada_acc[:, g:g + 1, cols], ada_w[:, j:j + 1, :],
                                                             cond[:, bass.ds(k, 1), g:g + 1].rearrange("p a b -> p (a b)"),
                                                             ada_acc[:, g:g + 1, cols], ALU.mult, ALU.add)
                    ins.then_inc(ada_step, 1)

            def add_turned(job, r):
                dv.wait_ge(acc_turned, job * JOB_ROUNDS + (r + 1))
                nc.vector.tensor_reduce(sums[:, 4 * r:4 * r + 4], (m1, m2)[r % 2][:].rearrange("p (a b) -> p a b", b=P),
                                        AX_X, ALU.add).then_inc(acc_summed, 1)

            def modulation(job, i, at, source):
                nc.vector.tensor_tensor(mod[:, i * JOB_T:(i + 1) * JOB_T, :], source,
                                        job_par[:, bass.ds(at, JOB_T), None].broadcast_to([P, JOB_T, 2]),
                                        ALU.add).then_inc(mods, 1)
                dv.wait_ge(mods, job * 3 + 1)
                nc.vector.scalar_tensor_tensor(
                    mod_a[:, i], mod[:, (3 * i + 1) * KT:(3 * i + 2) * KT, :], 1.0,
                    job_par[:, bass.ds(at + JOB_T, KT), None].broadcast_to([P, KT, 2]), ALU.add, ALU.mult).then_inc(mods, 1)
                nc.vector.tensor_scalar(gate[:, i], mod[:, (3 * i + 2) * KT:(3 * i + 3) * KT, :],
                                        1.0 if i == 1 else 0.5, None, ALU.mult).then_inc(mods, 1)
                dv.wait_ge(mods, job * 3 + 3)

            def add_to_x(l, at, done, which, q=0):
                b = at % 2
                dv.wait_ge(strip_done[1], q * 2 + filled(l, at))
                dv.wait_ge(x_upd, done)
                for s in range(2):
                    t = done_tile(q, b, s)
                    end = s * T2 + NLAT - T1
                    for g, cols, ps in ((0, slice(0, T1), bank[b][:, s:s + 1, 0:T1]),
                                        (0, slice(T1, NLAT), bank[b][:, 2:3, s * T2:end]),
                                        (1, slice(NLAT, NTOK), bank[b][:, 2:3, end:(s + 1) * T2])):
                        ins = nc.vector.scalar_tensor_tensor(x[:, t, cols], ps, gate_at(which, t, g), x[:, t, cols],
                                                             ALU.mult, ALU.add)
                    ins.then_inc(x_upd, 1)
                dv.wait_ge(x_upd, done + 2)
                dv.sem_inc(taken[b], 1)

            def done_tile(q, b, s):
                return bass.ds(q * 4 + (2 * b + s), 1)

            def gate_at(which, t, g):
                return gate[:, which, t, g]

            def add_pairs(l, at, done, which, n=None, job=None):
                if job is not None:
                    for p in range(KT // 2):
                        add_turned(job, 3 * p)
                        add_to_x(l, at + p % 2, done + 2 * p, which, p // 2)
                        add_turned(job, 3 * p + 1)
                        add_turned(job, 3 * p + 2)
                    return
                if n is not None:
                    for p in range(KT // 2):
                        if p >= 1:
                            sum_squares(n, p - 1)
                        add_to_x(l, at + p % 2, done + 2 * p, which, p // 2)
                    sum_squares(n, KT // 2 - 1)
                    return
                settle(dv)
                with dv.Fori(0, KT // 4) as q:
                    for b in range(2):
                        add_to_x(l, at + b, q * 4 + (done + 2 * b), which, q)

            def ffn(l, base, j, jobs):
                step = JOB_T + KT
                for f, n in enumerate(FF_PARTS):
                    first = sum(FF_PARTS[:f])
                    at = base + first + 4 * f
                    if f < len(jobs):
                        zero_acc(l * JOBS + (jobs[f] + 1))
                    settle(dv)
                    with dv.Fori(0, n // 2) as q:
                        for b in range(2):
                            if f < len(jobs):
                                ada(q * 2 + (b + ada_steps(l, jobs[f])), q * 2 + b)
                            done = q * 2 + (l * 2 + j) * (D_FF // P) + (first + b)
                            dv.wait_ge(silu_done, done + 1)
                            dv.wait_ge(g_lo_ready, done + 1)
                            nc.vector.tensor_tensor(gt[:, b, 0:T1], sg[:, b, 0:T1], bank[b][:, 1, 0:T1], ALU.mult)
                            nc.vector.tensor_tensor(gt[:, b, T1:NTOK], sg[:, b, T1:NTOK], bank[b][:, 2, T2:2 * T2],
                                                    ALU.mult).then_inc(taken[b], 1)
                            dv.wait_ge(g_hi_ready, done + 1)
                            nc.vector.tensor_tensor(g_lo[:, bass.ds(q * 2 + b, 1), :], gt[:, b:b + 1, :],
                                                    g_hi[:, bass.ds(q * 2 + b, 1), :].bitcast(F32), ALU.subtract)\
                                .then_inc(g_lo_ready, 1)
                    add_pairs(l, at + n, l * X_UPD + (X_IN + (0, 4 * KT)[j] + f * KT), 2 * j,
                              l * 3 + 1 + 2 * j if f == 2 else None, l * JOBS + jobs[f] if f < len(jobs) else None)
                    if f < len(jobs):
                        job = jobs[f]
                        dv.wait_ge(acc_summed, l * (JOBS * JOB_ROUNDS) + (job + 1) * JOB_ROUNDS)
                        modulation(l * JOBS + (job + 1), (job + 1) % JOBS, l * (JOBS * step) + job * step,
                                   sums[:].rearrange("p (g j) -> p j g", g=2))

            zero_acc(0)
            dv.wait_ge(cond_ready, 1)
            for k in range(KT):
                for j in range(JOB_PARTS - 1):
                    dv.wait_ge(first_in[k % 2 * JOB_PARTS + j], k // 2 * 16 + 16)
                    if k >= 1:
                        dv.wait_ge(first_dv, (k - 1) * (JOB_PARTS - 1) + (j + 1))
                    cols = slice(j * 1024, (j + 1) * 1024)
                    for g in range(2):
                        ins = nc.vector.scalar_tensor_tensor(ada_acc[:, g, cols], ada_w0[:, k % 2, cols], cond[:, k, g:g + 1],
                                                             ada_acc[:, g, cols], ALU.mult, ALU.add)
                    ins.then_inc(first_dv, 1)
            done = JOB_T - JOB_T // JOB_PARTS
            by_cond = sums[:].rearrange("p (g j) -> p g j", g=2)
            for r in range(FIRST_ROUNDS):
                g, first = divmod(4 * r, done)
                dv.wait_ge(first_turned, r + 1)
                nc.vector.tensor_reduce(by_cond[:, g, first:first + 4], first_out(r).rearrange("p (a b) -> p a b", b=P),
                                        AX_X, ALU.add).then_inc(first_summed, 1)
            dv.wait_ge(first_pe, KT)
            nc.vector.tensor_copy(by_cond[:, :, done:JOB_T], m1[:, 2 * done:2 * JOB_T].rearrange("p (j g) -> p g j", g=2))\
                .then_inc(first_summed, 1)
            dv.wait_ge(first_summed, FIRST_ROUNDS + 1)
            modulation(0, 0, (DEPTH * JOBS - 1) * (JOB_T + KT), sums[:].rearrange("p (g j) -> p j g", g=2))
            dv.sem_inc(ada_step, JOB_PARTS * (KT + 1))
            with dv.Fori(0, DEPTH) as l:
                norm(l, 0)
                ffn(l, F1, 0, (0, 1))
                norm(l, 1)
                dv.wait_ge(par_in, l * 16 + 16)
                settle(dv)
                nc.vector.memset(qrs[:, 0:NTOK], 0.0).then_inc(qrs_zeroed, 1)
                nc.vector.tensor_scalar(small[:, 73:74], par[:, P_GQK:P_GQK + 1], HD_A ** -0.5, None, ALU.mult)\
                    .then_inc(gq, 1)
                settle(dv)
                with dv.Fori(0, INA_PAIRS // 2) as q:
                    for b in range(2):
                        dv.wait_ge(strip_done[1], q * 2 + filled(l, INA + b))
                        for s in range(2):
                            dst = by_column(qkv[:, bass.ds(q * 4 + (2 * b + s), 1), 0:NLAT].rearrange("p a n -> p (a n)"))
                            end = s * T2 + NLAT - T1
                            nc.vector.tensor_copy(dst[:, 0:R1, :], by_row(bank[b][:, s, 0:T1]))
                            nc.vector.tensor_copy(dst[:, R1:ROWS, :], by_row(bank[b][:, 2, s * T2:end]))
                        nc.vector.tensor_copy(qkv[:, bass.ds(q * 4 + 2 * b, 2), NLAT:NTOK],
                                              piece2(b)[:, :, NLAT - T1:T2]).then_inc(taken[b], 1)
                dv.wait_ge(gq, l + 1)

                def q_norm(t):
                    dv.wait_ge(q_rms_done, l * 8 + t + 1)
                    g, out = small[:, 73:74] if t < 4 else par[:, P_GQK + 1:P_GQK + 2], q_rms_out(t)
                    nc.vector.scalar_tensor_tensor(qkv[:, t, 0:T1], qkv[:, t, 0:T1], g, out[0], ALU.mult, ALU.mult)
                    nc.vector.scalar_tensor_tensor(qkv[:, t, T1:NTOK], qkv[:, t, T1:NTOK], g, out[1], ALU.mult, ALU.mult)\
                        .then_inc(qk_normed, 1)

                for t in range(3):
                    q_norm(t)
                gr = slice(0, FROW + ROWP)
                dv.wait_ge(strip_done[0], l * SPLITS[0] + INB + 2)
                nc.vector.tensor_scalar(row_gate[gr, 0:T1], pb[gr, 0, 0:T1], par[gr, P_BG:P_BG + 1], None, ALU.add)\
                    .then_inc(gate_taken, 1)
                nc.vector.tensor_scalar(row_gate[gr, T1:NTOK], pb[gr, 2, 0:T2], par[gr, P_BG:P_BG + 1], None, ALU.add)\
                    .then_inc(gate_taken, 1)
                for t in range(3, 8):
                    q_norm(t)
                for u in range(NUNIT + 2):
                    n = l * NUNIT + u
                    if u < NUNIT:
                        h, qb = u // CH, u % CH
                        if qb == 0:
                            dv.wait_ge(bias_in[h % 2], (l * 4 + h // 2) * 16 + 16)
                        dv.wait_ge(s_done, n + 1)
                        if u >= 2:
                            dv.wait_ge(p_ready, n - 1)
                        lo, kind = (0, QB_KIND[qb]) if qb < LCH else (WIN, 0)
                        settle(dv)
                        nc.vector.tensor_tensor_reduce(s_neg[:, u % 2, lo:384], pa[:, u % 2, lo:384],
                                                       bias[:, 3 * (h % 2) + kind, lo:384], -1.0, 3.0e38,
                                                       ALU.add, ALU.min, stat[:, 0, u:u + 1]).then_inc(s_taken, 1)
                    if 1 <= u <= NUNIT:
                        dv.wait_ge(p_ready, n)
                        nc.vector.reciprocal(stat[:, 2, u - 1:u], stat[:, 1, u - 1:u]).then_inc(rinv_ready, 1)
                    if u >= 2:
                        v = u - 2
                        if v == 0:
                            dv.wait_ge(kv_out, l * 32 + 32)
                        dv.wait_ge(pv_done, n - 1)
                        dv.wait_ge(rinv_ready, n - 1)
                        nc.vector.tensor_scalar(att[:, v % CH, (v // CH) * HD_A:(v // CH + 1) * HD_A],
                                                pb[:, 1 + v % 2, 0:HD_A], stat[:, 2, v:v + 1], None, ALU.mult)\
                            .then_inc(att_ready, 1)
                for c in range(CH):
                    dv.wait_ge(at_hi, l * CH + c + 1)
                    src, dst = at_views(g_lo, c)
                    nc.vector.tensor_tensor(dst, src, at_views(g_hi, c)[1].bitcast(F32), ALU.subtract).then_inc(at_lo, 1)
                at = [l * ROW_STEPS]

                def step(ins):
                    ins.then_inc(row_step, 1)
                    at[0] = at[0] + 1
                    dv.wait_ge(row_step, at[0])

                fr, r0, rb = slice(FROW, FROW + ROWP), slice(0, ROWP), slice(32, ROWP)
                v = nc.vector
                step(v.scalar_tensor_tensor(row_exp[fr, :], row_gate[fr, :], -1.0, row_gate[fr, :], ALU.mult, ALU.max))
                v.memset(v_aug[:, :, :, HD_B:VW], 1.0).then_inc(ones_set, 1)
                dv.wait_ge(row_act, l * 2 + 2)
                step(v.scalar_tensor_tensor(row_lf[r0, :], row_gate[fr, :], 0.0, row_exp[fr, :], ALU.min, ALU.subtract))
                step(v.tensor_tensor_scan(row_b[r0, :], reset[r0, :], row_lf[r0, :], 0.0, ALU.mult, ALU.add))
                step(v.tensor_tensor_scan(row_b[rb, NTOK - 1::-1], reset[rb, NTOK - 1::-1], row_lf[rb, NTOK - 1::-1],
                                          0.0, ALU.mult, ALU.add))
                m0 = par[:, P_M0:P_M0 + 1]
                step(v.tensor_tensor_scan(row_m[r0, 0:NLAT], row_lf[r0, 0:NLAT], row_gate[r0, 0:NLAT], m0[r0], ALU.add, ALU.max))
                step(v.tensor_tensor_scan(row_m[r0, NLAT:NTOK], row_lf[r0, NLAT:NTOK], row_gate[r0, NLAT:NTOK], 0.0,
                                          ALU.add, ALU.max))
                step(v.tensor_tensor_scan(row_m[rb, NLAT - 1::-1], row_lf[rb, NLAT - 1::-1], row_gate[rb, NLAT - 1::-1],
                                          m0[rb], ALU.add, ALU.max))
                step(v.tensor_tensor_scan(row_m[rb, NTOK - 1:NLAT - 1:-1], row_lf[rb, NTOK - 1:NLAT - 1:-1],
                                          row_gate[rb, NTOK - 1:NLAT - 1:-1], 0.0, ALU.add, ALU.max))
                step(v.tensor_tensor(row_m_rel[r0, :], row_m[r0, :], row_b[r0, :], ALU.subtract))
                step(v.tensor_tensor(row_g[r0, :], row_gate[r0, :], row_b[r0, :], ALU.subtract))
                step(v.tensor_copy(mprev[r0, 0:1], m0[r0]))
                step(v.tensor_copy(mprev[r0, 1:LCH], row_m[r0, P - 1:(LCH - 1) * P:P]))
                step(v.memset(mprev[r0, LCH:CH], 0.0))
                step(v.tensor_copy(mprev[rb, 0:LCH - 1], row_m[rb, P:(LCH - 1) * P + 1:P]))
                step(v.tensor_copy(mprev[rb, LCH - 1:LCH], m0[rb]))

                def chunks(ap):
                    return ap.rearrange("p (c t) -> p c t", t=P)

                step(v.tensor_tensor(chunks(row_a[r0, :]), mprev[r0, 0:CH, None].broadcast_to([ROWP, CH, P]),
                                     chunks(row_m_rel[r0, :]), ALU.subtract))
                step(v.tensor_tensor(chunks(row_w[r0, :]), chunks(row_g[r0, :]),
                                     chunks(row_m_rel[r0, :])[:, :, P - 1:P].broadcast_to([ROWP, CH, P]), ALU.subtract))
                step(v.tensor_tensor(chunks(row_w[rb, :]), chunks(row_g[rb, :]),
                                     chunks(row_m_rel[rb, :])[:, :, 0:1].broadcast_to([ROWP - 32, CH, P]), ALU.subtract))
                dv.wait_ge(rope_in, l * 16 + 16)
                for i in range(INB_PAIRS):
                    dv.wait_ge(strip_done[1], filled(l, INB + i))
                    v.tensor_copy(qkv[:, 2 * i:2 * i + 2, 0:T1], piece1(i % 2))
                    v.tensor_copy(qkv[:, 2 * i:2 * i + 2, T1:NTOK], piece2(i % 2)).then_inc(taken[i % 2], 1)
                    for t in (2 * i, 2 * i + 1) if i < 4 else ():
                        r, sc = l * 24 + 3 * t, 1.0 if t < 4 else HD_B ** -0.5
                        dv.wait_ge(rot_done, l * 8 + t + 1)
                        if t >= 2:
                            dv.wait_ge(rope_step, r - 3)
                        v.scalar_tensor_tensor(rtmp[:, t % 2, :], (m1, m2)[t % 2][:], sc, sin, ALU.mult, ALU.mult)\
                            .then_inc(rope_step, 1)
                        dv.wait_ge(taken[i % 2], fills(l, INB + i) + 1)
                        v.scalar_tensor_tensor(qkv[:, t, :], qkv[:, t, :], sc, cos, ALU.mult, ALU.mult)\
                            .then_inc(rope_step, 1)
                        dv.wait_ge(rope_step, r + 2)
                        v.tensor_tensor(qkv[:, t, 0:NLAT], qkv[:, t, 0:NLAT], rtmp[:, t % 2, :], ALU.add)\
                            .then_inc(rope_step, 1)
                dv.wait_ge(rope_step, l * 24 + 24)
                for c in range(CH):
                    dv.wait_ge(kt_done, l * CH + c + 1)
                    v.tensor_copy(k_tok[:, c, :], (pa[:, 2, :], pb[:, 0, :])[c % 2]).then_inc(kt_taken, 1)
                dv.wait_ge(kt_taken, l * CH + CH)
                dv.wait_ge(cols_ready, l * 5 + 5)

                def ya(n):
                    dv.wait_ge(strip_done[1], filled(l, YA + n))
                    dv.wait_ge(ga_done, l * KT + n + 1)
                    v.tensor_tensor(y(n)[:, 0:T1], y(n)[:, 0:T1], pb[:, 1, 0:T1], ALU.mult)
                    v.tensor_tensor(y(n)[:, T1:NTOK], y(n)[:, T1:NTOK], pb[:, 2, T2:2 * T2], ALU.mult)\
                        .then_inc(taken[(YA + n) % 2], 1)

                for n in range(2 * H_B):
                    h, back, g, r = n // 2, n % 2, l * 8 + n, row_of(n)
                    order = range(LCH) if back == 0 else range(LCH - 1, -1, -1)
                    rest = 1 - back
                    mk = mask[:, back:back + 1, :]
                    if n >= 1:
                        ya(n - 1)
                    dv.wait_ge(mb_done, g + 1)
                    if n >= 1:
                        dv.wait_ge(st_ready, g * 2)
                    v.tensor_tensor(chunks(wt[:, 0:NLAT]), chunks(pa[:, 2, :]), mk.broadcast_to([P, LCH, P]), ALU.add)\
                        .then_inc(mb_taken, 1)
                    v.tensor_tensor(wt[:, NLAT:NTOK], pa[:, 1, P:2 * P], mask[:, back, :], ALU.add).then_inc(mb_taken, 1)
                    if n >= 1:
                        dv.wait_ge(upd_done, g)
                    v.tensor_tensor(kw, k_tok[:, :, h * P:(h + 1) * P],
                                    gcols[:, 2, :, r:r + 1].broadcast_to([P, CH, P]), ALU.mult).then_inc(kw_ready, 1)
                    dv.wait_ge(upd_done, g + 1)
                    dv.wait_ge(c_in[n % 2], (l * 4 + n // 2) * 16 + 16)
                    for j in range(3):
                        if j >= 1:
                            dv.wait_ge(c_step, g * 3 + j)
                        v.scalar_tensor_tensor(c_seq[n % 2][:, j + 1, :], c_seq[n % 2][:, j, :], dec[:, n, order[j]:order[j] + 1],
                                               m1[:, j * VW:(j + 1) * VW], ALU.mult, ALU.add).then_inc(c_step, 1)
                    dv.wait_ge(wt_ready, (g + 1) * CH)
                    dv.wait_ge(kq_done, l * 4 + h + 1)
                    if n >= 1:
                        dv.wait_ge(intra_done, g)
                    v.tensor_tensor(st[:, 0:NLAT], wt[:, 0:NLAT], pa[:, 0, :], ALU.mult).then_inc(st_ready, 1)
                    v.tensor_tensor(st[:, NLAT:NTOK], wt[:, NLAT:NTOK], pa[:, 1, 0:P], ALU.mult).then_inc(st_ready, 1)
                    s0 = steps_before(l, n)
                    dv.wait_ge(intra_done, g + 1)
                    dv.wait_ge(inter_done, g + 1)
                    if n >= 1:
                        dv.wait_ge(num_step, s0)
                    c0 = order[0]
                    v.tensor_tensor(num[:, rest:rest + 3, :], pa[:, 2, 0:3 * VW].rearrange("p (c d) -> p c d", d=VW),
                                    gcols[:, 1, rest:rest + 3, r:r + 1].broadcast_to([P, 3, VW]), ALU.mult).then_inc(num_step, 1)
                    v.tensor_scalar(num[:, c0, :], pa[:, 1, 2 * P:2 * P + VW], gcols[:, 1, c0, r:r + 1], None, ALU.mult)\
                        .then_inc(num_step, 1)
                    dv.wait_ge(num_step, s0 + 2)
                    v.tensor_tensor(num[:, 0:3, :], num[:, 0:3, :], m1[:, 0:3 * VW].rearrange("p (c d) -> p c d", d=VW),
                                    ALU.add).then_inc(num_step, 1)
                    v.tensor_tensor(num[:, 3, :], num[:, 3, :], m2[:, 0:VW], ALU.add).then_inc(num_step, 1)
                    v.tensor_copy(num[:, LCH, :], m2[:, VW:2 * VW]).then_inc(num_step, 1)
                    if n >= 2:
                        dv.wait_ge(cout_out[n % 2], (l * H_B + n // 2) * 16)
                    else:
                        dv.wait_ge(ones_set, l + 1)
                    v.tensor_copy(c_out[:, n % 2, :], m2[:, 2 * VW:3 * VW]).then_inc(cout_ready, 1)
                    dv.wait_ge(num_step, s0 + 5)
                    v.scalar_tensor_tensor(den, num[:, :, HD_B], -1.0, gcols[:, 3, :, r], ALU.mult, ALU.max)\
                        .then_inc(num_step, 1)
                    dv.wait_ge(num_step, s0 + 6)
                    v.tensor_tensor(den, den, num[:, :, HD_B], ALU.max).then_inc(num_step, 1)
                    dv.wait_ge(num_step, s0 + 7)
                    v.reciprocal(den, den).then_inc(num_step, 1)
                    dv.wait_ge(num_step, s0 + 8)
                    out = hb[:, :, h * P:(h + 1) * P] if back == 0 else hnum[:, :, 0:HD_B]
                    if n == 0:
                        dv.wait_ge(m_out, l * 32 + 32)
                    v.tensor_tensor(out, num[:, :, 0:HD_B], den[:, :, None].broadcast_to([P, CH, HD_B]), ALU.mult)\
                        .then_inc(num_step, 1)
                    if back:
                        dv.wait_ge(num_step, s0 + 9)
                        hh = hb[:, :, h * P:(h + 1) * P]
                        v.tensor_tensor(hh, hh, out, ALU.add).then_inc(num_step, 1)
                ya(2 * H_B - 1)
                dv.wait_ge(num_step, l * NUM_STEPS + NUM_STEPS)
                v.tensor_tensor(hsq, hb, hb, ALU.mult).then_inc(hb_step, 1)
                dv.wait_ge(hb_step, l * 3 + 1)
                v.tensor_reduce(hss, pool[:, 10260:12820].rearrange("p (a b) -> p a b", b=P), AX_X, ALU.add)\
                    .then_inc(hb_step, 1)
                dv.wait_ge(hb_act, l * 2 + 2)
                hb20 = pool[:, 12820:15380].rearrange("p (a b) -> p a b", b=P)
                v.tensor_tensor(hb20, hb20, hss[:, :, None].broadcast_to([P, CH * H_B, P]), ALU.mult).then_inc(hb_step, 1)
                dv.wait_ge(hb_step, l * 3 + 3)

                def h_low(c):
                    dv.wait_ge(ht_hi, l * CH + c + 1)
                    v.tensor_tensor(b_lo[:, :, c * P:(c + 1) * P], hbt[:, c % 2, :].rearrange("p (f t) -> p f t", f=4),
                                    b_hi[:, :, c * P:(c + 1) * P].bitcast(F32), ALU.subtract).then_inc(ht_lo, 1)

                dv.wait_ge(ob_done, l * 6 + 6)
                for c in range(CH):
                    dv.wait_ge(ht_done, l * CH + c + 1)
                    if c >= 2:
                        dv.wait_ge(ht_lo, l * CH + c - 1)
                    v.tensor_tensor(hbt[:, c % 2, :].rearrange("p (f t) -> p f t", f=4),
                                    (m1, m2)[c % 2][:, 0:512].rearrange("p (f t) -> p f t", f=4),
                                    ob_sig[:, :, c * P:(c + 1) * P], ALU.mult).then_inc(ht_prod, 1)
                    if c >= 1:
                        h_low(c - 1)
                h_low(CH - 1)
                settle(dv)
                def y_lo(k):
                    dv.wait_ge(h_hi_ready, l * H_TILES + 2 * KT + k + 1)
                    v.tensor_tensor(h_lo[:, k, :], y(k), h_hi[:, k, :].bitcast(F32), ALU.subtract).then_inc(h_lo_ready, 1)

                def yb(q, b, half, ys):
                    at = half * 4 + b
                    dv.wait_ge(strip_done[1], q * 2 + filled(l, YB + at))
                    dv.wait_ge(br_done, q * 2 + (l * KT + (at + 1)))
                    dv.wait_ge(ty_step, (q * 2 + l * KT) * 2 + (2 * at + 1))
                    v.tensor_tensor(ty[:, b, 0:T1], bank[b][:, 1, 0:T1], br_sig[:, b, 0:T1], ALU.mult).then_inc(ty_step, 1)
                    v.tensor_tensor(ty[:, b, T1:NTOK], bank[b][:, 2, T2:2 * T2], br_sig[:, b, T1:NTOK], ALU.mult)\
                        .then_inc(taken[b], 1)
                    dv.wait_ge(taken[b], q + (fills(l, YB + at) + 1))
                    v.tensor_tensor(ys, ys, ty[:, b:b + 1, :], ALU.add).then_inc(ty_step, 1)

                with dv.Fori(0, 2) as q:
                    for b in range(2):
                        yb(q, b, 0, g_hi32[:, bass.ds(q * 2 + (4 + b), 1), :])
                for d in range(KT // 2, KT):
                    if d == KT - 1:
                        for k in range(Y_EARLY):
                            y_lo(k)
                    yb(d // 2 - 2, d % 2, 1, g_lo32[:, d:d + 1, :])
                for k in range(Y_EARLY, KT):
                    y_lo(k)
                add_pairs(l, OS, l * X_UPD + (X_IN + 3 * KT), 1, l * 3 + 2)
                norm(l, 2)
                ffn(l, F2, 1, (2,))


def kernel(x_prompt, x_sample, cache_k, cache_v, state_C, state_n, state_m, c, c_ctx,
           w_ada, b_ada, g_norm, w_up1, w_dn1, w_in, b_gates, g_qn, g_kn, rpb, g_hn,
           w_pa, w_pb, w_o, w_up2, w_dn2):
    import numpy as np
    import concourse.bacc as bacc
    from concourse.bass_utils import run_bass_kernel_spmd

    A = np.asarray
    f32 = np.float32

    def strips(w):
        w = A(w)
        l, k, n = w.shape
        return w.reshape(l, k // P, P, n // P, P).transpose(0, 3, 2, 1, 4).reshape(l, n // P, P, k)

    def columns(v, tiles):
        v = A(v)
        return v.reshape(v.shape[0], -1, tiles, P).transpose(0, 3, 1, 2).reshape(v.shape[0], P, -1)

    def interleave(a, b):
        return np.stack([a, b], axis=2).reshape(a.shape[0], -1, *a.shape[2:])

    def up(w):
        s = strips(w)
        return interleave(s[:, :D_FF // P], s[:, D_FF // P:])

    def down(w):
        w, out, r = A(w), [], 0
        for n in FF_PARTS:
            out.append(strips(w[:, r:r + n * P]))
            r += n * P
        return np.concatenate(out[:2], axis=1), out[2]

    win = A(w_in)
    aw, bw = 3 * H_A * HD_A, 4 * H_B * HD_B
    s_main, s_br = strips(win[:, :, :aw + bw]), strips(win[:, :, aw + bw + 4 * H_B:])
    w_in_s = np.concatenate([s_main, s_br], axis=1)
    gate_at = [(0, 0), (FROW, 1), (32, 2), (FROW + 32, 3)]
    wg = np.zeros((DEPTH, D_MODEL, P), f32)
    for to, j in gate_at:
        wg[:, :, to:to + H_B] = win[:, :, aw + bw + j * H_B:aw + bw + (j + 1) * H_B]
    par = np.zeros((DEPTH, P, N_PAR), f32)
    par[:, :, P_GQK] = np.tile(A(g_qn), (1, 2))
    par[:, :, P_GQK + 1] = np.tile(A(g_kn), (1, 2))
    par[:, :, P_GHN:P_BG] = columns(g_hn, H_B)
    for to, j in gate_at:
        par[:, to:to + H_B, P_BG] = A(b_gates)[:, j * H_B:(j + 1) * H_B]
    par[:, 0:H_B, P_M0] = A(state_m)[0, :, 0]
    par[:, 32:32 + H_B, P_M0] = A(state_m)[0, :, 1]

    ba = A(b_ada).reshape(DEPTH * JOBS, JOB_T, P)
    gn = A(g_norm).reshape(DEPTH * JOBS, KT, P)
    job_par = np.roll(np.concatenate([ba, gn], axis=1), -1, axis=0).reshape(-1, P).T
    ada = A(w_ada).reshape(DEPTH, KT, P, JOBS, JOB_W).transpose(0, 3, 1, 2, 4).reshape(DEPTH * JOBS, KT, P, JOB_W)
    ada = np.roll(ada, -1, axis=0).reshape(-1, P, JOB_W)

    const = np.zeros((P, N_CONST), f32)
    i = np.arange(P)
    const[:, C_ID:C_ID + P] = np.eye(P)
    const[:, C_SEL:C_SEL + P] = (i[None] % 16 == 2 * (i[None] // 16) + i[:, None] // HD_A) / HD_A
    pick = (i[:, None] == np.arange(1024)[None] // HD_A).astype(f32)
    const[:, C_ON:C_ON + P] = 1.0 / D_MODEL
    half = HD_B // 2
    for m in range(half):
        const[m + half, C_ROT + m] = -1.0
        const[m, C_ROT + m + half] = 1.0
    const[:, C_MASK:C_MASK + P] = np.where(i[:, None] <= i[None], 0.0, 1e30)
    const[:, C_MASK + P:C_MASK + 2 * P] = np.where(i[:, None] >= i[None], 0.0, 1e30)
    t = np.arange(NTOK)
    const[:, C_RESET:C_RESET + NTOK] = (t % P != 0)
    const[32:, C_RESET:C_RESET + NTOK] = (t % P != P - 1)
    const[:, C_EPS] = EPS
    nf = half // 2
    inv = f32(10000.0) ** (-np.arange(nf, dtype=f32) / f32(nf))
    tl = np.arange(NLAT)
    ang = np.concatenate([(tl // GRID_W).astype(f32)[:, None] * inv, (tl % GRID_W).astype(f32)[:, None] * inv], axis=1)
    rope = np.zeros((P, NTOK + NLAT), f32)
    rope[:, :NLAT] = np.tile(np.cos(ang).T, (2, 1))
    rope[:, NLAT:NTOK] = 1.0
    rope[:, NTOK:] = np.tile(np.sin(ang).T, (2, 1))

    qc, qr = i[:, None] // ROWS, i[:, None] % ROWS
    kc, kr = np.arange(WIN)[None] // ROWS, np.arange(WIN)[None] % ROWS
    rp = A(rpb)
    bias = np.zeros((DEPTH, H_A, P, 3, 3 * P), f32)
    for kind, qb in enumerate((0, 1, 3)):
        cq, ck = qc + 16 * qb, kc + QB_KEY[qb] // ROWS
        start = np.clip(cq - 8, 0, GRID_W - 16)
        ok = (ck >= start) & (ck < start + 16)
        dr, dc = np.broadcast_to(kr - qr + 7, ok.shape), np.clip(ck - cq + 15, 0, 30)
        bias[:, :, :, kind, :WIN] = np.where(ok[None, None], rp[:, :, dr, dc], f32(-1e30))

    ff1, ff1b = down(w_dn1)
    ff2, ff2b = down(w_dn2)
    xs = np.concatenate([A(x_sample)[0], A(x_prompt)[0]], axis=0)
    sc, sn = A(state_C)[0], A(state_n)[0]
    state = np.concatenate([sc.transpose(0, 4, 2, 1, 3), sn.transpose(0, 3, 2, 1)[..., None]], axis=4)
    arrays = {
        "x": xs.T.reshape(KT, P, NTOK).transpose(1, 0, 2),
        "cond": np.stack([A(c)[0].reshape(KT, P).T, A(c_ctx).reshape(KT, P).T], axis=2),
        "const": const, "pick": pick, "rope": rope, "par": par, "bias": bias,
        "cache_k": A(cache_k)[0].reshape(DEPTH, P, 4, P).transpose(0, 3, 2, 1),
        "cache_v": A(cache_v)[0].reshape(DEPTH, P, H_A * HD_A),
        "state_c": state.reshape(DEPTH, P, 2 * H_B, VW),
        "w_ada": ada, "job_par": job_par, "up1": up(w_up1), "dn1a": ff1, "dn1b": ff1b, "wg": strips(wg)[:, 0],
        "w_in": w_in_s, "w_pab": np.concatenate([strips(w_pa), strips(w_pb)], axis=1), "w_o": strips(w_o),
        "up2": up(w_up2), "dn2a": ff2, "dn2b": ff2b,
    }
    outs = {"y": (P, KT, NTOK), "new_k": (DEPTH, P, 4, NCTX), "new_v": (DEPTH, P, 4, NCTX),
            "new_c": (DEPTH, P, 2 * H_B, VW), "new_m": (DEPTH, 2, H_B, 1)}
    nc = bacc.Bacc("TRN2", target_bir_lowering=False, num_devices=1)
    io, feed = {}, {}
    for name, a in arrays.items():
        a = np.ascontiguousarray(a)
        feed[f"in_{name}"] = a
        io[name] = nc.dram_tensor(f"in_{name}", a.shape, F32, kind="ExternalInput").ap()
    for name, shape in outs.items():
        io[name] = nc.dram_tensor(f"out_{name}", shape, F32, kind="ExternalOutput").ap()
    build(nc, io)
    r = run_bass_kernel_spmd(nc, [feed], core_ids=[0]).results[0]
    yt = r["out_y"].transpose(2, 1, 0).reshape(NTOK, D_MODEL)

    def cache(a):
        return a.transpose(0, 3, 2, 1).reshape(1, DEPTH, NCTX, H_A, HD_A)

    nc_ = r["out_new_c"].reshape(DEPTH, P, H_B, 2, VW)
    return (np.ascontiguousarray(yt[NLAT:])[None], np.ascontiguousarray(yt[:NLAT])[None],
            cache(r["out_new_k"]), cache(r["out_new_v"]),
            nc_[..., :HD_B].transpose(0, 3, 2, 4, 1)[None], nc_[..., HD_B].transpose(0, 3, 2, 1)[None],
            r["out_new_m"].reshape(1, DEPTH, 2, H_B))
```
